# Optimizing a Trainium2 kernel written in Bass

```python
import math
import jax, jax.numpy as jnp
from jax import lax
import numpy as np

D_MODEL = 1024
BATCH = 1
SEQ = 1024
DEPTH = 1
DEC_BATCH = 8
DEC_SEQ = 8
PAST_LEN = 8192
PAGE_SIZE = 128

D_PLE = 256
A_HEADS = 8
A_HEAD_DIM = 64
A_WIDTH = A_HEADS * A_HEAD_DIM
DECAY_LORA = 64
AAA_LORA = 64
GATE_LORA = 128
GN_EPS_RWKV = 64e-5
B_HEADS = 4
B_QK_DIM = 64
B_V_DIM = 128
B_QK_WIDTH = B_HEADS * B_QK_DIM
B_WIDTH = B_HEADS * B_V_DIM
RET_CHUNK = 128
ROPE_BASE = 10000.0
GN_EPS = 1e-5
MIX_WIDTH = A_WIDTH + B_WIDTH
SHIFT_WIDTH = 3 * A_WIDTH + DECAY_LORA + AAA_LORA + GATE_LORA
IN_WIDTH = SHIFT_WIDTH + 2 * B_QK_WIDTH + 2 * B_WIDTH
N_GROUPS = 4
EXPERTS_PER_GROUP = 4
N_EXPERTS = N_GROUPS * EXPERTS_PER_GROUP
D_EXPERT = 256
TOP_K_INNER = 2
DEEPNORM_ALPHA = (2 * DEPTH) ** 0.25
DEEPNORM_BETA = (8 * DEPTH) ** -0.25
LN_EPS = 1e-5

kernel_name = "hybrid_rwkv7_retention_hmoe_step"

def layer_norm(x, g, b):
    xf = x.astype(jnp.float32)
    mu = xf.mean(-1, keepdims=True)
    var = jnp.mean(jnp.square(xf - mu), -1, keepdims=True)
    return ((xf - mu) * lax.rsqrt(var + LN_EPS) * g + b).astype(x.dtype)

def rms_norm(x, g):
    xf = x.astype(jnp.float32)
    return (xf * lax.rsqrt(jnp.mean(jnp.square(xf), -1, keepdims=True) + LN_EPS) * g).astype(x.dtype)

def head_norm(y, g, b, eps):
    mu = y.mean(-1, keepdims=True)
    var = jnp.mean(jnp.square(y - mu), -1, keepdims=True)
    return (y - mu) * lax.rsqrt(var + eps) * g + b

def rotary(x, pos):
    half = x.shape[-1] // 2
    inv = ROPE_BASE ** (-jnp.arange(half, dtype=jnp.float32) / half)
    ang = pos.astype(jnp.float32)[:, None] * inv[None, :]
    cos = jnp.cos(ang)[:, None, :]
    sin = jnp.sin(ang)[:, None, :]
    x1, x2 = x[..., :half], x[..., half:]
    return jnp.concatenate([x1 * cos - x2 * sin, x1 * sin + x2 * cos], axis=-1)

def rwkv7_scan(r, w, k, v, kk, a, s0):
    def step(S, inp):
        r_t, w_t, k_t, v_t, kk_t, a_t = inp
        sa = jnp.einsum('bhvk,bhk->bhv', S, -kk_t)
        S = (S * w_t[:, :, None, :] + sa[..., None] * (kk_t * a_t)[:, :, None, :]
             + v_t[..., None] * k_t[:, :, None, :])
        return S, jnp.einsum('bhvk,bhk->bhv', S, r_t)
    xs = tuple(jnp.moveaxis(t, 1, 0) for t in (r, w, k, v, kk, a))
    S, ys = lax.scan(step, s0, xs)
    return jnp.moveaxis(ys, 0, 1), S

def retention_chunked(q, k, v, s0, chunk):
    Bsz, T, H, _ = q.shape
    dv = v.shape[-1]
    nc = T // chunk
    lg = jnp.log1p(-jnp.exp2(-5.0 - jnp.arange(H, dtype=jnp.float32)))
    idx = jnp.arange(chunk, dtype=jnp.float32)
    diff = idx[:, None] - idx[None, :]
    intra = jnp.where(diff >= 0, jnp.exp(lg[:, None, None] * jnp.maximum(diff, 0.0)), 0.0)
    cross = jnp.exp(lg[:, None] * (idx + 1.0))
    kdec = jnp.exp(lg[:, None] * (chunk - 1.0 - idx))
    cdec = jnp.exp(lg * chunk)

    def to_chunks(t):
        return t.reshape(Bsz, nc, chunk, H, t.shape[-1]).transpose(1, 0, 3, 2, 4)

    def step(S, inp):
        qc, kc, vc = inp
        sc = jnp.einsum('bhid,bhjd->bhij', qc, kc) * intra
        o = (jnp.einsum('bhij,bhjv->bhiv', sc, vc)
             + jnp.einsum('bhid,bhdv->bhiv', qc, S) * cross[:, :, None])
        S = S * cdec[:, None, None] + jnp.einsum('bhjd,bhjv->bhdv', kc * kdec[:, :, None], vc)
        return S, o

    S, o = lax.scan(step, s0, (to_chunks(q), to_chunks(k), to_chunks(v)))
    o = o.transpose(1, 0, 3, 2, 4).reshape(Bsz, T, H, dv)
    return o, S

def hybrid_mixer(x, x_prev, wkv0, ret0, pos0, w_in, mu_shift, w_decay_up, decay_base, w_aaa_up,
                 aaa_base, w_gate_up, k_k, k_a, r_k, lnx_g, lnx_b, ret_gn_g, ret_gn_b, w_out):
    f32 = jnp.float32
    Bsz, T, _ = x.shape
    x_ext = jnp.concatenate([x_prev[:, None, :].astype(x.dtype), x], axis=1)
    proj = jnp.einsum('btd,de->bte', x_ext, w_in).astype(f32)
    cur = proj[:, 1:]
    sc = cur[..., :SHIFT_WIDTH]
    sh = sc + (proj[:, :-1, :SHIFT_WIDTH] - sc) * mu_shift.astype(f32)
    r, k, v, w_lo, a_lo, g_lo = jnp.split(
        sh, (A_WIDTH, 2 * A_WIDTH, 3 * A_WIDTH, 3 * A_WIDTH + DECAY_LORA,
             3 * A_WIDTH + DECAY_LORA + AAA_LORA), axis=-1)
    log_w = -jax.nn.softplus(-(decay_base + jnp.tanh(w_lo) @ w_decay_up)) - 0.5
    decay = jnp.exp(-jnp.exp(log_w.astype(f32)))
    a = jax.nn.sigmoid(aaa_base + a_lo @ w_aaa_up).astype(f32)
    g = (jax.nn.sigmoid(g_lo) @ w_gate_up).astype(f32)

    def hs(t):
        return t.reshape(Bsz, T, A_HEADS, A_HEAD_DIM)
    kk = hs(k * k_k).astype(f32)
    kk = kk / jnp.maximum(jnp.sqrt(jnp.sum(jnp.square(kk), -1, keepdims=True)), 1e-12)
    k = (k * (1.0 + (a - 1.0) * k_a)).astype(f32)
    r4, k4, v4, a4, w4 = hs(r), hs(k), hs(v), hs(a), hs(decay)
    y_a, wkv1 = rwkv7_scan(r4, w4, k4, v4, kk, a4, wkv0.astype(f32))
    y_a = head_norm(y_a, lnx_g, lnx_b, GN_EPS_RWKV) + jnp.sum(r4 * k4 * r_k, -1, keepdims=True) * v4
    y_a = y_a.reshape(Bsz, T, A_WIDTH) * g
    q_b, k_b, v_b, g_b = jnp.split(
        cur[..., SHIFT_WIDTH:], (B_QK_WIDTH, 2 * B_QK_WIDTH, 2 * B_QK_WIDTH + B_WIDTH), axis=-1)
    pos = pos0 + jnp.arange(T, dtype=jnp.int32)
    q_b = rotary(q_b.reshape(Bsz, T, B_HEADS, B_QK_DIM), pos)
    k_b = rotary(k_b.reshape(Bsz, T, B_HEADS, B_QK_DIM), pos) * (B_QK_DIM ** -0.5)
    v_b = v_b.reshape(Bsz, T, B_HEADS, B_V_DIM)
    chunk = RET_CHUNK if T % RET_CHUNK == 0 else T
    o_b, ret1 = retention_chunked(q_b, k_b, v_b, ret0.astype(f32), chunk)
    y_b = head_norm(o_b, ret_gn_g, ret_gn_b, GN_EPS).reshape(Bsz, T, B_WIDTH) * jax.nn.silu(g_b)
    y = jnp.concatenate([y_a, y_b], axis=-1).astype(x.dtype)
    return jnp.einsum('bte,ed->btd', y, w_out), wkv1, ret1

def hier_moe(x, router_coarse_w, router_coarse_b, router_fine_w, router_fine_b, expert_w1, expert_w3, expert_w2):
    Bsz, T, D = x.shape
    xf = x.reshape(Bsz * T, D)
    n = xf.shape[0]
    rows = jnp.arange(n)
    cl = (xf @ router_coarse_w + router_coarse_b).astype(jnp.float32)
    grp = jnp.argmax(cl, axis=-1)
    gprob = jax.nn.softmax(cl, axis=-1)[rows, grp]
    fl = (xf @ router_fine_w + router_fine_b).astype(jnp.float32).reshape(n, N_GROUPS, EXPERTS_PER_GROUP)
    top_v, top_i = lax.top_k(fl[rows, grp], TOP_K_INNER)
    top_w = jax.nn.softmax(top_v, axis=-1) * gprob[:, None]
    expert_idx = grp[:, None] * EXPERTS_PER_GROUP + top_i
    gate = jnp.sum(jax.nn.one_hot(expert_idx, N_EXPERTS, dtype=jnp.float32) * top_w[..., None], axis=1)
    h = jax.nn.silu(jnp.einsum('nd,edf->nef', xf, expert_w1)) * jnp.einsum('nd,edf->nef', xf, expert_w3)
    y = jnp.einsum('nef,efd->nd', h * gate[..., None].astype(h.dtype), expert_w2)
    return y.reshape(Bsz, T, D)

def trunk_layer(x, p, x_prev, wkv0, ret0, pos0,
                w_in, mu_shift, w_decay_up, decay_base, w_aaa_up, aaa_base, w_gate_up, k_k, k_a, r_k,
                lnx_g, lnx_b, ret_gn_g, ret_gn_b, w_out, ln1_g, ln1_b,
                router_coarse_w, router_coarse_b, router_fine_w, router_fine_b,
                expert_w1, expert_w3, expert_w2, ln2_g, ln2_b, w_ple, w_ple_gate, ple_norm_g):
    mix, wkv1, ret1 = hybrid_mixer(x, x_prev, wkv0, ret0, pos0, w_in, mu_shift, w_decay_up, decay_base,
                                   w_aaa_up, aaa_base, w_gate_up, k_k, k_a, r_k, lnx_g, lnx_b,
                                   ret_gn_g, ret_gn_b, w_out)
    h = layer_norm(DEEPNORM_ALPHA * x + mix, ln1_g, ln1_b)
    ffn = hier_moe(h, router_coarse_w, router_coarse_b, router_fine_w, router_fine_b, expert_w1, expert_w3, expert_w2)
    h = layer_norm(DEEPNORM_ALPHA * h + ffn, ln2_g, ln2_b)
    ple = jnp.einsum('btp,pd->btd', p, w_ple) * jax.nn.sigmoid(jnp.einsum('btd,de->bte', h, w_ple_gate))
    h = h + rms_norm(ple, ple_norm_g)
    return h, x[:, -1], wkv1, ret1

def setup_inputs(seed: int = 0) -> dict:
    key = jax.random.key(seed)
    ks = iter(jax.random.split(key, 48))
    f32 = jnp.float32
    L = DEPTH

    def nrm(shape, scale):
        return scale * jax.random.normal(next(ks), shape, f32)

    def gain(shape):
        return 1.0 + nrm(shape, 0.02)

    return {
        "x_prompt": nrm((BATCH, SEQ, D_MODEL), 1.0),
        "x_sample": nrm((DEC_BATCH, DEC_SEQ, D_MODEL), 1.0),
        "p_prompt": nrm((DEPTH, BATCH, SEQ, D_PLE), 1.0),
        "p_sample": nrm((DEPTH, DEC_BATCH, DEC_SEQ, D_PLE), 1.0),
        "state_wkv": nrm((DEPTH, DEC_BATCH, A_HEADS, A_HEAD_DIM, A_HEAD_DIM), 0.3),
        "state_shift": nrm((DEPTH, DEC_BATCH, D_MODEL), 1.0),
        "state_ret": nrm((DEPTH, DEC_BATCH, B_HEADS, B_QK_DIM, B_V_DIM), 0.3),
        "w_in": nrm((L, D_MODEL, IN_WIDTH), D_MODEL ** -0.5),
        "mu_shift": jax.random.uniform(next(ks), (L, SHIFT_WIDTH), f32),
        "w_decay_up": nrm((L, DECAY_LORA, A_WIDTH), 0.5 * DECAY_LORA ** -0.5),
        "decay_base": jax.random.uniform(next(ks), (L, A_WIDTH), f32, -6.0, -1.0),
        "w_aaa_up": nrm((L, AAA_LORA, A_WIDTH), 0.5 * AAA_LORA ** -0.5),
        "aaa_base": nrm((L, A_WIDTH), 0.1),
        "w_gate_up": nrm((L, GATE_LORA, A_WIDTH), GATE_LORA ** -0.5),
        "k_k": 0.85 + nrm((L, A_WIDTH), 0.02),
        "k_a": gain((L, A_WIDTH)),
        "r_k": nrm((L, A_HEADS, A_HEAD_DIM), 0.1),
        "lnx_g": gain((L, A_HEADS, A_HEAD_DIM)),
        "lnx_b": nrm((L, A_HEADS, A_HEAD_DIM), 0.02),
        "ret_gn_g": gain((L, B_HEADS, B_V_DIM)),
        "ret_gn_b": nrm((L, B_HEADS, B_V_DIM), 0.02),
        "w_out": nrm((L, MIX_WIDTH, D_MODEL), DEEPNORM_BETA * MIX_WIDTH ** -0.5),
        "ln1_g": gain((L, D_MODEL)),
        "ln1_b": nrm((L, D_MODEL), 0.02),
        "router_coarse_w": nrm((L, D_MODEL, N_GROUPS), D_MODEL ** -0.5),
        "router_coarse_b": nrm((L, N_GROUPS), 0.01),
        "router_fine_w": nrm((L, D_MODEL, N_EXPERTS), D_MODEL ** -0.5),
        "router_fine_b": nrm((L, N_EXPERTS), 0.01),
        "expert_w1": nrm((L, N_EXPERTS, D_MODEL, D_EXPERT), D_MODEL ** -0.5),
        "expert_w3": nrm((L, N_EXPERTS, D_MODEL, D_EXPERT), D_MODEL ** -0.5),
        "expert_w2": nrm((L, N_EXPERTS, D_EXPERT, D_MODEL), DEEPNORM_BETA * D_EXPERT ** -0.5),
        "ln2_g": gain((L, D_MODEL)),
        "ln2_b": nrm((L, D_MODEL), 0.02),
        "w_ple": nrm((L, D_PLE, D_MODEL), D_PLE ** -0.5),
        "w_ple_gate": nrm((L, D_MODEL, D_MODEL), D_MODEL ** -0.5),
        "ple_norm_g": gain((L, D_MODEL)),
    }

def reference(x_prompt, x_sample, p_prompt, p_sample, state_wkv, state_shift, state_ret,
              w_in, mu_shift, w_decay_up, decay_base, w_aaa_up, aaa_base, w_gate_up, k_k, k_a, r_k,
              lnx_g, lnx_b, ret_gn_g, ret_gn_b, w_out, ln1_g, ln1_b,
              router_coarse_w, router_coarse_b, router_fine_w, router_fine_b,
              expert_w1, expert_w3, expert_w2, ln2_g, ln2_b, w_ple, w_ple_gate, ple_norm_g):
    yp, ys = x_prompt, x_sample
    nb = x_prompt.shape[0]
    wkv_p, shift_p, ret_p, wkv_s, shift_s, ret_s = [], [], [], [], [], []
    for i in range(DEPTH):
        lw = (w_in[i], mu_shift[i], w_decay_up[i], decay_base[i], w_aaa_up[i], aaa_base[i], w_gate_up[i],
              k_k[i], k_a[i], r_k[i], lnx_g[i], lnx_b[i], ret_gn_g[i], ret_gn_b[i], w_out[i], ln1_g[i], ln1_b[i],
              router_coarse_w[i], router_coarse_b[i], router_fine_w[i], router_fine_b[i],
              expert_w1[i], expert_w3[i], expert_w2[i], ln2_g[i], ln2_b[i], w_ple[i], w_ple_gate[i], ple_norm_g[i])
        zero_shift = jnp.zeros((nb, D_MODEL), yp.dtype)
        zero_wkv = jnp.zeros((nb, A_HEADS, A_HEAD_DIM, A_HEAD_DIM), jnp.float32)
        zero_ret = jnp.zeros((nb, B_HEADS, B_QK_DIM, B_V_DIM), jnp.float32)
        yp, sp, wp, rp = trunk_layer(yp, p_prompt[i], zero_shift, zero_wkv, zero_ret, 0, *lw)
        ys, ss, wsm, rsm = trunk_layer(ys, p_sample[i], state_shift[i], state_wkv[i], state_ret[i], PAST_LEN, *lw)
        wkv_p.append(wp); shift_p.append(sp); ret_p.append(rp)
        wkv_s.append(wsm); shift_s.append(ss); ret_s.append(rsm)
    new_wkv_prompt = jnp.stack(wkv_p, 0)
    new_shift_prompt = jnp.stack(shift_p, 0)
    new_ret_prompt = jnp.stack(ret_p, 0)
    new_wkv_sample = jnp.stack(wkv_s, 0)
    new_shift_sample = jnp.stack(shift_s, 0)
    new_ret_sample = jnp.stack(ret_s, 0)
    return (yp, ys, new_wkv_prompt, new_shift_prompt, new_ret_prompt, new_wkv_sample, new_shift_sample, new_ret_sample)


_drawn_inputs = setup_inputs


def setup_inputs(seed=0):
    import zlib

    import numpy as np

    out = dict(_drawn_inputs(seed))
    spreads = {}
    factors = {'k_k': 2.907,
     'k_a': 2.788,
     'lnx_g': 8.0,
     'lnx_b': 8.0,
     'ret_gn_g': 8.0,
     'ret_gn_b': 8.0,
     'ln1_g': 3.105,
     'ln1_b': 3.116,
     'router_coarse_b': 7.535,
     'router_fine_b': 8.0,
     'ln2_g': 12.333,
     'ln2_b': 11.758,
     'ple_norm_g': 16.522}
    for name, (base, spread) in spreads.items():
        noise = np.random.default_rng([zlib.crc32(name.encode()), seed]).standard_normal(out[name].shape)
        drawn = base * np.exp(spread * noise) if base else spread * noise
        out[name] = __import__('jax').numpy.asarray(drawn.astype(out[name].dtype))
    for name, factor in factors.items():
        out[name] = (out[name] * factor).astype(out[name].dtype)
    return out
```

```python
from contextlib import ExitStack

import numpy as np

import concourse.bass as bass
from concourse import mybir

F32 = mybir.dt.float32
ALU = mybir.AluOpType
ACT = mybir.ActivationFunctionType
AX = mybir.AxisListType.X

P = 128
D = 1024
KD = D // P
SEQ = 1024
DB, DS = 8, 8
PAST = 8192
D_PLE = 256
HA, NA = 8, 64
WA = HA * NA
HB, NK, NV = 4, 64, 128
SHIFT_W = 3 * WA + 64 + 64 + 128
IN_W = SHIFT_W + 2 * HB * NK + 2 * HB * NV
NG, EPG = 4, 4
NE = NG * EPG
FE = 256
ALPHA = 2 ** 0.25
LN_EPS = 1e-5
GN_EPS_A = 64e-5
GN_EPS_B = 1e-5

NT = SEQ // P
TILES = NT + 1
TS = DB * DS
ROWS = TILES * P
SAMPLE0 = 1 + SEQ
LEVELS = 7
LEVELS_S = 3
SLICE = 416
NSLICE = IN_W // SLICE
W_CONST = -float(np.exp(-0.5))
FC_TI, FC_TE, FC_SEL, FC_COS, FC_SIN, FC_CROSS, FC_KDEC, FC_N = 0, 128, 256, 264, 296, 328, 332, 336
MC_GRAM, MC_D, MC_M0, MC_LVL, MC_CDEC, MC_BLK, MC_N = 0, 512, 1024, 1152, 1152 + 7 * 128, 1152 + 7 * 128 + 2, 1152 + 7 * 128 + 10
VEC = ["mu_shift", "decay_base", "aaa_base", "k_k", "k_a", "r_k", "lnx_g", "lnx_b", "ret_gn_g", "ret_gn_b"]
VEC_OFF = dict(zip(VEC, np.cumsum([0, SHIFT_W] + [WA] * 8).tolist()))
VEC_N = SHIFT_W + WA * 9
C_READY, V2_READY = 2, 18
NCONST = 6


def shape_constants():
    lg = np.log1p(-np.exp2(-5.0 - np.arange(HB)))
    half = NK // 2
    inv = (10000.0 ** (-np.arange(half) / half)).astype(np.float32)
    fc = np.zeros((TILES, P, FC_N), np.float32)
    s, t = np.arange(P)[:, None], np.arange(P)[None, :]
    for n in range(TILES):
        if n < NT:
            pos = np.arange(P) + n * P
            idx, chunk = np.arange(P), P
            mid = (s < P // 2) * np.ones((1, P))
            fc[n, :, FC_TI:FC_TI + P] = (s <= t) - mid
            fc[n, :, FC_TE:FC_TE + P] = (s < t) - mid
            fc[n, :, FC_SEL] = np.arange(P) < P // 2
            fc[n, :, FC_SEL + 1] = np.arange(P) >= P // 2
        else:
            pos = PAST + np.arange(P) % DS
            idx, chunk = np.arange(P) % DS, DS
            same = (s // DS == t // DS) & (s < TS) & (t < TS)
            fc[n, :, FC_TI:FC_TI + P] = same & (s <= t)
            fc[n, :, FC_TE:FC_TE + P] = same & (s < t)
            fc[n, :, FC_SEL:FC_SEL + DB] = (np.arange(P)[:, None] // DS == np.arange(DB))
        ang = pos.astype(np.float32)[:, None] * inv[None, :]
        fc[n, :, FC_COS:FC_COS + half] = np.cos(ang)
        fc[n, :, FC_SIN:FC_SIN + half] = np.sin(ang)
        fc[n, :, FC_CROSS:FC_CROSS + HB] = np.exp(lg[None] * (idx[:, None] + 1.0))
        fc[n, :, FC_KDEC:FC_KDEC + HB] = np.exp(lg[None] * (chunk - 1.0 - idx[:, None])) * NK ** -0.5
    mc = np.zeros((2, P, MC_N), np.float32)
    for kind in range(2):
        ok = np.ones((P, P), bool) if kind == 0 else (s // DS == t // DS) & (s < TS) & (t < TS)
        for q in range(4):
            mc[kind, :, MC_GRAM + q * P:MC_GRAM + (q + 1) * P] = ok & ((s < t) if q % 2 == 0 else (s <= t))
        for h in range(HB):
            dec = np.where(s <= t, np.exp(lg[h] * np.maximum(t - s, 0)), 0.0) * NK ** -0.5
            at = MC_D + (h % 2 * 2 + h // 2) * P
            mc[kind, :, at:at + P] = dec * ok
        for j in range(LEVELS):
            b = 1 << j
            up = ok & (s // (2 * b) == t // (2 * b)) & (s // b % 2 == 0) & (t // b % 2 == 1)
            mc[kind, :, MC_LVL + j * P:MC_LVL + (j + 1) * P] = up
            if j == 0:
                mc[kind, :, MC_M0:MC_M0 + P] = up.T
        cd = np.exp(lg * (P if kind == 0 else DS))
        for pair in range(2):
            mc[kind, :64, MC_CDEC + pair] = cd[2 * pair]
            mc[kind, 64:, MC_CDEC + pair] = cd[2 * pair + 1]
        mc[kind, :, MC_BLK:MC_BLK + DB] = (np.arange(P)[:, None] // DS == np.arange(DB))
    return fc, mc


class Signal:

    def __init__(self, nc, ctx, name, per, by=1):
        self.sem = ctx.enter_context(nc.semaphore(name))
        self.per, self.by = per, by

    def at(self, t, j=None):
        return (t * self.per + (self.per if j is None else j)) * self.by


def project(nc, x_all, w_in, proj):
    nb = 6
    per = 2 * TILES
    assert per % nb == 0 and nb % 2 == 0
    with ExitStack() as ctx:
        xT = ctx.enter_context(nc.sbuf_tensor("pj_xT", [P, TILES, KD, P], F32))
        w = [ctx.enter_context(nc.sbuf_tensor(f"pj_w{u}", [P, KD, SLICE], F32)) for u in range(2)]
        stage = [ctx.enter_context(nc.sbuf_tensor(f"pj_out{b}", [P, SLICE], F32)) for b in range(nb)]
        bank = [ctx.enter_context(nc.psum_tensor(f"pj_ps{b}", [P, 512], F32)) for b in range(nb)]
        x_loaded = [ctx.enter_context(nc.semaphore(f"pj_x_loaded{g}")) for g in range(3)]
        w_loaded = [ctx.enter_context(nc.semaphore(f"pj_w_loaded{u}")) for u in range(2)]
        summed = ctx.enter_context(nc.semaphore("pj_summed"))
        bank_free = [ctx.enter_context(nc.semaphore(f"pj_bank_free{e}")) for e in range(2)]
        stored = [ctx.enter_context(nc.semaphore(f"pj_stored{b}")) for b in range(nb)]
        with nc.Block() as block:

            @block.sync
            def _(sp):
                for u in range(2):
                    sp.dma_start(w[u][:], w_in[u]).then_inc(w_loaded[u], 16)
                    if u == 0:
                        for g in range(3):
                            sp.dma_start(xT[:, 3 * g:3 * g + 3], x_all[:, 3 * g:3 * g + 3]).then_inc(x_loaded[g], 16)

                def two_slices(i, more):
                    for q in range(per):
                        b = q % nb
                        sp.wait_ge(bank_free[q % 2], i * TILES + q // 2 + 1 + nb // 2)
                        rows = proj[P * (q % TILES):P * (q % TILES) + P]
                        cols = rows.rearrange("p (s c) -> s p c", c=SLICE)[2 * i + q // TILES]
                        sp.dma_start(cols, stage[b][:]).then_inc(stored[b], 16)
                        if more and q % TILES == TILES - 1:
                            sp.wait_ge(summed, i * per + q + 1)
                            u = q // TILES
                            sp.dma_start(w[u][:], w_in[2 * i + 2 + u]).then_inc(w_loaded[u], 16)

                with sp.Fori(0, NSLICE // 2 - 1) as i:
                    two_slices(i, True)
                two_slices(NSLICE // 2 - 1, False)
                for b in range(nb):
                    sp.wait_ge(stored[b], 16 * (NSLICE // 2) * (per // nb))

            @block.tensor
            def _(pe):
                for g in range(3):
                    pe.wait_ge(x_loaded[g], 16)
                with pe.Fori(0, NSLICE // 2) as i:
                    for q in range(per):
                        u, m, b = q // TILES, q % TILES, q % nb
                        if m == 0:
                            pe.wait_ge(w_loaded[u], (i + 1) * 16)
                        pe.wait_ge(bank_free[q % 2], i * TILES + q // 2 + 1)
                        for k in range(KD):
                            mm = nc.tensor.matmul(bank[b][:, 0:SLICE], xT[:, m, k], w[u][:, k], start=(k == 0), stop=(k == KD - 1))
                        mm.then_inc(summed, 1)

            def copy_out(eng, e, copy):
                eng.sem_inc(bank_free[e], nb // 2)
                with eng.Fori(0, NSLICE // 2) as i:
                    for q in range(e, per, 2):
                        b = q % nb
                        eng.wait_ge(summed, i * per + q + 1)
                        eng.wait_ge(stored[b], (i * (per // nb) + q // nb) * 16)
                        copy(stage[b][:], bank[b][:, 0:SLICE]).then_inc(bank_free[e], 1)

            @block.scalar
            def _(act):
                copy_out(act, 0, nc.scalar.copy)

            @block.vector
            def _(dve):
                copy_out(dve, 1, nc.vector.tensor_copy)


def mixer(nc, proj, vecs, w_lora, w_gate, fconst, mconst, ident_d, s0T_d, r0_d, yT_d, wkv_p, ret_p, wkv_s, ret_s):
    with ExitStack() as ctx:
        def sb(name, shape):
            return ctx.enter_context(nc.sbuf_tensor("mx_" + name, shape, F32))

        def two(name, shape):
            return [sb(f"{name}{u}", shape) for u in range(2)]

        def sig(name, per, by=1):
            return Signal(nc, ctx, "mx_" + name, per, by)

        vec = sb("vec", [P, VEC_N])
        wlo = sb("wlo", [P, WA])
        wga = sb("wga", [P, WA])
        mc = sb("mc", [P, MC_N])
        ident = sb("ident", [P, P])
        halves = sb("halves", [P, 8])
        one = sb("one", [P, 1])
        fc = two("fc", [P, FC_N])
        cur = sb("cur", [P, SHIFT_W])
        sh = two("sh", [P, SHIFT_W])
        curB = two("curB", [P, IN_W - SHIFT_W])
        loraT = sb("loraT", [P, 2 * P])
        lw = sb("lw", [P, WA])
        ga = sb("ga", [P, WA])
        gate = two("gate", [P, WA])
        kk = sb("kk", [P, WA])
        kp = sb("kp", [P, WA])
        t1 = sb("t1", [P, WA])
        t3 = sb("t3", [P, WA])
        e1 = sb("e1", [P, WA])
        e2 = sb("e2", [P, WA])
        e3 = sb("e3", [P, WA])
        ss = sb("ss", [P, HA])
        rn = sb("rn", [P, HA])
        em = two("em", [P, HA // 2, DB])
        bt = two("bt", [P, WA])
        kt = two("kt", [P, WA])
        bonus = two("bonus", [P, HA])
        rot = sb("rot", [P, 2 * HB * NK])
        qh = sb("qh", [P, HB * NK])
        kh = two("kh", [P, HB * NK])
        arT = sb("arT", [P, HA // 2, 2, P])
        bT = sb("bT", [P, HA // 2, P])
        kT = sb("kT", [P, HA // 2, P])
        qT = sb("qT", [P, 4, P])
        kTr = sb("kTr", [P, 2, P])
        G = sb("G", [P, HA, 4, P])
        scT = sb("scT", [P, HB, P])
        ET = two("ET", [P, 4, P])
        M = two("M", [P, 4, P])
        MT = two("MT", [P, 4, P])
        X = two("X", [P, 4, P])
        wsb = sb("wsb", [P, HA, NA])
        usb = sb("usb", [P, HA, NA])
        S = sb("S", [P, HA // 2, NA])
        S0 = sb("S0", [P, HA // 2, 2, NA])
        R = sb("R", [P, HB // 2, 2, NV])
        t2 = sb("t2", [P, WA])
        y = sb("y", [P, HA + HB * 2, NA])
        sq = sb("sq", [P, WA])
        sg = sb("sg", [P, WA])
        mean = sb("mean", [P, HA + HB])
        var = sb("var", [P, HA + HB])
        rs = sb("rs", [P, HA + HB])
        yT = sb("yT", [P, KD, P])
        mcs = sb("mcs", [P, MC_N])
        s0T = sb("s0T", [P, DB, 4, NA])
        r0 = sb("r0", [P, DB, 2, NV])
        wTs = sb("wTs", [64, 2, 4, 2, TS])
        oTs = sb("oTs", [P, 2, 2, TS])
        B = [ctx.enter_context(nc.psum_tensor(f"mx_ps{b}", [P, 512], F32)) for b in range(8)]

        def v(name, width=WA):
            return vec[:, VEC_OFF[name]:VEC_OFF[name] + width]

        def heads(x, n):
            return x.rearrange("p (h d) -> p h d", h=n)

        def over(x, n):
            return x.unsqueeze(2).broadcast_to([P, x.shape[1], n])

        const_in = sig("const_in", 1)
        half_set = sig("half_set", 1)
        s_zero = sig("s_zero", 1)
        cur_in = [sig(f"cur_in{u}", 1, 16) for u in range(2)]
        sh_in = [sig(f"sh_in{u}", 1, 16) for u in range(2)]
        curB_in = [sig(f"curB_in{u}", 1, 16) for u in range(2)]
        fc_in = [sig(f"fc_in{u}", 1, 16) for u in range(2)]
        mix_d = sig("mix_d", 3)
        lora_d = sig("lora_d", 1)
        z_d = sig("z_d", 2)
        lwa_d = sig("lwa_d", 2)
        kk_d = sig("kk_d", 7)
        scaled_d = sig("scaled_d", 4)
        bonus_d = sig("bonus_d", 3)
        rot_d = sig("rot_d", 6)
        gram_d = sig("gram_d", HA)
        sc_d = sig("sc_d", 2)
        s0_d = sig("s0_d", 2)
        m0_d = sig("m0_d", 4)
        m_d = sig("m_d", 2 * (LEVELS - 2))
        mt_d = sig("mt_d", 2 * (LEVELS - 1))
        state_d = sig("state_d", 7)
        ya_d = sig("ya_d", 11)
        yb_d = sig("yb_d", 9)
        lora_a = sig("lora_a", 2)
        loraT_a = sig("loraT_a", 1)
        tz_a = sig("tz_a", 2)
        gate_a = sig("gate_a", 1)
        kksq_a = sig("kksq_a", 1)
        exp_a = sig("exp_a", 4)
        turn_a = sig("turn_a", 6)
        x_a = sig("x_a", 2 * (LEVELS - 1))
        w_a = sig("w_a", 1)
        u_a = sig("u_a", 1)
        sil_a = sig("sil_a", 1)
        sq_a = sig("sq_a", 2)
        yT_a = sig("yT_a", 2)
        rn_g = sig("rn_g", 1)
        mt0_g = sig("mt0_g", 4)
        et_g = sig("et_g", 2 * (LEVELS - 1))
        rs_g = sig("rs_g", 2)
        sil1_g = sig("sil1_g", 1)
        sil_g = sig("sil_g", 1)
        loraT_p = sig("loraT_p", 1)
        z_p = sig("z_p", 3)
        cum_p = sig("cum_p", 3)
        turn_p = sig("turn_p", 6)
        gram_p = sig("gram_p", HA)
        sc_p = sig("sc_p", 1)
        l0_p = sig("l0_p", 2)
        x_p = sig("x_p", 2 * (LEVELS - 1))
        m_p = sig("m_p", 2 * (LEVELS - 2))
        mt_p = sig("mt_p", 2 * (LEVELS - 1))
        w_p = sig("w_p", 1)
        u_p = sig("u_p", 1)
        y_p = sig("y_p", 1)
        ds_p = sig("ds_p", 1)
        o_p = sig("o_p", 1)
        dr_p = sig("dr_p", 1)
        yT_p = sig("yT_p", 2)
        yT_out = sig("yT_out", 1, 16)
        s0T_in = sig("s0T_in", 1, 16)
        blk_d = sig("blk_d", 8)
        sum_d = sig("sum_d", 4)
        new_d = sig("new_d", 8)
        new_p = sig("new_p", 8)
        sw_p = sig("sw_p", 1)
        sw_a = sig("sw_a", 4)
        st_out = sig("st_out", 1, 16)

        ex = ctx.enter_context(ExitStack())
        block = ex.enter_context(nc.Block())

        def tiles(eng, prologue, body, epilogue):
            prologue()
            with eng.Fori(0, NT // 2) as i:
                for u in range(2):
                    body(2 * i + u, u, i)
            epilogue()

        @block.sync
        def _(sp):
            for dst, src in ((vec, vecs.broadcast_to([P, VEC_N])), (wlo, w_lora), (wga, w_gate), (mc, mconst[0]), (mcs, mconst[1]), (ident, ident_d)):
                sp.dma_start(dst[:], src).then_inc(const_in.sem, 16)

            def load(t, u, k, sample=False):
                sp.wait_ge(mix_d.sem, mix_d.at(t, 0))
                if sample:
                    rows = proj[SAMPLE0:SAMPLE0 + DB * (DS + 1)].rearrange("(b t) c -> b t c", b=DB)
                    sp.dma_start(cur[0:TS, :], rows[:, 1:, 0:SHIFT_W]).then_inc(cur_in[u].sem, 16)
                    sp.dma_start(sh[u][0:TS, :], rows[:, :DS, 0:SHIFT_W]).then_inc(sh_in[u].sem, 16)
                    sp.dma_start(curB[u][0:TS, :], rows[:, 1:, SHIFT_W:]).then_inc(curB_in[u].sem, 16)
                else:
                    own = proj[1:1 + SEQ].rearrange("(n p) c -> n p c", p=P)[t]
                    sp.dma_start(cur[:], own[:, 0:SHIFT_W]).then_inc(cur_in[u].sem, 16)
                    sp.dma_start(sh[u][:], proj[0:SEQ].rearrange("(n p) c -> n p c", p=P)[t, :, 0:SHIFT_W]).then_inc(sh_in[u].sem, 16)
                    sp.dma_start(curB[u][:], own[:, SHIFT_W:]).then_inc(curB_in[u].sem, 16)
                sp.dma_start(fc[u][:], fconst[t]).then_inc(fc_in[u].sem, 16)

            def store(t):
                sp.wait_ge(yT_a.sem, yT_a.at(t))
                sp.dma_start(yT_d[t], yT[:]).then_inc(yT_out.sem, 16)

            load(0, 0, 0)
            sp.dma_start(s0T[:], s0T_d).then_inc(s0T_in.sem, 16)
            sp.dma_start(r0[:], r0_d).then_inc(s0T_in.sem, 16)
            with sp.Fori(0, NT // 2 - 1) as i:
                load(2 * i + 1, 1, i)
                store(2 * i)
                load(2 * i + 2, 0, i + 1)
                store(2 * i + 1)
            load(NT - 1, 1, NT // 2 - 1)
            store(NT - 2)
            load(NT, 0, NT // 2, sample=True)
            store(NT - 1)
            sp.wait_ge(state_d.sem, state_d.at(NT - 1))
            sp.dma_start(wkv_p, S[:]).then_inc(st_out.sem, 16)
            for o in range(2):
                r = slice(64 * o, 64 * o + 64)
                sp.dma_start(ret_p[r], R[r, :, o]).then_inc(st_out.sem, 16)
            store(NT)
            sp.wait_ge(new_d.sem, 8)
            sp.dma_start(wkv_s, s0T[:]).then_inc(st_out.sem, 16)
            sp.dma_start(ret_s, r0[:]).then_inc(st_out.sem, 16)
            sp.wait_ge(yT_out.sem, yT_out.at(NT))
            sp.wait_ge(st_out.sem, 16 * 5)

        @block.tensor
        def _(pe):
            mm = nc.tensor.matmul

            def f_loraT(t, u):
                pe.wait_ge(lora_d.sem, lora_d.at(t))
                pe.wait_ge(exp_a.sem, exp_a.at(t, 0))
                nc.tensor.transpose(B[0][:, 0:P], sh[u][:, 3 * WA:3 * WA + P], ident[:])
                nc.tensor.transpose(B[0][:, P:2 * P], sh[u][:, 3 * WA + P:3 * WA + 2 * P], ident[:]).then_inc(loraT_p.sem, 1)

            def f_z(t, u):
                pe.wait_ge(loraT_a.sem, loraT_a.at(t))
                mm(B[1][:], loraT[0:64, 0:P], wlo[0:64, :], start=True, stop=True).then_inc(z_p.sem, 1)
                mm(B[0][:], loraT[64:128, 0:P], wlo[64:128, :], start=True, stop=True).then_inc(z_p.sem, 1)
                pe.wait_ge(z_d.sem, z_d.at(t, 1))
                mm(B[1][:], loraT[:, P:2 * P], wga[:], start=True, stop=True).then_inc(z_p.sem, 1)

            def f_cum(t, u):
                pe.wait_ge(lwa_d.sem, lwa_d.at(t, 1))
                mm(B[0][:], fc[u][:, FC_TI:FC_TI + P], lw[:], start=True, stop=True).then_inc(cum_p.sem, 1)
                pe.wait_ge(gate_a.sem, gate_a.at(t))
                mm(B[1][:], fc[u][:, FC_TE:FC_TE + P], lw[:], start=True, stop=True).then_inc(cum_p.sem, 1)
                pe.wait_ge(exp_a.sem, exp_a.at(t, 2))
                for q in range(HA // 2):
                    m = mm(B[0][:, q * DB:(q + 1) * DB], lw[:, q * P:(q + 1) * P], fc[u][:, FC_SEL:FC_SEL + DB], start=True, stop=True)
                m.then_inc(cum_p.sem, 1)

            def turn(t, u):
                srcs = [(e2, scaled_d, 4), (bt[u], scaled_d, 1), (e1, scaled_d, 3), (kt[u], scaled_d, 2)]
                for n, (src, s, j) in enumerate(srcs):
                    pe.wait_ge(s.sem, s.at(t, j))
                    if n < 2:
                        pe.wait_ge(yT_a.sem, yT_a.at(t, 0))
                    else:
                        pe.wait_ge(turn_a.sem, turn_a.at(t, n - 1))
                    for q in range(4):
                        m = nc.tensor.transpose(B[2 + n % 2][:, q * P:(q + 1) * P], src[:, q * P:(q + 1) * P], ident[:])
                    m.then_inc(turn_p.sem, 1)
                pe.wait_ge(rot_d.sem, rot_d.at(t))
                pe.wait_ge(turn_a.sem, turn_a.at(t, 3))
                for q in range(4):
                    src = rot[:, q * P:(q + 1) * P] if q < 2 else qh[:, (q - 2) * P:(q - 1) * P]
                    m = nc.tensor.transpose(B[2][:, q * P:(q + 1) * P], src, ident[:])
                m.then_inc(turn_p.sem, 1)
                pe.wait_ge(turn_a.sem, turn_a.at(t, 4))
                for q in range(2):
                    m = nc.tensor.transpose(B[3][:, q * P:(q + 1) * P], rot[:, (q + 2) * P:(q + 3) * P], ident[:])
                m.then_inc(turn_p.sem, 1)

            def grams(t):
                pe.wait_ge(turn_a.sem, turn_a.at(t, 4))
                pe.wait_ge(state_d.sem, state_d.at(t, 0))
                for h in range(HA):
                    q, r = h // 2, slice(64 * (h % 2), 64 * (h % 2) + 64)
                    if h >= 2:
                        pe.wait_ge(gram_d.sem, gram_d.at(t, h - 1))
                    mm(B[4 + h % 2][:, 0:2 * P], bT[r, q], arT[r, q], start=True, stop=True)
                    mm(B[4 + h % 2][:, 2 * P:], kT[r, q], arT[r, q], start=True, stop=True).then_inc(gram_p.sem, 1)
                pe.wait_ge(turn_a.sem, turn_a.at(t, 6))
                for h in (0, 2, 1, 3):
                    q, r = h // 2, slice(64 * (h % 2), 64 * (h % 2) + 64)
                    m = mm(B[6 + h % 2][:, q * P:(q + 1) * P], kTr[r, q], qT[r, q], start=True, stop=True)
                m.then_inc(sc_p.sem, 1)
                for g in range(2):
                    pe.wait_ge(gram_d.sem, gram_d.at(t, 4 * g + 4))
                    for h in range(4):
                        m = nc.tensor.transpose(B[2 + g][:, h * P:(h + 1) * P], G[:, 4 * g + h, 0], ident[:])
                    m.then_inc(l0_p.sem, 1)

            def level(t, j, last=LEVELS - 1):
                n = 2 * (j - 1)
                for g in range(2):
                    pe.wait_ge(et_g.sem, et_g.at(t, n + g + 1))
                    if j == 1:
                        pe.wait_ge(m0_d.sem, m0_d.at(t, 2 * g + 2))
                    else:
                        pe.wait_ge(m_d.sem, m_d.at(t, n - 2 + g + 1))
                    for h in range(4):
                        m = mm(B[2 + g][:, h * P:(h + 1) * P], ET[g][:, h], M[g][:, h], start=True, stop=True)
                    m.then_inc(x_p.sem, 1)
                for g in range(2):
                    pe.wait_ge(x_a.sem, x_a.at(t, n + g + 1))
                    if j == 1:
                        pe.wait_ge(mt0_g.sem, mt0_g.at(t, 2 * g + 2))
                        pe.wait_ge(gram_d.sem, gram_d.at(t))
                        pe.wait_ge(sc_d.sem, sc_d.at(t))
                    else:
                        pe.wait_ge(mt_d.sem, mt_d.at(t, n - 2 + g + 1))
                    if j < last:
                        for h in range(4):
                            m = mm(B[4 + g][:, h * P:(h + 1) * P], MT[g][:, h], X[g][:, h], start=True, stop=True)
                        m.then_inc(m_p.sem, 1)
                    for h in range(4):
                        m = mm(B[6 + g][:, h * P:(h + 1) * P], X[g][:, h], MT[g][:, h], start=True, stop=True)
                    m.then_inc(mt_p.sem, 1)

            def chunk(t, u, i, sample, last):
                n = TS if sample else P
                vA, vB = sh[u], curB[u]
                pe.wait_ge(mt_d.sem, mt_d.at(t, 2 * last))
                if sample:
                    pe.wait_ge(s0T_in.sem, 32)
                    for par in range(2):
                        r = slice(64 * par, 64 * par + 64)
                        for q in range(4):
                            for b in range(DB):
                                out = B[2 + par][0:64, q * P:(q + 1) * P].rearrange("p (w t) -> p w t", w=2)[:, :, b * DS:(b + 1) * DS]
                                m = mm(out, s0T[r, b, q], arT[r, q, :, b * DS:(b + 1) * DS], start=True, stop=True)
                        m.then_inc(sw_p.sem, 1)
                        for q in range(2):
                            for b in range(DB):
                                m = mm(B[6 + par][:, q * TS + b * DS:q * TS + (b + 1) * DS], r0[r, b, q], qT[r, 2 + q, b * DS:(b + 1) * DS], start=True, stop=True)
                        m.then_inc(sw_p.sem, 1)
                    pe.wait_ge(sw_a.sem, 4)
                else:
                    pe.wait_ge(state_d.sem, state_d.at(t, 0))
                for h in range(HB):
                    q, r = h // 2, slice(64 * (h % 2), 64 * (h % 2) + 64)
                    o = B[6][0:n, h * NV:(h + 1) * NV]
                    if sample:
                        mm(o, oTs[:, h % 2, q], ident[:], start=True, stop=False)
                    elif h % 2 == 0:
                        mm(B[6][:, h * NV:(h + 2) * NV], qT[:, 2 + q], R[:, q], start=True, stop=False)
                    m = mm(o, scT[0:n, h, 0:n], vB[0:n, 512 + h * NV:512 + (h + 1) * NV], start=False, stop=sample or h % 2 == 1)
                m.then_inc(o_p.sem, 1)
                if not sample:
                    for h in range(HB):
                        q, r = h // 2, slice(64 * (h % 2), 64 * (h % 2) + 64)
                        m = mm(B[7][r, q * NV:(q + 1) * NV], kh[u][:, h * NK:(h + 1) * NK], vB[:, 512 + h * NV:512 + (h + 1) * NV], start=True, stop=True)
                    m.then_inc(dr_p.sem, 1)
                    pe.wait_ge(s0_d.sem, s0_d.at(t))
                pe.wait_ge(x_a.sem, x_a.at(t, 2 * last))
                for h in range(HA):
                    q, r = h // 2, slice(64 * (h % 2), 64 * (h % 2) + 64)
                    o = B[2][0:n, h * NA:(h + 1) * NA]
                    if sample:
                        mm(o, wTs[0:64, h % 2, q, 0], ident[0:64, 0:64], start=True, stop=False)
                    elif h % 2 == 0:
                        mm(B[2][:, h * NA:(h + 2) * NA], arT[:, q, 0], S0[:, q], start=True, stop=False)
                    m = mm(o, G[0:n, h, 2, 0:n], vA[0:n, 2 * WA + h * NA:2 * WA + (h + 1) * NA], start=False, stop=sample or h % 2 == 1)
                m.then_inc(w_p.sem, 1)
                pe.wait_ge(w_a.sem, w_a.at(t))
                for h in range(HA):
                    m = mm(B[3][0:n, h * NA:(h + 1) * NA], MT[h // 4][0:n, h % 4, 0:n], wsb[0:n, h], start=True, stop=True)
                m.then_inc(u_p.sem, 1)
                pe.wait_ge(u_a.sem, u_a.at(t))
                pe.wait_ge(m_d.sem, m_d.at(t, 2 * last - 2))
                if not sample:
                    for h in range(HA):
                        q, r = h // 2, slice(64 * (h % 2), 64 * (h % 2) + 64)
                        cols, val = slice(h * NA, (h + 1) * NA), slice(2 * WA + h * NA, 2 * WA + (h + 1) * NA)
                        mm(B[5][r, q * NA:(q + 1) * NA], bt[u][:, cols], usb[:, h], start=True, stop=False)
                        m = mm(B[5][r, q * NA:(q + 1) * NA], kt[u][:, cols], vA[:, val], start=False, stop=True)
                    m.then_inc(ds_p.sem, 1)
                for h in range(HA):
                    q, r = h // 2, slice(64 * (h % 2), 64 * (h % 2) + 64)
                    o = B[4][0:n, h * NA:(h + 1) * NA]
                    if sample:
                        mm(o, wTs[0:64, h % 2, q, 1], ident[0:64, 0:64], start=True, stop=False)
                    elif h % 2 == 0:
                        mm(B[4][:, h * NA:(h + 2) * NA], arT[:, q, 1], S0[:, q], start=True, stop=False)
                    mm(o, G[0:n, h, 1, 0:n], usb[0:n, h], start=False, stop=False)
                    m = mm(o, G[0:n, h, 3, 0:n], vA[0:n, 2 * WA + h * NA:2 * WA + (h + 1) * NA], start=False, stop=sample or h % 2 == 1)
                m.then_inc(y_p.sem, 1)

            def sampled_states(t, u):
                pe.wait_ge(exp_a.sem, exp_a.at(t))
                for j in range(8):
                    bank = B[5] if j % 2 == 0 else B[0]
                    pe.wait_ge(blk_d.sem, j + 1)
                    if j >= 2:
                        pe.wait_ge(new_d.sem, j - 1)
                    for o in range(2):
                        r = slice(64 * o, 64 * o + 64)
                        if j < 4:
                            cols = slice((2 * j + o) * NA, (2 * j + o + 1) * NA)
                            mm(bank[r, :], bt[u][0:TS, cols], X[o][0:TS], start=True, stop=False)
                            m = mm(bank[r, :], kt[u][0:TS, cols], ET[o][0:TS], start=False, stop=True)
                        else:
                            h = 2 * (j % 2) + o
                            m = mm(bank[r, :], kh[u][0:TS, h * NK:(h + 1) * NK], X[o][0:TS], start=True, stop=True)
                    m.then_inc(new_p.sem, 1)

            def turn_y(t):
                for n, (s, b) in enumerate(((ya_d, 2), (yb_d, 3))):
                    pe.wait_ge(s.sem, s.at(t))
                    pe.wait_ge(yT_a.sem, yT_a.at(t, 0))
                    for q in range(4):
                        src = y[:, 8 * n + 2 * q:8 * n + 2 * q + 2].rearrange("p h d -> p (h d)")
                        m = nc.tensor.transpose(B[b][:, q * P:(q + 1) * P], src, ident[:])
                    m.then_inc(yT_p.sem, 1)

            def start():
                pe.wait_ge(const_in.sem, 16 * NCONST)
                pe.wait_ge(fc_in[0].sem, 16)
                f_loraT(0, 0)
                f_z(0, 0)
                f_cum(0, 0)

            def body(t, u, i):
                turn(t, u)
                grams(t)
                level(t, 1)
                level(t, 2)
                f_loraT(t + 1, 1 - u)
                level(t, 3)
                f_z(t + 1, 1 - u)
                level(t, 4)
                level(t, 5)
                pe.wait_ge(fc_in[1 - u].sem, (i + 1 + u) * 16)
                f_cum(t + 1, 1 - u)
                level(t, 6)
                chunk(t, u, i, False, LEVELS - 1)
                turn_y(t)

            def end():
                turn(NT, 0)
                grams(NT)
                level(NT, 1, LEVELS_S - 1)
                level(NT, 2, LEVELS_S - 1)
                chunk(NT, 0, NT // 2, True, LEVELS_S - 1)
                turn_y(NT)
                sampled_states(NT, 0)

            tiles(pe, start, body, end)

        @block.scalar
        def _(act):
            fn = nc.scalar.activation
            cp = nc.scalar.copy

            def f_lora(t, u):
                act.wait_ge(mix_d.sem, mix_d.at(t))
                w, g = sh[u][:, 3 * WA:3 * WA + 64], sh[u][:, 3 * WA + P:3 * WA + 2 * P]
                fn(w, w, ACT.Tanh).then_inc(lora_a.sem, 1)
                fn(g, g, ACT.Tanh, scale=0.5).then_inc(lora_a.sem, 1)

            def f_kksq(t):
                act.wait_ge(kk_d.sem, kk_d.at(t, 1))
                fn(e3[:], kk[:], ACT.Square).then_inc(kksq_a.sem, 1)

            def f_loraT(t):
                act.wait_ge(loraT_p.sem, loraT_p.at(t))
                cp(loraT[:], B[0][:, 0:2 * P]).then_inc(loraT_a.sem, 1)

            def f_z(t, u):
                act.wait_ge(z_d.sem, z_d.at(t, 1))
                fn(lw[:], lw[:], ACT.Tanh, scale=0.5).then_inc(tz_a.sem, 1)
                act.wait_ge(z_d.sem, z_d.at(t, 2))
                fn(ga[:], ga[:], ACT.Tanh, scale=0.5).then_inc(tz_a.sem, 1)
                act.wait_ge(z_p.sem, z_p.at(t, 3))
                cp(gate[u][:], B[1][:]).then_inc(gate_a.sem, 1)

            def f_exp(t, u):
                act.wait_ge(cum_p.sem, cum_p.at(t, 1))
                fn(e1[:], B[0][:], ACT.Exp).then_inc(exp_a.sem, 1)
                act.wait_ge(kk_d.sem, kk_d.at(t, 2))
                fn(e3[:], B[0][:], ACT.Exp, scale=-1.0).then_inc(exp_a.sem, 1)
                act.wait_ge(cum_p.sem, cum_p.at(t, 2))
                fn(e2[:], B[1][:], ACT.Exp).then_inc(exp_a.sem, 1)
                act.wait_ge(cum_p.sem, cum_p.at(t, 3))
                fn(em[u][:], B[0][:, 0:HA // 2 * DB].rearrange("p (q b) -> p q b", b=DB), ACT.Exp).then_inc(exp_a.sem, 1)

            def turn(t):
                outs = [(arT[:, :, 0], 2, 512), (bT[:], 3, 512), (arT[:, :, 1], 2, 512), (kT[:], 3, 512), (qT[:], 2, 512), (kTr[:], 3, 256)]
                for n, (out, b, w) in enumerate(outs):
                    act.wait_ge(turn_p.sem, turn_p.at(t, n + 1))
                    cp(out, B[b][:, 0:w].rearrange("p (q t) -> p q t", t=P)).then_inc(turn_a.sem, 1)

            def level(t, j):
                for g in range(2):
                    n = 2 * (j - 1) + g + 1
                    act.wait_ge(x_p.sem, x_p.at(t, n))
                    if j > 1:
                        act.wait_ge(mt_p.sem, mt_p.at(t, n - 2))
                    cp(X[g][:], B[2 + g][:].rearrange("p (h t) -> p h t", t=P)).then_inc(x_a.sem, 1)

            def tail(t, u, n, sample):
                if sample:
                    for par in range(2):
                        act.wait_ge(sw_p.sem, 2 * par + 1)
                        cp(wTs[:, par], B[2 + par][0:64, :].rearrange("p (q w t) -> p q w t", q=4, w=2)).then_inc(sw_a.sem, 1)
                        act.wait_ge(sw_p.sem, 2 * par + 2)
                        cp(oTs[:, par], B[6 + par][:, 0:2 * TS].rearrange("p (q t) -> p q t", q=2)).then_inc(sw_a.sem, 1)
                fn(sg[:], curB[u][:, 1024:1536], ACT.Tanh, scale=0.5).then_inc(sil_a.sem, 1)
                act.wait_ge(w_p.sem, w_p.at(t))
                cp(wsb[0:n], B[2][0:n].rearrange("p (h d) -> p h d", h=HA)).then_inc(w_a.sem, 1)
                act.wait_ge(u_p.sem, u_p.at(t))
                cp(usb[0:n], B[3][0:n].rearrange("p (h d) -> p h d", h=HA)).then_inc(u_a.sem, 1)
                act.wait_ge(yb_d.sem, yb_d.at(t, 3))
                fn(sq[:], y[:, 8:16].rearrange("p h d -> p (h d)"), ACT.Square).then_inc(sq_a.sem, 1)
                act.wait_ge(ya_d.sem, ya_d.at(t, 3))
                fn(t2[:], y[:, 0:8].rearrange("p h d -> p (h d)"), ACT.Square).then_inc(sq_a.sem, 1)
                act.wait_ge(yT_out.sem, yT_out.at(t, 0))
                for k in range(2):
                    act.wait_ge(yT_p.sem, yT_p.at(t, k + 1))
                    cp(yT[:, 4 * k:4 * k + 4], B[2 + k][:].rearrange("p (k t) -> p k t", t=P)).then_inc(yT_a.sem, 1)

            def start():
                f_lora(0, 0)
                f_kksq(0)
                f_loraT(0)
                f_z(0, 0)
                f_exp(0, 0)

            def body(t, u, i):
                turn(t)
                level(t, 1)
                f_lora(t + 1, 1 - u)
                level(t, 2)
                f_kksq(t + 1)
                f_loraT(t + 1)
                level(t, 3)
                level(t, 4)
                f_z(t + 1, 1 - u)
                level(t, 5)
                f_exp(t + 1, 1 - u)
                level(t, 6)
                tail(t, u, P, False)

            def end():
                turn(NT)
                level(NT, 1)
                level(NT, 2)
                tail(NT, 0, TS, True)

            tiles(act, start, body, end)

        @block.vector
        def _(dve):
            tt = nc.vector.tensor_tensor
            ts = nc.vector.tensor_scalar
            stt = nc.vector.scalar_tensor_tensor

            def f_mix(t, u, k):
                dve.wait_ge(cur_in[u].sem, (k + 1) * 16)
                dve.wait_ge(sh_in[u].sem, (k + 1) * 16)
                tt(sh[u][:], sh[u][:], cur[:], ALU.subtract).then_inc(mix_d.sem, 1)
                dve.wait_ge(mix_d.sem, mix_d.at(t, 1))
                tt(sh[u][:], sh[u][:], v("mu_shift", SHIFT_W), ALU.mult).then_inc(mix_d.sem, 1)
                dve.wait_ge(mix_d.sem, mix_d.at(t, 2))
                tt(sh[u][:], sh[u][:], cur[:], ALU.add).then_inc(mix_d.sem, 1)

            def f_lora(t, u):
                dve.wait_ge(lora_a.sem, lora_a.at(t))
                g = sh[u][:, 3 * WA + P:3 * WA + 2 * P]
                ts(g, g, 0.5, 0.5, ALU.mult, ALU.add).then_inc(lora_d.sem, 1)

            def f_kk1(t, u):
                dve.wait_ge(mix_d.sem, mix_d.at(t))
                tt(kk[:], sh[u][:, WA:2 * WA], v("k_k"), ALU.mult).then_inc(kk_d.sem, 1)
                dve.wait_ge(kksq_a.sem, kksq_a.at(t))
                nc.vector.tensor_reduce(ss[:], heads(e3[:], HA), AX, ALU.add).then_inc(kk_d.sem, 1)
                dve.wait_ge(kk_d.sem, kk_d.at(t, 2))
                ts(ss[:], ss[:], 1e-24, None, ALU.max).then_inc(kk_d.sem, 1)

            def f_z(t):
                dve.wait_ge(z_p.sem, z_p.at(t, 1))
                tt(lw[:], B[1][:], v("decay_base"), ALU.add).then_inc(z_d.sem, 1)
                dve.wait_ge(z_p.sem, z_p.at(t, 2))
                tt(ga[:], B[0][:], v("aaa_base"), ALU.add).then_inc(z_d.sem, 1)

            def f_lwa(t):
                dve.wait_ge(tz_a.sem, tz_a.at(t, 1))
                ts(lw[:], lw[:], 1.0, W_CONST / 2, ALU.add, ALU.mult).then_inc(lwa_d.sem, 1)
                dve.wait_ge(tz_a.sem, tz_a.at(t, 2))
                ts(ga[:], ga[:], 0.5, 0.5, ALU.mult, ALU.add).then_inc(lwa_d.sem, 1)

            def f_kk2(t, u):
                dve.wait_ge(rn_g.sem, rn_g.at(t))
                tt(heads(kk[:], HA), heads(kk[:], HA), over(rn[:], NA), ALU.mult).then_inc(kk_d.sem, 1)
                dve.wait_ge(lwa_d.sem, lwa_d.at(t))
                dve.wait_ge(kk_d.sem, kk_d.at(t, 4))
                tt(bt[u][:], kk[:], ga[:], ALU.mult).then_inc(kk_d.sem, 1)
                if not isinstance(t, int):
                    dve.wait_ge(ya_d.sem, ya_d.at(t - 1, 0))
                stt(t1[:], ga[:], -1.0, v("k_a"), ALU.add, ALU.mult).then_inc(kk_d.sem, 1)
                dve.wait_ge(kk_d.sem, kk_d.at(t, 6))
                stt(kp[:], t1[:], 1.0, sh[u][:, WA:2 * WA], ALU.add, ALU.mult).then_inc(kk_d.sem, 1)

            def f_scale(t, u):
                dve.wait_ge(exp_a.sem, exp_a.at(t, 2))
                dve.wait_ge(kk_d.sem, kk_d.at(t, 7))
                tt(bt[u][:], bt[u][:], e3[:], ALU.mult).then_inc(scaled_d.sem, 1)
                tt(kt[u][:], kp[:], e3[:], ALU.mult).then_inc(scaled_d.sem, 1)
                tt(e1[:], e1[:], sh[u][:, 0:WA], ALU.mult).then_inc(scaled_d.sem, 1)
                dve.wait_ge(exp_a.sem, exp_a.at(t, 3))
                stt(e2[:], kk[:], -1.0, e2[:], ALU.mult, ALU.mult).then_inc(scaled_d.sem, 1)
                dve.wait_ge(rot_d.sem, rot_d.at(t))
                tt(t1[:], sh[u][:, 0:WA], kp[:], ALU.mult).then_inc(bonus_d.sem, 1)
                dve.wait_ge(bonus_d.sem, bonus_d.at(t, 1))
                tt(t1[:], t1[:], v("r_k"), ALU.mult).then_inc(bonus_d.sem, 1)
                dve.wait_ge(bonus_d.sem, bonus_d.at(t, 2))
                nc.vector.tensor_reduce(bonus[u][:], heads(t1[:], HA), AX, ALU.add).then_inc(bonus_d.sem, 1)

            def f_rot(t, u, k):
                dve.wait_ge(curB_in[u].sem, (k + 1) * 16)
                dve.wait_ge(fc_in[u].sem, (k + 1) * 16)
                dve.wait_ge(kk_d.sem, kk_d.at(t, 7))
                x = curB[u][:, 0:512].rearrange("p (n d) -> p n d", d=32)
                cos = fc[u][:, FC_COS:FC_COS + 32].unsqueeze(1).broadcast_to([P, 16, 32])
                sin = fc[u][:, FC_SIN:FC_SIN + 32].unsqueeze(1).broadcast_to([P, 16, 32])
                a4, b4 = (z[:].rearrange("p (h two d) -> p h two d", two=2, d=32) for z in (t3, t1))
                r4 = rot[:].rearrange("p (h two d) -> p h two d", two=2, d=32)
                tt(t3[:].rearrange("p (n d) -> p n d", d=32), x, cos, ALU.mult).then_inc(rot_d.sem, 1)
                tt(t1[:].rearrange("p (n d) -> p n d", d=32), x, sin, ALU.mult).then_inc(rot_d.sem, 1)
                dve.wait_ge(rot_d.sem, rot_d.at(t, 2))
                tt(r4[:, :, 0], a4[:, :, 0], b4[:, :, 1], ALU.subtract).then_inc(rot_d.sem, 1)
                tt(r4[:, :, 1], b4[:, :, 0], a4[:, :, 1], ALU.add).then_inc(rot_d.sem, 1)
                dve.wait_ge(rot_d.sem, rot_d.at(t, 4))
                for out, c0, col in ((qh, 0, FC_CROSS), (kh[u], 256, FC_KDEC)):
                    tt(heads(out[:], HB), heads(rot[:, c0:c0 + 256], HB), over(fc[u][:, col:col + HB], NK), ALU.mult).then_inc(rot_d.sem, 1)

            def grams(t, u, c, sample):
                for h in range(HA):
                    dve.wait_ge(gram_p.sem, gram_p.at(t, h + 1))
                    tt(G[:, h].rearrange("p a b -> p (a b)"), B[4 + h % 2][:], c[:, MC_GRAM:MC_GRAM + 512], ALU.mult).then_inc(gram_d.sem, 1)
                dve.wait_ge(sc_p.sem, sc_p.at(t))
                for o in range(2):
                    dmask = c[:, MC_D + 256 * o:MC_D + 256 * o + 256].rearrange("p (h t) -> p h t", h=2)
                    tt(scT[:, o::2], B[6 + o][:, 0:256].rearrange("p (h t) -> p h t", h=2), dmask, ALU.mult).then_inc(sc_d.sem, 1)
                if not sample:
                    dve.wait_ge(exp_a.sem, exp_a.at(t))
                    dve.wait_ge(state_d.sem, state_d.at(t, 0))
                    for o in range(2):
                        r = slice(64 * o, 64 * o + 64)
                        decay = em[u][r, :, 0].unsqueeze(2).broadcast_to([64, 4, NA])
                        tt(S0[r, :, o], S[r], decay, ALU.mult).then_inc(s0_d.sem, 1)
                for g in range(2):
                    dve.wait_ge(l0_p.sem, l0_p.at(t, g + 1))
                    m0 = c[:, MC_M0:MC_M0 + P].unsqueeze(1).broadcast_to([P, 4, P])
                    tt(M[g][:], B[2 + g][:].rearrange("p (h t) -> p h t", t=P), m0, ALU.mult).then_inc(m0_d.sem, 1)
                    dve.wait_ge(m0_d.sem, m0_d.at(t, 2 * g + 1))
                    tt(M[g][:], M[g][:], ident[:].unsqueeze(1).broadcast_to([P, 4, P]), ALU.add).then_inc(m0_d.sem, 1)

            def level(t, j, last=LEVELS - 1):
                for g in range(2):
                    n = 2 * (j - 1) + g + 1
                    if j < last:
                        dve.wait_ge(m_p.sem, m_p.at(t, n))
                        tt(M[g][:], B[4 + g][:].rearrange("p (h t) -> p h t", t=P), M[g][:], ALU.add).then_inc(m_d.sem, 1)
                    dve.wait_ge(mt_p.sem, mt_p.at(t, n))
                    tt(MT[g][:], B[6 + g][:].rearrange("p (h t) -> p h t", t=P), MT[g][:], ALU.add).then_inc(mt_d.sem, 1)

            def moments(s, t, off, n, width, bank, dst, sqv, sq_step):
                dve.wait_ge(bank[0].sem, bank[0].at(t))
                src = heads(bank[1][:], n)
                nc.vector.tensor_reduce(mean[:, off:off + n], src, AX, ALU.add).then_inc(s.sem, 1)
                dve.wait_ge(s.sem, s.at(t, 1))
                ts(mean[:, off:off + n], mean[:, off:off + n], 1.0 / width, None, ALU.mult).then_inc(s.sem, 1)
                dve.wait_ge(s.sem, s.at(t, 2))
                tt(dst, src, over(mean[:, off:off + n], width), ALU.subtract).then_inc(s.sem, 1)

            def variance(s, t, off, n, width, sqv, sq_step, eps):
                dve.wait_ge(sq_a.sem, sq_a.at(t, sq_step))
                nc.vector.tensor_reduce(var[:, off:off + n], heads(sqv[:], n), AX, ALU.add).then_inc(s.sem, 1)
                dve.wait_ge(s.sem, s.at(t, 4))
                ts(var[:, off:off + n], var[:, off:off + n], 1.0 / width, eps, ALU.mult, ALU.add).then_inc(s.sem, 1)

            def tail(t, u, c, sample):
                yA, yB = y[:, 0:8], y[:, 8:16].rearrange("p (h a) d -> p h (a d)", a=2)
                moments(yb_d, t, HA, HB, NV, (o_p, B[6]), yB, sq, 1)
                if not sample:
                    dve.wait_ge(dr_p.sem, dr_p.at(t))
                    for h in range(HB):
                        q, r = h // 2, slice(64 * (h % 2), 64 * (h % 2) + 64)
                        stt(R[r, q, h % 2], R[r, q, h % 2], c[r, MC_CDEC + q:MC_CDEC + q + 1], B[7][r, q * NV:(q + 1) * NV], ALU.mult, ALU.add).then_inc(state_d.sem, 1)
                variance(yb_d, t, HA, HB, NV, sq, 1, GN_EPS_B)
                if not sample:
                    dve.wait_ge(ds_p.sem, ds_p.at(t))
                    for o in range(2):
                        r = slice(64 * o, 64 * o + 64)
                        tt(S[r], B[5][r, 0:256].rearrange("p (q d) -> p q d", q=4), S0[r, :, o], ALU.add).then_inc(state_d.sem, 1)
                    dve.wait_ge(state_d.sem, state_d.at(t, 6))
                    tt(S[:], S[:], over(em[u][:, :, 1], NA), ALU.mult).then_inc(state_d.sem, 1)
                moments(ya_d, t, 0, HA, NA, (y_p, B[4]), yA, t2, 2)
                dve.wait_ge(rs_g.sem, rs_g.at(t, 1))
                tt(yB, yB, over(rs[:, HA:HA + HB], NV), ALU.mult).then_inc(yb_d.sem, 1)
                dve.wait_ge(yb_d.sem, yb_d.at(t, 6))
                flatB, flatA = y[:, 8:16].rearrange("p h d -> p (h d)"), y[:, 0:8].rearrange("p h d -> p (h d)")
                tt(flatB, flatB, v("ret_gn_g"), ALU.mult).then_inc(yb_d.sem, 1)
                variance(ya_d, t, 0, HA, NA, t2, 2, GN_EPS_A)
                dve.wait_ge(yb_d.sem, yb_d.at(t, 7))
                tt(flatB, flatB, v("ret_gn_b"), ALU.add).then_inc(yb_d.sem, 1)
                dve.wait_ge(bonus_d.sem, bonus_d.at(t if sample else t + 1))
                tt(heads(t1[:], HA), heads(sh[u][:, 2 * WA:3 * WA], HA), over(bonus[u][:], NA), ALU.mult).then_inc(ya_d.sem, 1)
                dve.wait_ge(sil_g.sem, sil_g.at(t))
                dve.wait_ge(yb_d.sem, yb_d.at(t, 8))
                stt(flatB, flatB, 0.5, sg[:], ALU.mult, ALU.mult).then_inc(yb_d.sem, 1)
                dve.wait_ge(rs_g.sem, rs_g.at(t, 2))
                tt(yA, yA, over(rs[:, 0:HA], NA), ALU.mult).then_inc(ya_d.sem, 1)
                dve.wait_ge(ya_d.sem, ya_d.at(t, 7))
                tt(flatA, flatA, v("lnx_g"), ALU.mult).then_inc(ya_d.sem, 1)
                dve.wait_ge(ya_d.sem, ya_d.at(t, 8))
                tt(flatA, flatA, v("lnx_b"), ALU.add).then_inc(ya_d.sem, 1)
                dve.wait_ge(ya_d.sem, ya_d.at(t, 9))
                tt(flatA, flatA, t1[:], ALU.add).then_inc(ya_d.sem, 1)
                dve.wait_ge(gate_a.sem, gate_a.at(t))
                dve.wait_ge(ya_d.sem, ya_d.at(t, 10))
                tt(flatA, flatA, gate[u][:], ALU.mult).then_inc(ya_d.sem, 1)

            def sampled_states(t, u, c):
                blk = c[0:TS, MC_BLK:MC_BLK + DB]
                dve.wait_ge(u_a.sem, u_a.at(t))
                dve.wait_ge(exp_a.sem, exp_a.at(t))
                for j in range(8):
                    if j >= 1:
                        dve.wait_ge(new_p.sem, j)
                    for o in range(2):
                        if j < 4:
                            h = 2 * j + o
                            for dst, src in ((X[o], usb[0:TS, h]), (ET[o], sh[u][0:TS, 2 * WA + h * NA:2 * WA + (h + 1) * NA])):
                                out = dst[0:TS].rearrange("p a (c d) -> p (a c) d", d=NA)
                                m = tt(out, src.unsqueeze(1).broadcast_to([TS, DB, NA]), blk.unsqueeze(2).broadcast_to([TS, DB, NA]), ALU.mult)
                        else:
                            h, half = 2 * (j % 2) + o, (j - 4) // 2
                            src = curB[u][0:TS, 512 + h * NV:512 + (h + 1) * NV].unsqueeze(1).broadcast_to([TS, 4, NV])
                            m = tt(X[o][0:TS], src, blk[:, 4 * half:4 * half + 4].unsqueeze(2).broadcast_to([TS, 4, NV]), ALU.mult)
                    m.then_inc(blk_d.sem, 1)
                    dve.wait_ge(new_p.sem, j + 1)
                    bank = B[5] if j % 2 == 0 else B[0]
                    if j < 4:
                        st = s0T[:, :, j]
                        tt(st, bank[:].rearrange("p (b d) -> p b d", b=DB), st, ALU.add).then_inc(sum_d.sem, 1)
                        dve.wait_ge(sum_d.sem, j + 1)
                        tt(st, st, over(em[u][:, j], NA), ALU.mult).then_inc(new_d.sem, 1)
                    else:
                        q, half = j % 2, (j - 4) // 2
                        st = r0[:, 4 * half:4 * half + 4, q]
                        stt(st, st, c[:, MC_CDEC + q:MC_CDEC + q + 1], bank[:].rearrange("p (b d) -> p b d", b=4), ALU.mult, ALU.add).then_inc(new_d.sem, 1)

            def start():
                nc.vector.memset(S[:], 0.0).then_inc(s_zero.sem, 1)
                nc.vector.memset(R[:], 0.0).then_inc(s_zero.sem, 1)
                nc.vector.memset(S0[:], 0.0).then_inc(s_zero.sem, 1)
                dve.wait_ge(s_zero.sem, 3)
                dve.wait_ge(const_in.sem, 16 * NCONST)
                f_mix(0, 0, 0)
                f_lora(0, 0)
                f_kk1(0, 0)
                f_z(0)
                f_lwa(0)
                f_kk2(0, 0)
                f_rot(0, 0, 0)
                f_scale(0, 0)

            def body(t, u, i):
                grams(t, u, mc, False)
                f_mix(t + 1, 1 - u, i + u)
                level(t, 1)
                f_lora(t + 1, 1 - u)
                level(t, 2)
                f_kk1(t + 1, 1 - u)
                level(t, 3)
                f_z(t + 1)
                level(t, 4)
                f_lwa(t + 1)
                f_kk2(t + 1, 1 - u)
                level(t, 5)
                f_rot(t + 1, 1 - u, i + u)
                level(t, 6)
                f_scale(t + 1, 1 - u)
                tail(t, u, mc, False)

            def end():
                grams(NT, 0, mcs, True)
                level(NT, 1, LEVELS_S - 1)
                level(NT, 2, LEVELS_S - 1)
                tail(NT, 0, mcs, True)
                sampled_states(NT, 0, mcs)

            tiles(dve, start, body, end)

        @block.gpsimd
        def _(pool):
            tt = nc.gpsimd.tensor_tensor

            def f_rn(t):
                pool.wait_ge(kk_d.sem, kk_d.at(t, 3))
                tt(rn[:], ss[:], halves[:, 0:HA], ALU.pow).then_inc(rn_g.sem, 1)

            def first(t, c):
                m0 = c[:, MC_LVL:MC_LVL + P].unsqueeze(1).broadcast_to([P, 4, P])
                for g in range(2):
                    pool.wait_ge(gram_d.sem, gram_d.at(t, 4 * g + 4))
                    tt(MT[g][:], G[:, 4 * g:4 * g + 4, 0], m0, ALU.mult).then_inc(mt0_g.sem, 1)
                    pool.wait_ge(mt0_g.sem, mt0_g.at(t, 2 * g + 1))
                    tt(MT[g][:], MT[g][:], ident[:].unsqueeze(1).broadcast_to([P, 4, P]), ALU.add).then_inc(mt0_g.sem, 1)

            def level(t, j, c):
                m = c[:, MC_LVL + j * P:MC_LVL + (j + 1) * P].unsqueeze(1).broadcast_to([P, 4, P])
                for g in range(2):
                    n = 2 * (j - 1) + g + 1
                    if j > 1:
                        pool.wait_ge(x_p.sem, x_p.at(t, n - 2))
                    tt(ET[g][:], G[:, 4 * g:4 * g + 4, 0], m, ALU.mult).then_inc(et_g.sem, 1)

            def tail(t, u):
                pool.wait_ge(sil_a.sem, sil_a.at(t))
                tt(sg[:], sg[:], one[:].broadcast_to([P, WA]), ALU.add).then_inc(sil1_g.sem, 1)
                pool.wait_ge(sil1_g.sem, sil1_g.at(t))
                tt(sg[:], sg[:], curB[u][:, 1024:1536], ALU.mult).then_inc(sil_g.sem, 1)
                pool.wait_ge(yb_d.sem, yb_d.at(t, 5))
                tt(rs[:, HA:], var[:, HA:], halves[:, 0:HB], ALU.pow).then_inc(rs_g.sem, 1)
                pool.wait_ge(ya_d.sem, ya_d.at(t, 5))
                tt(rs[:, 0:HA], var[:, 0:HA], halves[:, 0:HA], ALU.pow).then_inc(rs_g.sem, 1)

            def start():
                nc.gpsimd.memset(halves[:], -0.5).then_inc(half_set.sem, 1)
                nc.gpsimd.memset(one[:], 1.0).then_inc(half_set.sem, 1)
                pool.wait_ge(half_set.sem, 2)
                pool.wait_ge(const_in.sem, 16 * NCONST)
                f_rn(0)

            def body(t, u, i):
                first(t, mc)
                level(t, 1, mc)
                level(t, 2, mc)
                level(t, 3, mc)
                f_rn(t + 1)
                level(t, 4, mc)
                level(t, 5, mc)
                level(t, 6, mc)
                tail(t, u)

            def end():
                first(NT, mcs)
                level(NT, 1, mcs)
                level(NT, 2, mcs)
                tail(NT, 0)

            tiles(pool, start, body, end)

        ex.close()



def normalize(dve, s, t, base, x, stats, mv, rs, rs_done, out, g, b):
    for half in range(2):
        dve.bn_stats(stats[:, 6 * half:6 * half + 6], x[:, 512 * half:512 * half + 512]).then_inc(s.sem, 1)
    dve.wait_ge(s.sem, s.at(t, base + 2))
    dve.memset(mv[:, 3:4], 0.0)
    dve.bn_aggr(mv[:, 0:2], stats[:]).then_inc(s.sem, 1)
    dve.wait_ge(s.sem, s.at(t, base + 3))
    dve.tensor_scalar(mv[:, 2:3], mv[:, 1:2], LN_EPS, None, ALU.add).then_inc(s.sem, 1)
    dve.wait_ge(rs_done.sem, rs_done.at(t, 1))
    dve.tensor_scalar(out, x, mv[:, 0:1], rs, ALU.subtract, ALU.mult).then_inc(s.sem, 1)
    dve.wait_ge(s.sem, s.at(t, base + 5))
    dve.tensor_tensor(out, out, g, ALU.mult).then_inc(s.sem, 1)
    dve.wait_ge(s.sem, s.at(t, base + 6))
    dve.tensor_tensor(out, out, b, ALU.add).then_inc(s.sem, 1)


def merge(nc, x_rows, shift_p, shift_s, yT_d, w_out, w_router, vec2, ident_d, hT, acc, logits):
    with ExitStack() as ctx:
        def sb(name, shape):
            return ctx.enter_context(nc.sbuf_tensor("mg_" + name, shape, F32))

        def two(name, shape):
            return [sb(f"{name}{u}", shape) for u in range(2)]

        def sig(name, per, by=1):
            return Signal(nc, ctx, "mg_" + name, per, by)

        wo = sb("wo", [P, KD, D])
        wr = sb("wr", [P, KD, NG + NE])
        gb = sb("gb", [P, 2 * D + NG + NE])
        ident = sb("ident", [P, P])
        yT, x, h, hs = two("yT", [P, KD, P]), two("x", [P, D]), two("h", [P, D]), two("hs", [P, KD, P])
        stats, mv, rs = sb("stats", [P, 12]), sb("mv", [P, 4]), sb("rs", [P, 1])
        halves = sb("halves", [P, 1])
        B = [ctx.enter_context(nc.psum_tensor(f"mg_ps{b}", [P, 512], F32)) for b in range(8)]

        half_set = sig("half_set", 1)
        shift_out = sig("shift_out", 2, 16)
        const_in = sig("const_in", 5, 16)
        yT_in = [sig(f"yT_in{u}", 1, 16) for u in range(2)]
        x_in = [sig(f"x_in{u}", 1, 16) for u in range(2)]
        mix_p = sig("mix_p", 2)
        h_d = sig("h_d", 9)
        rs_g = sig("rs_g", 1)
        turn_p = sig("turn_p", 2)
        acc_a = sig("acc_a", 1)
        turn_a = sig("turn_a", 2)
        router_p = sig("router_p", 1)
        logit_d = sig("logit_d", 1)
        hT_out = [sig(f"hT_out{u}", 1, 16) for u in range(2)]

        with nc.Block() as block:

            def loop(eng, f, last=None):
                with eng.Fori(0, NT // 2) as i:
                    f(2 * i, 0, i)
                    f(2 * i + 1, 1, i)
                f(NT, 0, NT // 2)

            @block.sync
            def _(sp):
                for dst, src in ((gb, vec2.broadcast_to([P, 2 * D + NG + NE])), (ident, ident_d), (wr, w_router)):
                    sp.dma_start(dst[:], src).then_inc(const_in.sem, 16)
                for half in range(2):
                    sp.dma_start(wo[:, :, 512 * half:512 * half + 512], w_out[:, :, 512 * half:512 * half + 512]).then_inc(const_in.sem, 16)

                def tile(t, u, i):
                    sp.wait_ge(turn_a.sem, turn_a.at(t))
                    sp.dma_start(hT[:, t], hs[u][:]).then_inc(hT_out[u].sem, 16)
                loop(sp, tile)
                sp.dma_start(shift_p, x_rows[SEQ:SEQ + 1]).then_inc(shift_out.sem, 16)
                last = x_rows[SAMPLE0:SAMPLE0 + DB * (DS + 1)].rearrange("(b t) c -> b t c", b=DB)[:, DS]
                sp.dma_start(shift_s, last).then_inc(shift_out.sem, 16)
                for u in range(2):
                    sp.wait_ge(hT_out[u].sem, 16 * (NT // 2 + (u == 0)))
                sp.wait_ge(shift_out.sem, 32)

            @block.gpsimd
            def _(pool):
                nc.gpsimd.memset(halves[:], -0.5).then_inc(half_set.sem, 1)
                pool.wait_ge(half_set.sem, 1)

                def load(t, u):
                    if isinstance(t, int) and t == NT:
                        pool.dma_start(x[u][0:TS], x_rows[SAMPLE0:SAMPLE0 + DB * (DS + 1)].rearrange("(b t) c -> b t c", b=DB)[:, 1:]).then_inc(x_in[u].sem, 16)
                    else:
                        pool.dma_start(x[u][:], x_rows[1:1 + SEQ].rearrange("(n p) c -> n p c", p=P)[t]).then_inc(x_in[u].sem, 16)
                    pool.dma_start(yT[u][:], yT_d[t]).then_inc(yT_in[u].sem, 16)

                def power(t):
                    pool.wait_ge(h_d.sem, h_d.at(t, 6))
                    nc.gpsimd.tensor_tensor(rs[:], mv[:, 2:3], halves[:], ALU.pow).then_inc(rs_g.sem, 1)

                load(0, 0)
                load(1, 1)
                with pool.Fori(0, NT // 2 - 1) as i:
                    for u in range(2):
                        power(2 * i + u)
                        load(2 * i + u + 2, u)
                power(NT - 2)
                load(NT, 0)
                power(NT - 1)
                power(NT)

            @block.tensor
            def _(pe):
                pe.wait_ge(const_in.sem, const_in.at(1, 0))

                def mix(t, u, i):
                    pe.wait_ge(yT_in[u].sem, (i + 1) * 16)
                    for half in range(2):
                        for k in range(KD):
                            m = nc.tensor.matmul(B[2 * u + half][:], yT[u][:, k], wo[:, k, 512 * half:512 * half + 512], start=(k == 0), stop=(k == KD - 1))
                        m.then_inc(mix_p.sem, 1)

                def turn(t, u):
                    pe.wait_ge(h_d.sem, h_d.at(t))
                    for half in range(2):
                        pe.wait_ge(turn_a.sem, turn_a.at(t, 0))
                        for q in range(4):
                            k = 4 * half + q
                            m = nc.tensor.transpose(B[4 + half][:, q * P:(q + 1) * P], h[u][:, k * P:(k + 1) * P], ident[:])
                        m.then_inc(turn_p.sem, 1)

                def router(t, u):
                    pe.wait_ge(turn_a.sem, turn_a.at(t))
                    pe.wait_ge(logit_d.sem, logit_d.at(t, 0))
                    for k in range(KD):
                        m = nc.tensor.matmul(B[6][:, 0:NG + NE], hs[u][:, k], wr[:, k], start=(k == 0), stop=(k == KD - 1))
                    m.then_inc(router_p.sem, 1)

                mix(0, 0, 0)
                with pe.Fori(0, NT // 2) as i:
                    mix(2 * i + 1, 1, i)
                    turn(2 * i, 0)
                    router(2 * i, 0)
                    mix(2 * i + 2, 0, i + 1)
                    turn(2 * i + 1, 1)
                    router(2 * i + 1, 1)
                turn(NT, 0)
                router(NT, 0)

            @block.scalar
            def _(act):
                def tile(t, u, i):
                    act.wait_ge(h_d.sem, h_d.at(t))
                    nc.scalar.mul(acc[:, t], h[u][:], ALPHA).then_inc(acc_a.sem, 1)
                    act.wait_ge(hT_out[u].sem, i * 16)
                    act.wait_ge(router_p.sem, router_p.at(t, 0))
                    for half in range(2):
                        act.wait_ge(turn_p.sem, turn_p.at(t, half + 1))
                        nc.scalar.copy(hs[u][:, 4 * half:4 * half + 4], B[4 + half][:].rearrange("p (k t) -> p k t", t=P)).then_inc(turn_a.sem, 1)
                loop(act, tile)

            @block.vector
            def _(dve):
                dve.wait_ge(const_in.sem, const_in.at(1, 0))

                def tile(t, u, i):
                    dve.wait_ge(x_in[u].sem, (i + 1) * 16)
                    dve.wait_ge(turn_a.sem, turn_a.at(t, 0))
                    for half in range(2):
                        c = slice(512 * half, 512 * half + 512)
                        dve.wait_ge(mix_p.sem, mix_p.at(t, half + 1))
                        nc.vector.scalar_tensor_tensor(h[u][:, c], x[u][:, c], ALPHA, B[2 * u + half][:], ALU.mult, ALU.add).then_inc(h_d.sem, 1)
                    dve.wait_ge(h_d.sem, h_d.at(t, 2))
                    normalize(nc.vector, h_d, t, 2, h[u][:], stats, mv, rs[:], rs_g, h[u][:], gb[:, 0:D], gb[:, D:2 * D])
                    dve.wait_ge(router_p.sem, router_p.at(t))
                    nc.vector.tensor_tensor(logits[:, t], B[6][:, 0:NG + NE], gb[:, 2 * D:], ALU.add).then_inc(logit_d.sem, 1)
                loop(dve, tile)



def route(nc, logits, gates, prio_d):
    n = TILES
    with ExitStack() as ctx:
        def sb(name, shape):
            return ctx.enter_context(nc.sbuf_tensor("rt_" + name, shape, F32))

        prio = sb("prio", [P, 4])
        cmax, z, gp, pm, v1, v2, e, w1 = (sb(x, [P, n]) for x in ("cmax", "z", "gp", "pm", "v1", "v2", "e", "w1"))
        c, ex, pr, oh, f4, oh1, oh2, d = (sb(x, [P, n, 4]) for x in ("c", "ex", "pr", "oh", "f4", "oh1", "oh2", "d"))
        prod = sb("prod", [P, n, 4, 4])
        prio_in = Signal(nc, ctx, "rt_prio_in", 1, 16)
        step = Signal(nc, ctx, "rt_step", 1)
        exp_a = Signal(nc, ctx, "rt_exp_a", 1)

        def over(x):
            return x.unsqueeze(2).broadcast_to([P, n, 4])

        with nc.Block() as block:

            @block.sync
            def _(sp):
                sp.dma_start(prio[:], prio_d.broadcast_to([P, 4])).then_inc(prio_in.sem, 16)

            @block.scalar
            def _(act):
                act.wait_ge(step.sem, C_READY)
                nc.scalar.activation(ex[:], c[:], ACT.Exp).then_inc(exp_a.sem, 1)
                act.wait_ge(step.sem, V2_READY)
                nc.scalar.activation(e[:], v2[:], ACT.Exp).then_inc(exp_a.sem, 1)

            @block.vector
            def _(dve):
                tt, ts, red = nc.vector.tensor_tensor, nc.vector.tensor_scalar, nc.vector.tensor_reduce
                done = [0]

                def then(ins):
                    done[0] += 1
                    ins.then_inc(step.sem, 1)
                    dve.wait_ge(step.sem, done[0])

                def first_max(out, x, floor):
                    then(tt(pr[:], x, floor, ALU.is_ge))
                    then(tt(pr[:], pr[:], prio[:].unsqueeze(1).broadcast_to([P, n, 4]), ALU.mult))
                    then(red(pm[:], pr[:], AX, ALU.max))
                    then(tt(out, pr[:], over(pm[:]), ALU.is_equal))

                dve.wait_ge(prio_in.sem, 16)
                coarse = logits[:, :, 0:NG]
                fine = logits[:, :, NG:].rearrange("p n (g j) -> p n g j", g=NG)
                then(red(cmax[:], coarse, AX, ALU.max))
                then(tt(c[:], coarse, over(cmax[:]), ALU.subtract))
                assert done[0] == C_READY
                first_max(oh[:], coarse, over(cmax[:]))
                dve.wait_ge(exp_a.sem, 1)
                then(red(z[:], ex[:], AX, ALU.add))
                then(nc.vector.reciprocal(gp[:], z[:]))
                then(tt(prod[:], fine, oh[:].unsqueeze(3).broadcast_to([P, n, 4, 4]), ALU.mult))
                then(red(f4[:], prod[:].rearrange("p n g j -> p n j g"), AX, ALU.add))
                then(red(v1[:], f4[:], AX, ALU.max))
                first_max(oh1[:], f4[:], over(v1[:]))
                then(tt(d[:], f4[:], over(v1[:]), ALU.subtract))
                then(nc.vector.scalar_tensor_tensor(d[:], oh1[:], -3e38, d[:], ALU.mult, ALU.add))
                then(red(v2[:], d[:], AX, ALU.max))
                assert done[0] == V2_READY
                first_max(oh2[:], d[:], over(v2[:]))
                dve.wait_ge(exp_a.sem, 2)
                then(ts(w1[:], e[:], 1.0, None, ALU.add))
                then(nc.vector.reciprocal(w1[:], w1[:]))
                then(tt(w1[:], w1[:], gp[:], ALU.mult))
                then(tt(e[:], e[:], w1[:], ALU.mult))
                then(tt(oh1[:], oh1[:], over(w1[:]), ALU.mult))
                then(tt(oh2[:], oh2[:], over(e[:]), ALU.mult))
                then(tt(oh1[:], oh1[:], oh2[:], ALU.add))
                then(tt(gates[:].rearrange("p n (g j) -> p n g j", g=NG), oh[:].unsqueeze(3).broadcast_to([P, n, 4, 4]),
                        oh1[:].unsqueeze(2).broadcast_to([P, n, 4, 4]), ALU.mult))


def experts(nc, w1_d, w3_d, w2_d, hT, acc, gates):
    groups = [(0, 4, 512), (4, 4, 512), (8, 1, TS)]
    NF = FE // P
    with ExitStack() as ctx:
        def sb(name, shape):
            return ctx.enter_context(nc.sbuf_tensor("ex_" + name, shape, F32))

        def sig(name, per, by=1):
            return Signal(nc, ctx, "ex_" + name, per, by)

        w13 = [sb(f"w13{u}", [P, 2, KD, FE]) for u in range(2)]
        w2 = [sb(f"w2{u}", [P, NF, D]) for u in range(2)]
        hid = [sb(f"hid{u}", [P, NF, 512]) for u in range(2)]
        th = [sb(f"th{u}", [P, 512]) for u in range(2)]
        gcur = sb("gcur", [P, TILES])
        B = [ctx.enter_context(nc.psum_tensor(f"ex_ps{b}", [P, 512], F32)) for b in range(8)]
        NU = len(groups) * NF
        NY = TILES * 2
        w13_in = [sig(f"w13_in{u}", 1, 32) for u in range(2)]
        w2_in = [sig(f"w2_in{u}", 1, 16) for u in range(2)]
        up_p = sig("up_p", NU)
        th_a = sig("th_a", NU)
        hid_d = sig("hid_d", 2 * NU)
        gate_d = sig("gate_d", 1)
        y_p = sig("y_p", NY)
        y_d = sig("y_d", NY)

        with nc.Block() as block:

            @block.sync
            def _(sp):
                def load(e, u):
                    sp.dma_start(w13[u][:, 0], w1_d[e]).then_inc(w13_in[u].sem, 16)
                    sp.dma_start(w13[u][:, 1], w3_d[e]).then_inc(w13_in[u].sem, 16)
                    sp.dma_start(w2[u][:], w2_d[e]).then_inc(w2_in[u].sem, 16)
                load(0, 0)
                load(1, 1)
                with sp.Fori(0, NE // 2 - 1) as i:
                    for u in range(2):
                        sp.wait_ge(y_p.sem, y_p.at(2 * i + u))
                        load(2 * i + u + 2, u)

            @block.tensor
            def _(pe):
                with pe.Fori(0, NE // 2) as i:
                    for u in range(2):
                        e = 2 * i + u
                        pe.wait_ge(w13_in[u].sem, (i + 1) * 32)

                        def up(g):
                            t0, nt, n = groups[g]
                            for f in range(NF):
                                j = g * NF + f
                                if j >= 2:
                                    pe.wait_ge(hid_d.sem, hid_d.at(e, 2 * (j - 1)))
                                else:
                                    pe.wait_ge(hid_d.sem, hid_d.at(e, 0))
                                for w in range(2):
                                    for k in range(KD):
                                        rhs = hT[:, t0:t0 + nt, k] if nt > 1 else hT[:, t0, k, 0:n]
                                        out = B[2 * (j % 2) + w][:, 0:n]
                                        if nt > 1:
                                            out = out.rearrange("p (a t) -> p a t", t=P)
                                        m = nc.tensor.matmul(out, w13[u][:, w, k, f * P:(f + 1) * P], rhs, start=(k == 0), stop=(k == KD - 1))
                                m.then_inc(up_p.sem, 1)

                        def down(g):
                            t0, nt, n = groups[g]
                            if g == 0:
                                pe.wait_ge(w2_in[u].sem, (i + 1) * 16)
                            pe.wait_ge(hid_d.sem, hid_d.at(e, 2 * NF * (g + 1)))
                            for t in range(nt):
                                m_rows = P if nt > 1 else n
                                for half in range(2):
                                    j = 2 * (t0 + t) + half
                                    pe.wait_ge(y_d.sem, y_d.at(e, j - 3) if j >= 4 else y_d.at(e, 0))
                                    for f in range(NF):
                                        m = nc.tensor.matmul(B[4 + j % 4][0:m_rows, :], hid[g % 2][:, f, t * P:t * P + m_rows], w2[u][:, f, 512 * half:512 * half + 512], start=(f == 0), stop=(f == NF - 1))
                                    m.then_inc(y_p.sem, 1)

                        up(0)
                        up(1)
                        down(0)
                        up(2)
                        down(1)
                        down(2)

            @block.scalar
            def _(act):
                with act.Fori(0, NE // 2) as i:
                    for u in range(2):
                        e = 2 * i + u
                        for g, (t0, nt, n) in enumerate(groups):
                            for f in range(NF):
                                j = g * NF + f
                                act.wait_ge(up_p.sem, up_p.at(e, j + 1))
                                act.wait_ge(hid_d.sem, hid_d.at(e, 2 * (j - 1)) if j >= 2 else hid_d.at(e, 0))
                                nc.scalar.activation(th[j % 2][:, 0:n], B[2 * (j % 2)][:, 0:n], ACT.Tanh, scale=0.5).then_inc(th_a.sem, 1)

            @block.vector
            def _(dve):
                stt = nc.vector.scalar_tensor_tensor
                with dve.Fori(0, NE // 2) as i:
                    for u in range(2):
                        e = 2 * i + u
                        dve.wait_ge(y_d.sem, y_d.at(e, 0))
                        nc.vector.tensor_scalar(gcur[:].unsqueeze(2), gates[:, :, e:e + 1] if isinstance(e, int) else gates[:, :, bass.ds(e, 1)], 0.5, None, ALU.mult).then_inc(gate_d.sem, 1)

                        def hidden(g):
                            t0, nt, n = groups[g]
                            for f in range(NF):
                                j = g * NF + f
                                dve.wait_ge(th_a.sem, th_a.at(e, j + 1))
                                t_, b = th[j % 2][:, 0:n], 2 * (j % 2)
                                if g == 2:
                                    dve.wait_ge(y_p.sem, y_p.at(e, 8))
                                else:
                                    dve.wait_ge(y_p.sem, y_p.at(e, 0))
                                stt(t_, t_, 1.0, B[b][:, 0:n], ALU.add, ALU.mult).then_inc(hid_d.sem, 1)
                                dve.wait_ge(hid_d.sem, hid_d.at(e, 2 * j + 1))
                                nc.vector.tensor_tensor(hid[g % 2][:, f, 0:n], t_, B[b + 1][:, 0:n], ALU.mult).then_inc(hid_d.sem, 1)

                        def add(g):
                            t0, nt, n = groups[g]
                            rows = P if nt > 1 else n
                            for t in range(t0, t0 + nt):
                                for half in range(2):
                                    j = 2 * t + half
                                    dve.wait_ge(y_p.sem, y_p.at(e, j + 1))
                                    if j == 0:
                                        dve.wait_ge(gate_d.sem, gate_d.at(e))
                                    dst = acc[0:rows, t, 512 * half:512 * half + 512]
                                    stt(dst, B[4 + j % 4][0:rows], gcur[0:rows, t:t + 1], dst, ALU.mult, ALU.add).then_inc(y_d.sem, 1)

                        hidden(0)
                        hidden(1)
                        add(0)
                        hidden(2)
                        add(1)
                        add(2)


def finish(nc, acc, pT_d, w_ple, w_pgate, vec3, ident_d, out_d):
    with ExitStack() as ctx:
        def sb(name, shape):
            return ctx.enter_context(nc.sbuf_tensor("fi_" + name, shape, F32))

        def two(name, shape):
            return [sb(f"{name}{u}", shape) for u in range(2)]

        def sig(name, per, by=1):
            return Signal(nc, ctx, "fi_" + name, per, by)

        KP = D_PLE // P
        wp, wg = sb("wp", [P, KP, D]), sb("wg", [P, KD, D])
        gb = sb("gb", [P, 3 * D])
        ident = sb("ident", [P, P])
        pT, h, hs, q = two("pT", [P, KP, P]), two("h", [P, D]), two("hs", [P, KD, P]), two("q", [P, D])
        junk = sb("junk", [P, D])
        stats, mv, rs, rr = sb("stats", [P, 12]), sb("mv", [P, 4]), sb("rs", [P, 1]), sb("rr", [P, 1])
        ssq = two("ssq", [P, 1])
        var2 = sb("var2", [P, 1])
        halves = sb("halves", [P, 1])
        B = [ctx.enter_context(nc.psum_tensor(f"fi_ps{b}", [P, 512], F32)) for b in range(8)]
        half_set = sig("half_set", 1)
        const_in = sig("const_in", 5, 16)
        pT_in = [sig(f"pT_in{u}", 1, 16) for u in range(2)]
        h_d = sig("h_d", 7)
        rs_g = sig("rs_g", 1)
        turn_p = sig("turn_p", 2)
        turn_a = sig("turn_a", 2)
        gate_p = sig("gate_p", 2)
        ple_p = sig("ple_p", 2)
        tanh_a = sig("tanh_a", 2)
        sq_a = sig("sq_a", 1)
        q_d = sig("q_d", 6)
        rr_g = sig("rr_g", 1)
        out_s = [sig(f"out_s{u}", 1, 16) for u in range(2)]

        with nc.Block() as block:

            @block.sync
            def _(sp):
                for dst, src in ((gb, vec3.broadcast_to([P, 3 * D])), (ident, ident_d), (wp, w_ple)):
                    sp.dma_start(dst[:], src).then_inc(const_in.sem, 16)
                for half in range(2):
                    sp.dma_start(wg[:, :, 512 * half:512 * half + 512], w_pgate[:, :, 512 * half:512 * half + 512]).then_inc(const_in.sem, 16)

                def store(t, u):
                    sp.wait_ge(q_d.sem, q_d.at(t))
                    sp.dma_start(out_d[t], q[u][:]).then_inc(out_s[u].sem, 16)
                with sp.Fori(0, NT // 2) as i:
                    store(2 * i, 0)
                    store(2 * i + 1, 1)
                store(NT, 0)
                sp.wait_ge(out_s[0].sem, 16 * (NT // 2 + 1))
                sp.wait_ge(out_s[1].sem, 16 * (NT // 2))

            @block.gpsimd
            def _(pool):
                nc.gpsimd.memset(halves[:], -0.5).then_inc(half_set.sem, 1)
                pool.wait_ge(half_set.sem, 1)

                def load(t, u):
                    pool.dma_start(pT[u][:], pT_d[t]).then_inc(pT_in[u].sem, 16)

                def power(t):
                    pool.wait_ge(h_d.sem, h_d.at(t, 4))
                    nc.gpsimd.tensor_tensor(rs[:], mv[:, 2:3], halves[:], ALU.pow).then_inc(rs_g.sem, 1)

                def power2(t):
                    pool.wait_ge(q_d.sem, q_d.at(t, 3))
                    nc.gpsimd.tensor_tensor(rr[:], var2[:], halves[:], ALU.pow).then_inc(rr_g.sem, 1)

                load(0, 0)
                load(1, 1)
                power(0)
                with pool.Fori(0, NT // 2 - 1) as i:
                    for u in range(2):
                        power(2 * i + u + 1)
                        power2(2 * i + u)
                        load(2 * i + u + 2, u)
                power(NT - 1)
                power2(NT - 2)
                load(NT, 0)
                power(NT)
                power2(NT - 1)
                power2(NT)

            @block.tensor
            def _(pe):
                pe.wait_ge(const_in.sem, const_in.at(1, 0))

                def tile(t, u, i):
                    pe.wait_ge(h_d.sem, h_d.at(t))
                    pe.wait_ge(turn_a.sem, turn_a.at(t, 0))
                    for half in range(2):
                        for c in range(4):
                            k = 4 * half + c
                            m = nc.tensor.transpose(B[half][:, c * P:(c + 1) * P], h[u][:, k * P:(k + 1) * P], ident[:])
                        m.then_inc(turn_p.sem, 1)
                    pe.wait_ge(pT_in[u].sem, (i + 1) * 16)
                    for half in range(2):
                        pe.wait_ge(q_d.sem, q_d.at(t, 0))
                        for k in range(KP):
                            m = nc.tensor.matmul(B[4 + half][:], pT[u][:, k], wp[:, k, 512 * half:512 * half + 512], start=(k == 0), stop=(k == KP - 1))
                        m.then_inc(ple_p.sem, 1)
                    pe.wait_ge(turn_a.sem, turn_a.at(t))
                    for half in range(2):
                        for k in range(KD):
                            m = nc.tensor.matmul(B[2 + half][:], hs[u][:, k], wg[:, k, 512 * half:512 * half + 512], start=(k == 0), stop=(k == KD - 1))
                        m.then_inc(gate_p.sem, 1)
                with pe.Fori(0, NT // 2) as i:
                    tile(2 * i, 0, i)
                    tile(2 * i + 1, 1, i)
                tile(NT, 0, NT // 2)

            @block.scalar
            def _(act):
                def tile(t, u, i):
                    for half in range(2):
                        act.wait_ge(turn_p.sem, turn_p.at(t, half + 1))
                        nc.scalar.copy(hs[u][:, 4 * half:4 * half + 4], B[half][:].rearrange("p (k t) -> p k t", t=P)).then_inc(turn_a.sem, 1)
                    act.wait_ge(out_s[u].sem, i * 16)
                    for half in range(2):
                        act.wait_ge(gate_p.sem, gate_p.at(t, half + 1))
                        nc.scalar.activation(q[u][:, 512 * half:512 * half + 512], B[2 + half][:], ACT.Tanh, scale=0.5).then_inc(tanh_a.sem, 1)
                    act.wait_ge(q_d.sem, q_d.at(t, 2))
                    nc.scalar.activation(junk[:], q[u][:], ACT.Square, accum_out=ssq[u][:]).then_inc(sq_a.sem, 1)
                with act.Fori(0, NT // 2) as i:
                    tile(2 * i, 0, i)
                    tile(2 * i + 1, 1, i)
                tile(NT, 0, NT // 2)

            @block.vector
            def _(dve):
                tt, stt = nc.vector.tensor_tensor, nc.vector.scalar_tensor_tensor
                dve.wait_ge(const_in.sem, const_in.at(1, 0))

                def norm(t, u):
                    if not isinstance(t, int):
                        dve.wait_ge(q_d.sem, q_d.at(t - 1, 0))
                    normalize(nc.vector, h_d, t, 0, acc[:, t], stats, mv, rs[:], rs_g, h[u][:], gb[:, 0:D], gb[:, D:2 * D])

                def embed(t, u):
                    for half in range(2):
                        c = slice(512 * half, 512 * half + 512)
                        dve.wait_ge(tanh_a.sem, tanh_a.at(t, half + 1))
                        stt(q[u][:, c], q[u][:, c], 1.0, B[4 + half][:], ALU.add, ALU.mult).then_inc(q_d.sem, 1)
                    dve.wait_ge(sq_a.sem, sq_a.at(t))
                    nc.vector.tensor_scalar(var2[:], ssq[u][:], 0.25 / D, LN_EPS, ALU.mult, ALU.add).then_inc(q_d.sem, 1)
                    dve.wait_ge(rr_g.sem, rr_g.at(t))
                    nc.vector.tensor_scalar(q[u][:], q[u][:], rr[:], 0.5, ALU.mult, ALU.mult).then_inc(q_d.sem, 1)
                    dve.wait_ge(q_d.sem, q_d.at(t, 4))
                    tt(q[u][:], q[u][:], gb[:, 2 * D:], ALU.mult).then_inc(q_d.sem, 1)
                    dve.wait_ge(q_d.sem, q_d.at(t, 5))
                    tt(q[u][:], q[u][:], h[u][:], ALU.add).then_inc(q_d.sem, 1)

                norm(0, 0)
                with dve.Fori(0, NT // 2) as i:
                    norm(2 * i + 1, 1)
                    embed(2 * i, 0)
                    norm(2 * i + 2, 0)
                    embed(2 * i + 1, 1)
                embed(NT, 0)


INPUTS = ["x_all", "x_rows", "w_in", "vecs", "w_lora", "w_gate", "fconst", "mconst", "ident", "s0T", "r0", "w_out", "w_router",
          "vec2", "prio", "w1", "w3", "w2", "pT", "w_ple", "w_pgate", "vec3"]
OUTPUTS = {"out": (TILES, P, D), "shift_p": (1, D), "shift_s": (DB, D), "wkv_p": (P, 4, NA), "ret_p": (P, 2, NV), "wkv_s": (P, DB, 4, NA), "ret_s": (P, DB, 2, NV)}


def program(nc, a, o):
    proj = nc.dram_tensor("proj", (ROWS, IN_W), F32, kind="Internal").ap()
    yT_d = nc.dram_tensor("yT_d", (TILES, P, KD, P), F32, kind="Internal").ap()
    project(nc, a["x_all"], a["w_in"], proj)
    mixer(nc, proj, a["vecs"], a["w_lora"], a["w_gate"], a["fconst"], a["mconst"], a["ident"], a["s0T"], a["r0"],
          yT_d, o["wkv_p"], o["ret_p"], o["wkv_s"], o["ret_s"])
    with ExitStack() as ctx:
        hT = ctx.enter_context(nc.sbuf_tensor("hT", [P, TILES, KD, P], F32))
        acc = ctx.enter_context(nc.sbuf_tensor("acc", [P, TILES, D], F32))
        logits = ctx.enter_context(nc.sbuf_tensor("logits", [P, TILES, NG + NE], F32))
        gates = ctx.enter_context(nc.sbuf_tensor("gates", [P, TILES, NE], F32))
        merge(nc, a["x_rows"], o["shift_p"], o["shift_s"], yT_d, a["w_out"], a["w_router"], a["vec2"], a["ident"], hT, acc, logits)
        route(nc, logits, gates, a["prio"])
        experts(nc, a["w1"], a["w3"], a["w2"], hT, acc, gates)
        finish(nc, acc, a["pT"], a["w_ple"], a["w_pgate"], a["vec3"], a["ident"], o["out"])


def layout(inputs):
    z = {n: np.asarray(a) for n, a in inputs.items()}
    out = {}
    rows = np.zeros((ROWS, D), np.float32)
    rows[1:1 + SEQ] = z["x_prompt"][0]
    tail = rows[SAMPLE0:SAMPLE0 + DB * (DS + 1)].reshape(DB, DS + 1, D)
    tail[:, 0] = z["state_shift"][0]
    tail[:, 1:] = z["x_sample"]
    out["x_rows"] = rows
    out["x_all"] = np.ascontiguousarray(rows.reshape(TILES, P, KD, P).transpose(3, 0, 2, 1))
    out["w_in"] = np.ascontiguousarray(z["w_in"][0].reshape(KD, P, NSLICE, SLICE).transpose(2, 1, 0, 3))
    out["vecs"] = np.concatenate([z[n][0].reshape(-1) for n in VEC])[None]
    out["w_lora"] = np.concatenate([z["w_decay_up"][0], z["w_aaa_up"][0]])
    out["w_gate"] = z["w_gate_up"][0]
    out["s0T"] = z["state_wkv"][0].reshape(DB, 4, 2, NA, NA).transpose(2, 4, 0, 1, 3).reshape(P, DB, 4, NA)
    out["r0"] = z["state_ret"][0].reshape(DB, 2, 2, NK, NV).transpose(2, 3, 0, 1, 4).reshape(P, DB, 2, NV)
    out["w_out"] = z["w_out"][0].reshape(KD, P, D).transpose(1, 0, 2)
    out["w_router"] = np.concatenate([z["router_coarse_w"][0], z["router_fine_w"][0]], 1).reshape(KD, P, NG + NE).transpose(1, 0, 2)
    out["vec2"] = np.concatenate([z[n][0] for n in ("ln1_g", "ln1_b", "router_coarse_b", "router_fine_b")])[None]
    out["prio"] = np.arange(4, 0, -1, dtype=np.float32)[None]
    for n in ("w1", "w3"):
        out[n] = z["expert_" + n][0].reshape(NE, KD, P, FE).transpose(0, 2, 1, 3)
    out["w2"] = z["expert_w2"][0].reshape(NE, FE // P, P, D).transpose(0, 2, 1, 3)
    p = np.zeros((ROWS, D_PLE), np.float32)
    p[:SEQ] = z["p_prompt"][0, 0]
    p[SEQ:SEQ + TS] = z["p_sample"][0].reshape(TS, D_PLE)
    out["pT"] = p.reshape(TILES, P, D_PLE // P, P).transpose(0, 3, 2, 1)
    out["w_ple"] = z["w_ple"][0].reshape(D_PLE // P, P, D).transpose(1, 0, 2)
    out["w_pgate"] = z["w_ple_gate"][0].reshape(KD, P, D).transpose(1, 0, 2)
    out["vec3"] = np.concatenate([z[n][0] for n in ("ln2_g", "ln2_b", "ple_norm_g")])[None]
    out["fconst"], out["mconst"] = shape_constants()
    out["ident"] = np.eye(P, dtype=np.float32)
    return out


def kernel(**inputs):
    import concourse.bacc as bacc
    from concourse.bass_utils import run_bass_kernel_spmd as run

    laid = layout(inputs)
    nc = bacc.Bacc("TRN2", target_bir_lowering=False, num_devices=1)
    arrays, a, o = {}, {}, {}
    for name in INPUTS:
        arrays["in_" + name] = np.ascontiguousarray(laid[name])
        a[name] = nc.dram_tensor("in_" + name, arrays["in_" + name].shape, F32, kind="ExternalInput").ap()
    for name, shape in OUTPUTS.items():
        o[name] = nc.dram_tensor("out_" + name, shape, F32, kind="ExternalOutput").ap()
    program(nc, a, o)
    got = run(nc, [arrays], core_ids=[0]).results[0]
    y = np.asarray(got["out_out"]).reshape(ROWS, D)
    wkv_p = np.asarray(got["out_wkv_p"]).reshape(2, NA, 4, NA).transpose(2, 0, 3, 1).reshape(1, 1, HA, NA, NA)
    ret_p = np.asarray(got["out_ret_p"]).reshape(2, NK, 2, NV).transpose(2, 0, 1, 3).reshape(1, 1, HB, NK, NV)
    wkv_s = np.asarray(got["out_wkv_s"]).reshape(2, NA, DB, 4, NA).transpose(2, 3, 0, 4, 1).reshape(1, DB, HA, NA, NA)
    ret_s = np.asarray(got["out_ret_s"]).reshape(2, NK, DB, 2, NV).transpose(2, 3, 0, 1, 4).reshape(1, DB, HB, NK, NV)
    shift_p = np.asarray(got["out_shift_p"]).reshape(1, 1, D)
    shift_s = np.asarray(got["out_shift_s"]).reshape(1, DB, D)
    return (y[:SEQ].reshape(1, SEQ, D), y[SEQ:SEQ + TS].reshape(DB, DS, D), wkv_p, shift_p, ret_p, wkv_s, shift_s, ret_s)
```

```python
from contextlib import ExitStack

import numpy as np

import concourse.bass as bass
from concourse import mybir

F32 = mybir.dt.float32
U32 = mybir.dt.uint32
I32 = mybir.dt.int32
ALU = mybir.AluOpType
ACT = mybir.ActivationFunctionType
AX = mybir.AxisListType.X

P = 128
D = 1024
KD = D // P
SEQ = 1024
DB, DS = 8, 8
PAST = 8192
D_PLE = 256
HA, NA = 8, 64
WA = HA * NA
HB, NK, NV = 4, 64, 128
SHIFT_W = 3 * WA + 64 + 64 + 128
IN_W = SHIFT_W + 2 * HB * NK + 2 * HB * NV
NG, EPG = 4, 4
NE = NG * EPG
FE = 256
ALPHA = 2 ** 0.25
LN_EPS = 1e-5
GN_EPS_A = 64e-5
GN_EPS_B = 1e-5

NT = SEQ // P
TILES = NT + 1
TS = DB * DS
ROWS = TILES * P
SAMPLE0 = 1 + SEQ
LEVELS = 7
LEVELS_S = 3
SLICE = 416
NSLICE = IN_W // SLICE
W_CONST = -float(np.exp(-0.5))
FC_TI, FC_TE, FC_SEL, FC_COS, FC_SIN, FC_CROSS, FC_KDEC, FC_N = 0, 128, 256, 264, 296, 328, 332, 336
MC_GRAM, MC_D, MC_M0, MC_LVL, MC_CDEC, MC_BLK, MC_N = 0, 512, 1024, 1152, 1152 + 7 * 128, 1152 + 7 * 128 + 2, 1152 + 7 * 128 + 10
VEC = ["mu_shift", "decay_base", "aaa_base", "k_k", "k_a", "r_k", "lnx_g", "lnx_b", "ret_gn_g", "ret_gn_b"]
VEC_OFF = dict(zip(VEC, np.cumsum([0, SHIFT_W] + [WA] * 8).tolist()))
VEC_N = SHIFT_W + WA * 9
SLOTS = (2 * (SEQ + TS) + NE * (P - 1)) // P * P
RC_PRIO, RC_THR, RC_LT, RC_TILE, RC_VALID, RC_TRI = 0, 4, 16, 16 + NE * NE, 48 + NE * NE, 60 + NE * NE
RC_N = RC_TRI + P
C_READY, V2_READY, O_READY = 2, 16, 25
NCONST = 6


def shape_constants():
    lg = np.log1p(-np.exp2(-5.0 - np.arange(HB)))
    half = NK // 2
    inv = (10000.0 ** (-np.arange(half) / half)).astype(np.float32)
    fc = np.zeros((TILES, P, FC_N), np.float32)
    s, t = np.arange(P)[:, None], np.arange(P)[None, :]
    for n in range(TILES):
        if n < NT:
            pos = np.arange(P) + n * P
            idx, chunk = np.arange(P), P
            mid = (s < P // 2) * np.ones((1, P))
            fc[n, :, FC_TI:FC_TI + P] = (s <= t) - mid
            fc[n, :, FC_TE:FC_TE + P] = (s < t) - mid
            fc[n, :, FC_SEL] = np.arange(P) < P // 2
            fc[n, :, FC_SEL + 1] = np.arange(P) >= P // 2
        else:
            pos = PAST + np.arange(P) % DS
            idx, chunk = np.arange(P) % DS, DS
            same = (s // DS == t // DS) & (s < TS) & (t < TS)
            fc[n, :, FC_TI:FC_TI + P] = same & (s <= t)
            fc[n, :, FC_TE:FC_TE + P] = same & (s < t)
            fc[n, :, FC_SEL:FC_SEL + DB] = (np.arange(P)[:, None] // DS == np.arange(DB))
        ang = pos.astype(np.float32)[:, None] * inv[None, :]
        fc[n, :, FC_COS:FC_COS + half] = np.cos(ang)
        fc[n, :, FC_SIN:FC_SIN + half] = np.sin(ang)
        fc[n, :, FC_CROSS:FC_CROSS + HB] = np.exp(lg[None] * (idx[:, None] + 1.0))
        fc[n, :, FC_KDEC:FC_KDEC + HB] = np.exp(lg[None] * (chunk - 1.0 - idx[:, None])) * NK ** -0.5
    mc = np.zeros((2, P, MC_N), np.float32)
    for kind in range(2):
        ok = np.ones((P, P), bool) if kind == 0 else (s // DS == t // DS) & (s < TS) & (t < TS)
        for q in range(4):
            mc[kind, :, MC_GRAM + q * P:MC_GRAM + (q + 1) * P] = ok & ((s < t) if q % 2 == 0 else (s <= t))
        for h in range(HB):
            dec = np.where(s <= t, np.exp(lg[h] * np.maximum(t - s, 0)), 0.0) * NK ** -0.5
            at = MC_D + (h % 2 * 2 + h // 2) * P
            mc[kind, :, at:at + P] = dec * ok
        for j in range(LEVELS):
            b = 1 << j
            up = ok & (s // (2 * b) == t // (2 * b)) & (s // b % 2 == 0) & (t // b % 2 == 1)
            mc[kind, :, MC_LVL + j * P:MC_LVL + (j + 1) * P] = up
            if j == 0:
                mc[kind, :, MC_M0:MC_M0 + P] = up.T
        cd = np.exp(lg * (P if kind == 0 else DS))
        for pair in range(2):
            mc[kind, :64, MC_CDEC + pair] = cd[2 * pair]
            mc[kind, 64:, MC_CDEC + pair] = cd[2 * pair + 1]
        mc[kind, :, MC_BLK:MC_BLK + DB] = (np.arange(P)[:, None] // DS == np.arange(DB))
    rc = np.zeros((P, RC_N), np.float32)
    rc[:, RC_PRIO:RC_PRIO + 4] = np.arange(4, 0, -1)
    rc[:, RC_THR:RC_THR + TILES] = P * np.arange(TILES)
    rc[:, RC_LT:RC_LT + NE * NE] = (np.arange(NE)[None, :] < np.arange(NE)[:, None]).reshape(-1)
    rc[:, RC_TILE:RC_TILE + SLOTS // P] = np.arange(SLOTS // P)
    rc[:, RC_VALID:RC_VALID + TILES] = (np.arange(TILES) < NT) | (np.arange(P)[:, None] < TS)
    rc[:, RC_TRI:RC_TRI + P] = s < t
    return fc, mc, rc


class Signal:

    def __init__(self, nc, ctx, name, per, by=1):
        self.sem = ctx.enter_context(nc.semaphore(name))
        self.per, self.by = per, by

    def at(self, t, j=None):
        return (t * self.per + (self.per if j is None else j)) * self.by


def project(nc, x_all, w_in, proj, sorted_h):
    nb = 6
    per = 2 * TILES
    assert per % nb == 0 and nb % 2 == 0
    with ExitStack() as ctx:
        xT = ctx.enter_context(nc.sbuf_tensor("pj_xT", [P, TILES, KD, P], F32))
        w = [ctx.enter_context(nc.sbuf_tensor(f"pj_w{u}", [P, KD, SLICE], F32)) for u in range(2)]
        stage = [ctx.enter_context(nc.sbuf_tensor(f"pj_out{b}", [P, SLICE], F32)) for b in range(nb)]
        bank = [ctx.enter_context(nc.psum_tensor(f"pj_ps{b}", [P, 512], F32)) for b in range(nb)]
        x_loaded = [ctx.enter_context(nc.semaphore(f"pj_x_loaded{g}")) for g in range(3)]
        w_loaded = [ctx.enter_context(nc.semaphore(f"pj_w_loaded{u}")) for u in range(2)]
        summed = ctx.enter_context(nc.semaphore("pj_summed"))
        bank_free = [ctx.enter_context(nc.semaphore(f"pj_bank_free{e}")) for e in range(2)]
        stored = [ctx.enter_context(nc.semaphore(f"pj_stored{b}")) for b in range(nb)]
        zero = ctx.enter_context(nc.sbuf_tensor("pj_zero", [P, D], F32))
        zero_set = ctx.enter_context(nc.semaphore("pj_zero_set"))
        zeroed = ctx.enter_context(nc.semaphore("pj_zeroed"))
        with nc.Block() as block:

            @block.sync
            def _(sp):
                for u in range(2):
                    sp.dma_start(w[u][:], w_in[u]).then_inc(w_loaded[u], 16)
                    if u == 0:
                        for g in range(3):
                            sp.dma_start(xT[:, 3 * g:3 * g + 3], x_all[:, 3 * g:3 * g + 3]).then_inc(x_loaded[g], 16)

                def two_slices(i, more):
                    for q in range(per):
                        b = q % nb
                        sp.wait_ge(bank_free[q % 2], i * TILES + q // 2 + 1 + nb // 2)
                        rows = proj[P * (q % TILES):P * (q % TILES) + P]
                        cols = rows.rearrange("p (s c) -> s p c", c=SLICE)[2 * i + q // TILES]
                        sp.dma_start(cols, stage[b][:]).then_inc(stored[b], 16)
                        if more and q % TILES == TILES - 1:
                            sp.wait_ge(summed, i * per + q + 1)
                            u = q // TILES
                            sp.dma_start(w[u][:], w_in[2 * i + 2 + u]).then_inc(w_loaded[u], 16)

                with sp.Fori(0, NSLICE // 2 - 1) as i:
                    two_slices(i, True)
                two_slices(NSLICE // 2 - 1, False)
                for b in range(nb):
                    sp.wait_ge(stored[b], 16 * (NSLICE // 2) * (per // nb))

            @block.tensor
            def _(pe):
                for g in range(3):
                    pe.wait_ge(x_loaded[g], 16)
                with pe.Fori(0, NSLICE // 2) as i:
                    for q in range(per):
                        u, m, b = q // TILES, q % TILES, q % nb
                        if m == 0:
                            pe.wait_ge(w_loaded[u], (i + 1) * 16)
                        pe.wait_ge(bank_free[q % 2], i * TILES + q // 2 + 1)
                        for k in range(KD):
                            mm = nc.tensor.matmul(bank[b][:, 0:SLICE], xT[:, m, k], w[u][:, k], start=(k == 0), stop=(k == KD - 1))
                        mm.then_inc(summed, 1)

            @block.gpsimd
            def _(pool):
                nc.gpsimd.memset(zero[:], 0.0).then_inc(zero_set, 1)
                pool.wait_ge(zero_set, 1)
                with pool.Fori(0, SLOTS // P) as j:
                    pool.dma_start(sorted_h.rearrange("(j p) d -> j p d", p=P)[j], zero[:]).then_inc(zeroed, 16)
                pool.wait_ge(zeroed, 16 * (SLOTS // P))

            def copy_out(eng, e, copy):
                eng.sem_inc(bank_free[e], nb // 2)
                with eng.Fori(0, NSLICE // 2) as i:
                    for q in range(e, per, 2):
                        b = q % nb
                        eng.wait_ge(summed, i * per + q + 1)
                        eng.wait_ge(stored[b], (i * (per // nb) + q // nb) * 16)
                        copy(stage[b][:], bank[b][:, 0:SLICE]).then_inc(bank_free[e], 1)

            @block.scalar
            def _(act):
                copy_out(act, 0, nc.scalar.copy)

            @block.vector
            def _(dve):
                copy_out(dve, 1, nc.vector.tensor_copy)


def mixer(nc, proj, vecs, w_lora, w_gate, fconst, mconst, ident_d, s0T_d, r0_d, yT_d, wkv_p, ret_p, wkv_s, ret_s):
    with ExitStack() as ctx:
        def sb(name, shape):
            return ctx.enter_context(nc.sbuf_tensor("mx_" + name, shape, F32))

        def two(name, shape):
            return [sb(f"{name}{u}", shape) for u in range(2)]

        def sig(name, per, by=1):
            return Signal(nc, ctx, "mx_" + name, per, by)

        vec = sb("vec", [P, VEC_N])
        wlo = sb("wlo", [P, WA])
        wga = sb("wga", [P, WA])
        mc = sb("mc", [P, MC_N])
        ident = sb("ident", [P, P])
        halves = sb("halves", [P, 8])
        one = sb("one", [P, 1])
        fc = two("fc", [P, FC_N])
        cur = sb("cur", [P, SHIFT_W])
        sh = two("sh", [P, SHIFT_W])
        curB = two("curB", [P, IN_W - SHIFT_W])
        loraT = sb("loraT", [P, 2 * P])
        lw = sb("lw", [P, WA])
        ga = sb("ga", [P, WA])
        gate = two("gate", [P, WA])
        kk = sb("kk", [P, WA])
        kp = sb("kp", [P, WA])
        t1 = sb("t1", [P, WA])
        t3 = sb("t3", [P, WA])
        e1 = sb("e1", [P, WA])
        e2 = sb("e2", [P, WA])
        e3 = sb("e3", [P, WA])
        ss = sb("ss", [P, HA])
        rn = sb("rn", [P, HA])
        em = two("em", [P, HA // 2, DB])
        bt = two("bt", [P, WA])
        kt = two("kt", [P, WA])
        bonus = two("bonus", [P, HA])
        rot = sb("rot", [P, 2 * HB * NK])
        qh = sb("qh", [P, HB * NK])
        kh = two("kh", [P, HB * NK])
        arT = sb("arT", [P, HA // 2, 2, P])
        bT = sb("bT", [P, HA // 2, P])
        kT = sb("kT", [P, HA // 2, P])
        qT = sb("qT", [P, 4, P])
        kTr = sb("kTr", [P, 2, P])
        G = sb("G", [P, HA, 4, P])
        scT = sb("scT", [P, HB, P])
        ET = two("ET", [P, 4, P])
        M = two("M", [P, 4, P])
        MT = two("MT", [P, 4, P])
        X = two("X", [P, 4, P])
        wsb = sb("wsb", [P, HA, NA])
        usb = sb("usb", [P, HA, NA])
        S = sb("S", [P, HA // 2, NA])
        S0 = sb("S0", [P, HA // 2, 2, NA])
        R = sb("R", [P, HB // 2, 2, NV])
        t2 = sb("t2", [P, WA])
        y = sb("y", [P, HA + HB * 2, NA])
        sq = sb("sq", [P, WA])
        sg = sb("sg", [P, WA])
        mean = sb("mean", [P, HA + HB])
        var = sb("var", [P, HA + HB])
        rs = sb("rs", [P, HA + HB])
        yT = sb("yT", [P, KD, P])
        mcs = sb("mcs", [P, MC_N])
        s0T = sb("s0T", [P, DB, 4, NA])
        r0 = sb("r0", [P, DB, 2, NV])
        wTs = sb("wTs", [64, 2, 4, 2, TS])
        oTs = sb("oTs", [P, 2, 2, TS])
        B = [ctx.enter_context(nc.psum_tensor(f"mx_ps{b}", [P, 512], F32)) for b in range(8)]

        def v(name, width=WA):
            return vec[:, VEC_OFF[name]:VEC_OFF[name] + width]

        def heads(x, n):
            return x.rearrange("p (h d) -> p h d", h=n)

        def over(x, n):
            return x.unsqueeze(2).broadcast_to([P, x.shape[1], n])

        const_in = sig("const_in", 1)
        half_set = sig("half_set", 1)
        s_zero = sig("s_zero", 1)
        cur_in = [sig(f"cur_in{u}", 1, 16) for u in range(2)]
        sh_in = [sig(f"sh_in{u}", 1, 16) for u in range(2)]
        curB_in = [sig(f"curB_in{u}", 1, 16) for u in range(2)]
        fc_in = [sig(f"fc_in{u}", 1, 16) for u in range(2)]
        mix_d = sig("mix_d", 3)
        lora_d = sig("lora_d", 1)
        z_d = sig("z_d", 2)
        lwa_d = sig("lwa_d", 2)
        kk_d = sig("kk_d", 7)
        scaled_d = sig("scaled_d", 4)
        bonus_d = sig("bonus_d", 3)
        rot_d = sig("rot_d", 6)
        gram_d = sig("gram_d", HA)
        sc_d = sig("sc_d", 2)
        s0_d = sig("s0_d", 2)
        m0_d = sig("m0_d", 4)
        m_d = sig("m_d", 2 * (LEVELS - 2))
        mt_d = sig("mt_d", 2 * (LEVELS - 1))
        state_d = sig("state_d", 7)
        ya_d = sig("ya_d", 11)
        yb_d = sig("yb_d", 9)
        lora_a = sig("lora_a", 2)
        loraT_a = sig("loraT_a", 1)
        tz_a = sig("tz_a", 2)
        gate_a = sig("gate_a", 1)
        kksq_a = sig("kksq_a", 1)
        exp_a = sig("exp_a", 4)
        turn_a = sig("turn_a", 6)
        x_a = sig("x_a", 2 * (LEVELS - 1))
        w_a = sig("w_a", 1)
        u_a = sig("u_a", 1)
        sil_a = sig("sil_a", 1)
        sq_a = sig("sq_a", 2)
        yT_a = sig("yT_a", 2)
        rn_g = sig("rn_g", 1)
        mt0_g = sig("mt0_g", 4)
        et_g = sig("et_g", 2 * (LEVELS - 1))
        rs_g = sig("rs_g", 2)
        sil1_g = sig("sil1_g", 1)
        sil_g = sig("sil_g", 1)
        loraT_p = sig("loraT_p", 1)
        z_p = sig("z_p", 3)
        cum_p = sig("cum_p", 3)
        turn_p = sig("turn_p", 6)
        gram_p = sig("gram_p", HA)
        sc_p = sig("sc_p", 1)
        l0_p = sig("l0_p", 2)
        x_p = sig("x_p", 2 * (LEVELS - 1))
        m_p = sig("m_p", 2 * (LEVELS - 2))
        mt_p = sig("mt_p", 2 * (LEVELS - 1))
        w_p = sig("w_p", 1)
        u_p = sig("u_p", 1)
        y_p = sig("y_p", 1)
        ds_p = sig("ds_p", 1)
        o_p = sig("o_p", 1)
        dr_p = sig("dr_p", 1)
        yT_p = sig("yT_p", 2)
        yT_out = sig("yT_out", 1, 16)
        s0T_in = sig("s0T_in", 1, 16)
        blk_d = sig("blk_d", 8)
        sum_d = sig("sum_d", 4)
        new_d = sig("new_d", 8)
        new_p = sig("new_p", 8)
        sw_p = sig("sw_p", 1)
        sw_a = sig("sw_a", 4)
        st_out = sig("st_out", 1, 16)

        ex = ctx.enter_context(ExitStack())
        block = ex.enter_context(nc.Block())

        def tiles(eng, prologue, body, epilogue):
            prologue()
            with eng.Fori(0, NT // 2) as i:
                for u in range(2):
                    body(2 * i + u, u, i)
            epilogue()

        @block.sync
        def _(sp):
            for dst, src in ((vec, vecs.broadcast_to([P, VEC_N])), (wlo, w_lora), (wga, w_gate), (mc, mconst[0]), (mcs, mconst[1]), (ident, ident_d)):
                sp.dma_start(dst[:], src).then_inc(const_in.sem, 16)

            def load(t, u, k, sample=False):
                sp.wait_ge(mix_d.sem, mix_d.at(t, 0))
                if sample:
                    rows = proj[SAMPLE0:SAMPLE0 + DB * (DS + 1)].rearrange("(b t) c -> b t c", b=DB)
                    sp.dma_start(cur[0:TS, :], rows[:, 1:, 0:SHIFT_W]).then_inc(cur_in[u].sem, 16)
                    sp.dma_start(sh[u][0:TS, :], rows[:, :DS, 0:SHIFT_W]).then_inc(sh_in[u].sem, 16)
                    sp.dma_start(curB[u][0:TS, :], rows[:, 1:, SHIFT_W:]).then_inc(curB_in[u].sem, 16)
                else:
                    own = proj[1:1 + SEQ].rearrange("(n p) c -> n p c", p=P)[t]
                    sp.dma_start(cur[:], own[:, 0:SHIFT_W]).then_inc(cur_in[u].sem, 16)
                    sp.dma_start(sh[u][:], proj[0:SEQ].rearrange("(n p) c -> n p c", p=P)[t, :, 0:SHIFT_W]).then_inc(sh_in[u].sem, 16)
                    sp.dma_start(curB[u][:], own[:, SHIFT_W:]).then_inc(curB_in[u].sem, 16)
                sp.dma_start(fc[u][:], fconst[t]).then_inc(fc_in[u].sem, 16)

            def store(t):
                sp.wait_ge(yT_a.sem, yT_a.at(t))
                sp.dma_start(yT_d[t], yT[:]).then_inc(yT_out.sem, 16)

            load(0, 0, 0)
            sp.dma_start(s0T[:], s0T_d).then_inc(s0T_in.sem, 16)
            sp.dma_start(r0[:], r0_d).then_inc(s0T_in.sem, 16)
            with sp.Fori(0, NT // 2 - 1) as i:
                load(2 * i + 1, 1, i)
                store(2 * i)
                load(2 * i + 2, 0, i + 1)
                store(2 * i + 1)
            load(NT - 1, 1, NT // 2 - 1)
            store(NT - 2)
            load(NT, 0, NT // 2, sample=True)
            store(NT - 1)
            sp.wait_ge(state_d.sem, state_d.at(NT - 1))
            sp.dma_start(wkv_p, S[:]).then_inc(st_out.sem, 16)
            for o in range(2):
                r = slice(64 * o, 64 * o + 64)
                sp.dma_start(ret_p[r], R[r, :, o]).then_inc(st_out.sem, 16)
            store(NT)
            sp.wait_ge(new_d.sem, 8)
            sp.dma_start(wkv_s, s0T[:]).then_inc(st_out.sem, 16)
            sp.dma_start(ret_s, r0[:]).then_inc(st_out.sem, 16)
            sp.wait_ge(yT_out.sem, yT_out.at(NT))
            sp.wait_ge(st_out.sem, 16 * 5)

        @block.tensor
        def _(pe):
            mm = nc.tensor.matmul

            def f_loraT(t, u):
                pe.wait_ge(lora_d.sem, lora_d.at(t))
                pe.wait_ge(exp_a.sem, exp_a.at(t, 0))
                nc.tensor.transpose(B[0][:, 0:P], sh[u][:, 3 * WA:3 * WA + P], ident[:])
                nc.tensor.transpose(B[0][:, P:2 * P], sh[u][:, 3 * WA + P:3 * WA + 2 * P], ident[:]).then_inc(loraT_p.sem, 1)

            def f_z(t, u):
                pe.wait_ge(loraT_a.sem, loraT_a.at(t))
                mm(B[1][:], loraT[0:64, 0:P], wlo[0:64, :], start=True, stop=True).then_inc(z_p.sem, 1)
                mm(B[0][:], loraT[64:128, 0:P], wlo[64:128, :], start=True, stop=True).then_inc(z_p.sem, 1)
                pe.wait_ge(z_d.sem, z_d.at(t, 1))
                mm(B[1][:], loraT[:, P:2 * P], wga[:], start=True, stop=True).then_inc(z_p.sem, 1)

            def f_cum(t, u):
                pe.wait_ge(lwa_d.sem, lwa_d.at(t, 1))
                mm(B[0][:], fc[u][:, FC_TI:FC_TI + P], lw[:], start=True, stop=True).then_inc(cum_p.sem, 1)
                pe.wait_ge(gate_a.sem, gate_a.at(t))
                mm(B[1][:], fc[u][:, FC_TE:FC_TE + P], lw[:], start=True, stop=True).then_inc(cum_p.sem, 1)
                pe.wait_ge(exp_a.sem, exp_a.at(t, 2))
                for q in range(HA // 2):
                    m = mm(B[0][:, q * DB:(q + 1) * DB], lw[:, q * P:(q + 1) * P], fc[u][:, FC_SEL:FC_SEL + DB], start=True, stop=True)
                m.then_inc(cum_p.sem, 1)

            def turn(t, u):
                srcs = [(e2, scaled_d, 4), (bt[u], scaled_d, 1), (e1, scaled_d, 3), (kt[u], scaled_d, 2)]
                for n, (src, s, j) in enumerate(srcs):
                    pe.wait_ge(s.sem, s.at(t, j))
                    if n < 2:
                        pe.wait_ge(yT_a.sem, yT_a.at(t, 0))
                    else:
                        pe.wait_ge(turn_a.sem, turn_a.at(t, n - 1))
                    for q in range(4):
                        m = nc.tensor.transpose(B[2 + n % 2][:, q * P:(q + 1) * P], src[:, q * P:(q + 1) * P], ident[:])
                    m.then_inc(turn_p.sem, 1)
                pe.wait_ge(rot_d.sem, rot_d.at(t))
                pe.wait_ge(turn_a.sem, turn_a.at(t, 3))
                for q in range(4):
                    src = rot[:, q * P:(q + 1) * P] if q < 2 else qh[:, (q - 2) * P:(q - 1) * P]
                    m = nc.tensor.transpose(B[2][:, q * P:(q + 1) * P], src, ident[:])
                m.then_inc(turn_p.sem, 1)
                pe.wait_ge(turn_a.sem, turn_a.at(t, 4))
                for q in range(2):
                    m = nc.tensor.transpose(B[3][:, q * P:(q + 1) * P], rot[:, (q + 2) * P:(q + 3) * P], ident[:])
                m.then_inc(turn_p.sem, 1)

            def grams(t):
                pe.wait_ge(turn_a.sem, turn_a.at(t, 4))
                pe.wait_ge(state_d.sem, state_d.at(t, 0))
                for h in range(HA):
                    q, r = h // 2, slice(64 * (h % 2), 64 * (h % 2) + 64)
                    if h >= 2:
                        pe.wait_ge(gram_d.sem, gram_d.at(t, h - 1))
                    mm(B[4 + h % 2][:, 0:2 * P], bT[r, q], arT[r, q], start=True, stop=True)
                    mm(B[4 + h % 2][:, 2 * P:], kT[r, q], arT[r, q], start=True, stop=True).then_inc(gram_p.sem, 1)
                pe.wait_ge(turn_a.sem, turn_a.at(t, 6))
                for h in (0, 2, 1, 3):
                    q, r = h // 2, slice(64 * (h % 2), 64 * (h % 2) + 64)
                    m = mm(B[6 + h % 2][:, q * P:(q + 1) * P], kTr[r, q], qT[r, q], start=True, stop=True)
                m.then_inc(sc_p.sem, 1)
                for g in range(2):
                    pe.wait_ge(gram_d.sem, gram_d.at(t, 4 * g + 4))
                    for h in range(4):
                        m = nc.tensor.transpose(B[2 + g][:, h * P:(h + 1) * P], G[:, 4 * g + h, 0], ident[:])
                    m.then_inc(l0_p.sem, 1)

            def level(t, j, last=LEVELS - 1):
                n = 2 * (j - 1)
                for g in range(2):
                    pe.wait_ge(et_g.sem, et_g.at(t, n + g + 1))
                    if j == 1:
                        pe.wait_ge(m0_d.sem, m0_d.at(t, 2 * g + 2))
                    else:
                        pe.wait_ge(m_d.sem, m_d.at(t, n - 2 + g + 1))
                    for h in range(4):
                        m = mm(B[2 + g][:, h * P:(h + 1) * P], ET[g][:, h], M[g][:, h], start=True, stop=True)
                    m.then_inc(x_p.sem, 1)
                for g in range(2):
                    pe.wait_ge(x_a.sem, x_a.at(t, n + g + 1))
                    if j == 1:
                        pe.wait_ge(mt0_g.sem, mt0_g.at(t, 2 * g + 2))
                        pe.wait_ge(gram_d.sem, gram_d.at(t))
                        pe.wait_ge(sc_d.sem, sc_d.at(t))
                    else:
                        pe.wait_ge(mt_d.sem, mt_d.at(t, n - 2 + g + 1))
                    if j < last:
                        for h in range(4):
                            m = mm(B[4 + g][:, h * P:(h + 1) * P], MT[g][:, h], X[g][:, h], start=True, stop=True)
                        m.then_inc(m_p.sem, 1)
                    for h in range(4):
                        m = mm(B[6 + g][:, h * P:(h + 1) * P], X[g][:, h], MT[g][:, h], start=True, stop=True)
                    m.then_inc(mt_p.sem, 1)

            def chunk(t, u, i, sample, last):
                n = TS if sample else P
                vA, vB = sh[u], curB[u]
                pe.wait_ge(mt_d.sem, mt_d.at(t, 2 * last))
                if sample:
                    pe.wait_ge(s0T_in.sem, 32)
                    for par in range(2):
                        r = slice(64 * par, 64 * par + 64)
                        for q in range(4):
                            for b in range(DB):
                                out = B[2 + par][0:64, q * P:(q + 1) * P].rearrange("p (w t) -> p w t", w=2)[:, :, b * DS:(b + 1) * DS]
                                m = mm(out, s0T[r, b, q], arT[r, q, :, b * DS:(b + 1) * DS], start=True, stop=True)
                        m.then_inc(sw_p.sem, 1)
                        for q in range(2):
                            for b in range(DB):
                                m = mm(B[6 + par][:, q * TS + b * DS:q * TS + (b + 1) * DS], r0[r, b, q], qT[r, 2 + q, b * DS:(b + 1) * DS], start=True, stop=True)
                        m.then_inc(sw_p.sem, 1)
                    pe.wait_ge(sw_a.sem, 4)
                else:
                    pe.wait_ge(state_d.sem, state_d.at(t, 0))
                for h in range(HB):
                    q, r = h // 2, slice(64 * (h % 2), 64 * (h % 2) + 64)
                    o = B[6][0:n, h * NV:(h + 1) * NV]
                    if sample:
                        mm(o, oTs[:, h % 2, q], ident[:], start=True, stop=False)
                    elif h % 2 == 0:
                        mm(B[6][:, h * NV:(h + 2) * NV], qT[:, 2 + q], R[:, q], start=True, stop=False)
                    m = mm(o, scT[0:n, h, 0:n], vB[0:n, 512 + h * NV:512 + (h + 1) * NV], start=False, stop=sample or h % 2 == 1)
                m.then_inc(o_p.sem, 1)
                if not sample:
                    for h in range(HB):
                        q, r = h // 2, slice(64 * (h % 2), 64 * (h % 2) + 64)
                        m = mm(B[7][r, q * NV:(q + 1) * NV], kh[u][:, h * NK:(h + 1) * NK], vB[:, 512 + h * NV:512 + (h + 1) * NV], start=True, stop=True)
                    m.then_inc(dr_p.sem, 1)
                    pe.wait_ge(s0_d.sem, s0_d.at(t))
                pe.wait_ge(x_a.sem, x_a.at(t, 2 * last))
                for h in range(HA):
                    q, r = h // 2, slice(64 * (h % 2), 64 * (h % 2) + 64)
                    o = B[2][0:n, h * NA:(h + 1) * NA]
                    if sample:
                        mm(o, wTs[0:64, h % 2, q, 0], ident[0:64, 0:64], start=True, stop=False)
                    elif h % 2 == 0:
                        mm(B[2][:, h * NA:(h + 2) * NA], arT[:, q, 0], S0[:, q], start=True, stop=False)
                    m = mm(o, G[0:n, h, 2, 0:n], vA[0:n, 2 * WA + h * NA:2 * WA + (h + 1) * NA], start=False, stop=sample or h % 2 == 1)
                m.then_inc(w_p.sem, 1)
                pe.wait_ge(w_a.sem, w_a.at(t))
                for h in range(HA):
                    m = mm(B[3][0:n, h * NA:(h + 1) * NA], MT[h // 4][0:n, h % 4, 0:n], wsb[0:n, h], start=True, stop=True)
                m.then_inc(u_p.sem, 1)
                pe.wait_ge(u_a.sem, u_a.at(t))
                pe.wait_ge(m_d.sem, m_d.at(t, 2 * last - 2))
                if not sample:
                    for h in range(HA):
                        q, r = h // 2, slice(64 * (h % 2), 64 * (h % 2) + 64)
                        cols, val = slice(h * NA, (h + 1) * NA), slice(2 * WA + h * NA, 2 * WA + (h + 1) * NA)
                        mm(B[5][r, q * NA:(q + 1) * NA], bt[u][:, cols], usb[:, h], start=True, stop=False)
                        m = mm(B[5][r, q * NA:(q + 1) * NA], kt[u][:, cols], vA[:, val], start=False, stop=True)
                    m.then_inc(ds_p.sem, 1)
                for h in range(HA):
                    q, r = h // 2, slice(64 * (h % 2), 64 * (h % 2) + 64)
                    o = B[4][0:n, h * NA:(h + 1) * NA]
                    if sample:
                        mm(o, wTs[0:64, h % 2, q, 1], ident[0:64, 0:64], start=True, stop=False)
                    elif h % 2 == 0:
                        mm(B[4][:, h * NA:(h + 2) * NA], arT[:, q, 1], S0[:, q], start=True, stop=False)
                    mm(o, G[0:n, h, 1, 0:n], usb[0:n, h], start=False, stop=False)
                    m = mm(o, G[0:n, h, 3, 0:n], vA[0:n, 2 * WA + h * NA:2 * WA + (h + 1) * NA], start=False, stop=sample or h % 2 == 1)
                m.then_inc(y_p.sem, 1)

            def sampled_states(t, u):
                pe.wait_ge(exp_a.sem, exp_a.at(t))
                for j in range(8):
                    bank = B[5] if j % 2 == 0 else B[0]
                    pe.wait_ge(blk_d.sem, j + 1)
                    if j >= 2:
                        pe.wait_ge(new_d.sem, j - 1)
                    for o in range(2):
                        r = slice(64 * o, 64 * o + 64)
                        if j < 4:
                            cols = slice((2 * j + o) * NA, (2 * j + o + 1) * NA)
                            mm(bank[r, :], bt[u][0:TS, cols], X[o][0:TS], start=True, stop=False)
                            m = mm(bank[r, :], kt[u][0:TS, cols], ET[o][0:TS], start=False, stop=True)
                        else:
                            h = 2 * (j % 2) + o
                            m = mm(bank[r, :], kh[u][0:TS, h * NK:(h + 1) * NK], X[o][0:TS], start=True, stop=True)
                    m.then_inc(new_p.sem, 1)

            def turn_y(t):
                for n, (s, b) in enumerate(((ya_d, 2), (yb_d, 3))):
                    pe.wait_ge(s.sem, s.at(t))
                    pe.wait_ge(yT_a.sem, yT_a.at(t, 0))
                    for q in range(4):
                        src = y[:, 8 * n + 2 * q:8 * n + 2 * q + 2].rearrange("p h d -> p (h d)")
                        m = nc.tensor.transpose(B[b][:, q * P:(q + 1) * P], src, ident[:])
                    m.then_inc(yT_p.sem, 1)

            def start():
                pe.wait_ge(const_in.sem, 16 * NCONST)
                pe.wait_ge(fc_in[0].sem, 16)
                f_loraT(0, 0)
                f_z(0, 0)
                f_cum(0, 0)

            def body(t, u, i):
                turn(t, u)
                grams(t)
                level(t, 1)
                level(t, 2)
                f_loraT(t + 1, 1 - u)
                level(t, 3)
                f_z(t + 1, 1 - u)
                level(t, 4)
                level(t, 5)
                pe.wait_ge(fc_in[1 - u].sem, (i + 1 + u) * 16)
                f_cum(t + 1, 1 - u)
                level(t, 6)
                chunk(t, u, i, False, LEVELS - 1)
                turn_y(t)

            def end():
                turn(NT, 0)
                grams(NT)
                level(NT, 1, LEVELS_S - 1)
                level(NT, 2, LEVELS_S - 1)
                chunk(NT, 0, NT // 2, True, LEVELS_S - 1)
                turn_y(NT)
                sampled_states(NT, 0)

            tiles(pe, start, body, end)

        @block.scalar
        def _(act):
            fn = nc.scalar.activation
            cp = nc.scalar.copy

            def f_lora(t, u):
                act.wait_ge(mix_d.sem, mix_d.at(t))
                w, g = sh[u][:, 3 * WA:3 * WA + 64], sh[u][:, 3 * WA + P:3 * WA + 2 * P]
                fn(w, w, ACT.Tanh).then_inc(lora_a.sem, 1)
                fn(g, g, ACT.Tanh, scale=0.5).then_inc(lora_a.sem, 1)

            def f_kksq(t):
                act.wait_ge(kk_d.sem, kk_d.at(t, 1))
                fn(e3[:], kk[:], ACT.Square).then_inc(kksq_a.sem, 1)

            def f_loraT(t):
                act.wait_ge(loraT_p.sem, loraT_p.at(t))
                cp(loraT[:], B[0][:, 0:2 * P]).then_inc(loraT_a.sem, 1)

            def f_z(t, u):
                act.wait_ge(z_d.sem, z_d.at(t, 1))
                fn(lw[:], lw[:], ACT.Tanh, scale=0.5).then_inc(tz_a.sem, 1)
                act.wait_ge(z_d.sem, z_d.at(t, 2))
                fn(ga[:], ga[:], ACT.Tanh, scale=0.5).then_inc(tz_a.sem, 1)
                act.wait_ge(z_p.sem, z_p.at(t, 3))
                cp(gate[u][:], B[1][:]).then_inc(gate_a.sem, 1)

            def f_exp(t, u):
                act.wait_ge(cum_p.sem, cum_p.at(t, 1))
                fn(e1[:], B[0][:], ACT.Exp).then_inc(exp_a.sem, 1)
                act.wait_ge(kk_d.sem, kk_d.at(t, 2))
                fn(e3[:], B[0][:], ACT.Exp, scale=-1.0).then_inc(exp_a.sem, 1)
                act.wait_ge(cum_p.sem, cum_p.at(t, 2))
                fn(e2[:], B[1][:], ACT.Exp).then_inc(exp_a.sem, 1)
                act.wait_ge(cum_p.sem, cum_p.at(t, 3))
                fn(em[u][:], B[0][:, 0:HA // 2 * DB].rearrange("p (q b) -> p q b", b=DB), ACT.Exp).then_inc(exp_a.sem, 1)

            def turn(t):
                outs = [(arT[:, :, 0], 2, 512), (bT[:], 3, 512), (arT[:, :, 1], 2, 512), (kT[:], 3, 512), (qT[:], 2, 512), (kTr[:], 3, 256)]
                for n, (out, b, w) in enumerate(outs):
                    act.wait_ge(turn_p.sem, turn_p.at(t, n + 1))
                    cp(out, B[b][:, 0:w].rearrange("p (q t) -> p q t", t=P)).then_inc(turn_a.sem, 1)

            def level(t, j):
                for g in range(2):
                    n = 2 * (j - 1) + g + 1
                    act.wait_ge(x_p.sem, x_p.at(t, n))
                    if j > 1:
                        act.wait_ge(mt_p.sem, mt_p.at(t, n - 2))
                    cp(X[g][:], B[2 + g][:].rearrange("p (h t) -> p h t", t=P)).then_inc(x_a.sem, 1)

            def tail(t, u, n, sample):
                if sample:
                    for par in range(2):
                        act.wait_ge(sw_p.sem, 2 * par + 1)
                        cp(wTs[:, par], B[2 + par][0:64, :].rearrange("p (q w t) -> p q w t", q=4, w=2)).then_inc(sw_a.sem, 1)
                        act.wait_ge(sw_p.sem, 2 * par + 2)
                        cp(oTs[:, par], B[6 + par][:, 0:2 * TS].rearrange("p (q t) -> p q t", q=2)).then_inc(sw_a.sem, 1)
                fn(sg[:], curB[u][:, 1024:1536], ACT.Tanh, scale=0.5).then_inc(sil_a.sem, 1)
                act.wait_ge(w_p.sem, w_p.at(t))
                cp(wsb[0:n], B[2][0:n].rearrange("p (h d) -> p h d", h=HA)).then_inc(w_a.sem, 1)
                act.wait_ge(u_p.sem, u_p.at(t))
                cp(usb[0:n], B[3][0:n].rearrange("p (h d) -> p h d", h=HA)).then_inc(u_a.sem, 1)
                act.wait_ge(yb_d.sem, yb_d.at(t, 3))
                fn(sq[:], y[:, 8:16].rearrange("p h d -> p (h d)"), ACT.Square).then_inc(sq_a.sem, 1)
                act.wait_ge(ya_d.sem, ya_d.at(t, 3))
                fn(t2[:], y[:, 0:8].rearrange("p h d -> p (h d)"), ACT.Square).then_inc(sq_a.sem, 1)
                act.wait_ge(yT_out.sem, yT_out.at(t, 0))
                for k in range(2):
                    act.wait_ge(yT_p.sem, yT_p.at(t, k + 1))
                    cp(yT[:, 4 * k:4 * k + 4], B[2 + k][:].rearrange("p (k t) -> p k t", t=P)).then_inc(yT_a.sem, 1)

            def start():
                f_lora(0, 0)
                f_kksq(0)
                f_loraT(0)
                f_z(0, 0)
                f_exp(0, 0)

            def body(t, u, i):
                turn(t)
                level(t, 1)
                f_lora(t + 1, 1 - u)
                level(t, 2)
                f_kksq(t + 1)
                f_loraT(t + 1)
                level(t, 3)
                level(t, 4)
                f_z(t + 1, 1 - u)
                level(t, 5)
                f_exp(t + 1, 1 - u)
                level(t, 6)
                tail(t, u, P, False)

            def end():
                turn(NT)
                level(NT, 1)
                level(NT, 2)
                tail(NT, 0, TS, True)

            tiles(act, start, body, end)

        @block.vector
        def _(dve):
            tt = nc.vector.tensor_tensor
            ts = nc.vector.tensor_scalar
            stt = nc.vector.scalar_tensor_tensor

            def f_mix(t, u, k):
                dve.wait_ge(cur_in[u].sem, (k + 1) * 16)
                dve.wait_ge(sh_in[u].sem, (k + 1) * 16)
                tt(sh[u][:], sh[u][:], cur[:], ALU.subtract).then_inc(mix_d.sem, 1)
                dve.wait_ge(mix_d.sem, mix_d.at(t, 1))
                tt(sh[u][:], sh[u][:], v("mu_shift", SHIFT_W), ALU.mult).then_inc(mix_d.sem, 1)
                dve.wait_ge(mix_d.sem, mix_d.at(t, 2))
                tt(sh[u][:], sh[u][:], cur[:], ALU.add).then_inc(mix_d.sem, 1)

            def f_lora(t, u):
                dve.wait_ge(lora_a.sem, lora_a.at(t))
                g = sh[u][:, 3 * WA + P:3 * WA + 2 * P]
                ts(g, g, 0.5, 0.5, ALU.mult, ALU.add).then_inc(lora_d.sem, 1)

            def f_kk1(t, u):
                dve.wait_ge(mix_d.sem, mix_d.at(t))
                tt(kk[:], sh[u][:, WA:2 * WA], v("k_k"), ALU.mult).then_inc(kk_d.sem, 1)
                dve.wait_ge(kksq_a.sem, kksq_a.at(t))
                nc.vector.tensor_reduce(ss[:], heads(e3[:], HA), AX, ALU.add).then_inc(kk_d.sem, 1)
                dve.wait_ge(kk_d.sem, kk_d.at(t, 2))
                ts(ss[:], ss[:], 1e-24, None, ALU.max).then_inc(kk_d.sem, 1)

            def f_z(t):
                dve.wait_ge(z_p.sem, z_p.at(t, 1))
                tt(lw[:], B[1][:], v("decay_base"), ALU.add).then_inc(z_d.sem, 1)
                dve.wait_ge(z_p.sem, z_p.at(t, 2))
                tt(ga[:], B[0][:], v("aaa_base"), ALU.add).then_inc(z_d.sem, 1)

            def f_lwa(t):
                dve.wait_ge(tz_a.sem, tz_a.at(t, 1))
                ts(lw[:], lw[:], 1.0, W_CONST / 2, ALU.add, ALU.mult).then_inc(lwa_d.sem, 1)
                dve.wait_ge(tz_a.sem, tz_a.at(t, 2))
                ts(ga[:], ga[:], 0.5, 0.5, ALU.mult, ALU.add).then_inc(lwa_d.sem, 1)

            def f_kk2(t, u):
                dve.wait_ge(rn_g.sem, rn_g.at(t))
                tt(heads(kk[:], HA), heads(kk[:], HA), over(rn[:], NA), ALU.mult).then_inc(kk_d.sem, 1)
                dve.wait_ge(lwa_d.sem, lwa_d.at(t))
                dve.wait_ge(kk_d.sem, kk_d.at(t, 4))
                tt(bt[u][:], kk[:], ga[:], ALU.mult).then_inc(kk_d.sem, 1)
                if not isinstance(t, int):
                    dve.wait_ge(ya_d.sem, ya_d.at(t - 1, 0))
                stt(t1[:], ga[:], -1.0, v("k_a"), ALU.add, ALU.mult).then_inc(kk_d.sem, 1)
                dve.wait_ge(kk_d.sem, kk_d.at(t, 6))
                stt(kp[:], t1[:], 1.0, sh[u][:, WA:2 * WA], ALU.add, ALU.mult).then_inc(kk_d.sem, 1)

            def f_scale(t, u):
                dve.wait_ge(exp_a.sem, exp_a.at(t, 2))
                dve.wait_ge(kk_d.sem, kk_d.at(t, 7))
                tt(bt[u][:], bt[u][:], e3[:], ALU.mult).then_inc(scaled_d.sem, 1)
                tt(kt[u][:], kp[:], e3[:], ALU.mult).then_inc(scaled_d.sem, 1)
                tt(e1[:], e1[:], sh[u][:, 0:WA], ALU.mult).then_inc(scaled_d.sem, 1)
                dve.wait_ge(exp_a.sem, exp_a.at(t, 3))
                stt(e2[:], kk[:], -1.0, e2[:], ALU.mult, ALU.mult).then_inc(scaled_d.sem, 1)
                dve.wait_ge(rot_d.sem, rot_d.at(t))
                tt(t1[:], sh[u][:, 0:WA], kp[:], ALU.mult).then_inc(bonus_d.sem, 1)
                dve.wait_ge(bonus_d.sem, bonus_d.at(t, 1))
                tt(t1[:], t1[:], v("r_k"), ALU.mult).then_inc(bonus_d.sem, 1)
                dve.wait_ge(bonus_d.sem, bonus_d.at(t, 2))
                nc.vector.tensor_reduce(bonus[u][:], heads(t1[:], HA), AX, ALU.add).then_inc(bonus_d.sem, 1)

            def f_rot(t, u, k):
                dve.wait_ge(curB_in[u].sem, (k + 1) * 16)
                dve.wait_ge(fc_in[u].sem, (k + 1) * 16)
                dve.wait_ge(kk_d.sem, kk_d.at(t, 7))
                x = curB[u][:, 0:512].rearrange("p (n d) -> p n d", d=32)
                cos = fc[u][:, FC_COS:FC_COS + 32].unsqueeze(1).broadcast_to([P, 16, 32])
                sin = fc[u][:, FC_SIN:FC_SIN + 32].unsqueeze(1).broadcast_to([P, 16, 32])
                a4, b4 = (z[:].rearrange("p (h two d) -> p h two d", two=2, d=32) for z in (t3, t1))
                r4 = rot[:].rearrange("p (h two d) -> p h two d", two=2, d=32)
                tt(t3[:].rearrange("p (n d) -> p n d", d=32), x, cos, ALU.mult).then_inc(rot_d.sem, 1)
                tt(t1[:].rearrange("p (n d) -> p n d", d=32), x, sin, ALU.mult).then_inc(rot_d.sem, 1)
                dve.wait_ge(rot_d.sem, rot_d.at(t, 2))
                tt(r4[:, :, 0], a4[:, :, 0], b4[:, :, 1], ALU.subtract).then_inc(rot_d.sem, 1)
                tt(r4[:, :, 1], b4[:, :, 0], a4[:, :, 1], ALU.add).then_inc(rot_d.sem, 1)
                dve.wait_ge(rot_d.sem, rot_d.at(t, 4))
                for out, c0, col in ((qh, 0, FC_CROSS), (kh[u], 256, FC_KDEC)):
                    tt(heads(out[:], HB), heads(rot[:, c0:c0 + 256], HB), over(fc[u][:, col:col + HB], NK), ALU.mult).then_inc(rot_d.sem, 1)

            def grams(t, u, c, sample):
                for h in range(HA):
                    dve.wait_ge(gram_p.sem, gram_p.at(t, h + 1))
                    tt(G[:, h].rearrange("p a b -> p (a b)"), B[4 + h % 2][:], c[:, MC_GRAM:MC_GRAM + 512], ALU.mult).then_inc(gram_d.sem, 1)
                dve.wait_ge(sc_p.sem, sc_p.at(t))
                for o in range(2):
                    dmask = c[:, MC_D + 256 * o:MC_D + 256 * o + 256].rearrange("p (h t) -> p h t", h=2)
                    tt(scT[:, o::2], B[6 + o][:, 0:256].rearrange("p (h t) -> p h t", h=2), dmask, ALU.mult).then_inc(sc_d.sem, 1)
                if not sample:
                    dve.wait_ge(exp_a.sem, exp_a.at(t))
                    dve.wait_ge(state_d.sem, state_d.at(t, 0))
                    for o in range(2):
                        r = slice(64 * o, 64 * o + 64)
                        decay = em[u][r, :, 0].unsqueeze(2).broadcast_to([64, 4, NA])
                        tt(S0[r, :, o], S[r], decay, ALU.mult).then_inc(s0_d.sem, 1)
                for g in range(2):
                    dve.wait_ge(l0_p.sem, l0_p.at(t, g + 1))
                    m0 = c[:, MC_M0:MC_M0 + P].unsqueeze(1).broadcast_to([P, 4, P])
                    tt(M[g][:], B[2 + g][:].rearrange("p (h t) -> p h t", t=P), m0, ALU.mult).then_inc(m0_d.sem, 1)
                    dve.wait_ge(m0_d.sem, m0_d.at(t, 2 * g + 1))
                    tt(M[g][:], M[g][:], ident[:].unsqueeze(1).broadcast_to([P, 4, P]), ALU.add).then_inc(m0_d.sem, 1)

            def level(t, j, last=LEVELS - 1):
                for g in range(2):
                    n = 2 * (j - 1) + g + 1
                    if j < last:
                        dve.wait_ge(m_p.sem, m_p.at(t, n))
                        tt(M[g][:], B[4 + g][:].rearrange("p (h t) -> p h t", t=P), M[g][:], ALU.add).then_inc(m_d.sem, 1)
                    dve.wait_ge(mt_p.sem, mt_p.at(t, n))
                    tt(MT[g][:], B[6 + g][:].rearrange("p (h t) -> p h t", t=P), MT[g][:], ALU.add).then_inc(mt_d.sem, 1)

            def moments(s, t, off, n, width, bank, dst, sqv, sq_step):
                dve.wait_ge(bank[0].sem, bank[0].at(t))
                src = heads(bank[1][:], n)
                nc.vector.tensor_reduce(mean[:, off:off + n], src, AX, ALU.add).then_inc(s.sem, 1)
                dve.wait_ge(s.sem, s.at(t, 1))
                ts(mean[:, off:off + n], mean[:, off:off + n], 1.0 / width, None, ALU.mult).then_inc(s.sem, 1)
                dve.wait_ge(s.sem, s.at(t, 2))
                tt(dst, src, over(mean[:, off:off + n], width), ALU.subtract).then_inc(s.sem, 1)

            def variance(s, t, off, n, width, sqv, sq_step, eps):
                dve.wait_ge(sq_a.sem, sq_a.at(t, sq_step))
                nc.vector.tensor_reduce(var[:, off:off + n], heads(sqv[:], n), AX, ALU.add).then_inc(s.sem, 1)
                dve.wait_ge(s.sem, s.at(t, 4))
                ts(var[:, off:off + n], var[:, off:off + n], 1.0 / width, eps, ALU.mult, ALU.add).then_inc(s.sem, 1)

            def tail(t, u, c, sample):
                yA, yB = y[:, 0:8], y[:, 8:16].rearrange("p (h a) d -> p h (a d)", a=2)
                moments(yb_d, t, HA, HB, NV, (o_p, B[6]), yB, sq, 1)
                if not sample:
                    dve.wait_ge(dr_p.sem, dr_p.at(t))
                    for h in range(HB):
                        q, r = h // 2, slice(64 * (h % 2), 64 * (h % 2) + 64)
                        stt(R[r, q, h % 2], R[r, q, h % 2], c[r, MC_CDEC + q:MC_CDEC + q + 1], B[7][r, q * NV:(q + 1) * NV], ALU.mult, ALU.add).then_inc(state_d.sem, 1)
                variance(yb_d, t, HA, HB, NV, sq, 1, GN_EPS_B)
                if not sample:
                    dve.wait_ge(ds_p.sem, ds_p.at(t))
                    for o in range(2):
                        r = slice(64 * o, 64 * o + 64)
                        tt(S[r], B[5][r, 0:256].rearrange("p (q d) -> p q d", q=4), S0[r, :, o], ALU.add).then_inc(state_d.sem, 1)
                    dve.wait_ge(state_d.sem, state_d.at(t, 6))
                    tt(S[:], S[:], over(em[u][:, :, 1], NA), ALU.mult).then_inc(state_d.sem, 1)
                moments(ya_d, t, 0, HA, NA, (y_p, B[4]), yA, t2, 2)
                dve.wait_ge(rs_g.sem, rs_g.at(t, 1))
                tt(yB, yB, over(rs[:, HA:HA + HB], NV), ALU.mult).then_inc(yb_d.sem, 1)
                dve.wait_ge(yb_d.sem, yb_d.at(t, 6))
                flatB, flatA = y[:, 8:16].rearrange("p h d -> p (h d)"), y[:, 0:8].rearrange("p h d -> p (h d)")
                tt(flatB, flatB, v("ret_gn_g"), ALU.mult).then_inc(yb_d.sem, 1)
                variance(ya_d, t, 0, HA, NA, t2, 2, GN_EPS_A)
                dve.wait_ge(yb_d.sem, yb_d.at(t, 7))
                tt(flatB, flatB, v("ret_gn_b"), ALU.add).then_inc(yb_d.sem, 1)
                dve.wait_ge(bonus_d.sem, bonus_d.at(t if sample else t + 1))
                tt(heads(t1[:], HA), heads(sh[u][:, 2 * WA:3 * WA], HA), over(bonus[u][:], NA), ALU.mult).then_inc(ya_d.sem, 1)
                dve.wait_ge(sil_g.sem, sil_g.at(t))
                dve.wait_ge(yb_d.sem, yb_d.at(t, 8))
                stt(flatB, flatB, 0.5, sg[:], ALU.mult, ALU.mult).then_inc(yb_d.sem, 1)
                dve.wait_ge(rs_g.sem, rs_g.at(t, 2))
                tt(yA, yA, over(rs[:, 0:HA], NA), ALU.mult).then_inc(ya_d.sem, 1)
                dve.wait_ge(ya_d.sem, ya_d.at(t, 7))
                tt(flatA, flatA, v("lnx_g"), ALU.mult).then_inc(ya_d.sem, 1)
                dve.wait_ge(ya_d.sem, ya_d.at(t, 8))
                tt(flatA, flatA, v("lnx_b"), ALU.add).then_inc(ya_d.sem, 1)
                dve.wait_ge(ya_d.sem, ya_d.at(t, 9))
                tt(flatA, flatA, t1[:], ALU.add).then_inc(ya_d.sem, 1)
                dve.wait_ge(gate_a.sem, gate_a.at(t))
                dve.wait_ge(ya_d.sem, ya_d.at(t, 10))
                tt(flatA, flatA, gate[u][:], ALU.mult).then_inc(ya_d.sem, 1)

            def sampled_states(t, u, c):
                blk = c[0:TS, MC_BLK:MC_BLK + DB]
                dve.wait_ge(u_a.sem, u_a.at(t))
                dve.wait_ge(exp_a.sem, exp_a.at(t))
                for j in range(8):
                    if j >= 1:
                        dve.wait_ge(new_p.sem, j)
                    for o in range(2):
                        if j < 4:
                            h = 2 * j + o
                            for dst, src in ((X[o], usb[0:TS, h]), (ET[o], sh[u][0:TS, 2 * WA + h * NA:2 * WA + (h + 1) * NA])):
                                out = dst[0:TS].rearrange("p a (c d) -> p (a c) d", d=NA)
                                m = tt(out, src.unsqueeze(1).broadcast_to([TS, DB, NA]), blk.unsqueeze(2).broadcast_to([TS, DB, NA]), ALU.mult)
                        else:
                            h, half = 2 * (j % 2) + o, (j - 4) // 2
                            src = curB[u][0:TS, 512 + h * NV:512 + (h + 1) * NV].unsqueeze(1).broadcast_to([TS, 4, NV])
                            m = tt(X[o][0:TS], src, blk[:, 4 * half:4 * half + 4].unsqueeze(2).broadcast_to([TS, 4, NV]), ALU.mult)
                    m.then_inc(blk_d.sem, 1)
                    dve.wait_ge(new_p.sem, j + 1)
                    bank = B[5] if j % 2 == 0 else B[0]
                    if j < 4:
                        st = s0T[:, :, j]
                        tt(st, bank[:].rearrange("p (b d) -> p b d", b=DB), st, ALU.add).then_inc(sum_d.sem, 1)
                        dve.wait_ge(sum_d.sem, j + 1)
                        tt(st, st, over(em[u][:, j], NA), ALU.mult).then_inc(new_d.sem, 1)
                    else:
                        q, half = j % 2, (j - 4) // 2
                        st = r0[:, 4 * half:4 * half + 4, q]
                        stt(st, st, c[:, MC_CDEC + q:MC_CDEC + q + 1], bank[:].rearrange("p (b d) -> p b d", b=4), ALU.mult, ALU.add).then_inc(new_d.sem, 1)

            def start():
                nc.vector.memset(S[:], 0.0).then_inc(s_zero.sem, 1)
                nc.vector.memset(R[:], 0.0).then_inc(s_zero.sem, 1)
                nc.vector.memset(S0[:], 0.0).then_inc(s_zero.sem, 1)
                dve.wait_ge(s_zero.sem, 3)
                dve.wait_ge(const_in.sem, 16 * NCONST)
                f_mix(0, 0, 0)
                f_lora(0, 0)
                f_kk1(0, 0)
                f_z(0)
                f_lwa(0)
                f_kk2(0, 0)
                f_rot(0, 0, 0)
                f_scale(0, 0)

            def body(t, u, i):
                grams(t, u, mc, False)
                f_mix(t + 1, 1 - u, i + u)
                level(t, 1)
                f_lora(t + 1, 1 - u)
                level(t, 2)
                f_kk1(t + 1, 1 - u)
                level(t, 3)
                f_z(t + 1)
                level(t, 4)
                f_lwa(t + 1)
                f_kk2(t + 1, 1 - u)
                level(t, 5)
                f_rot(t + 1, 1 - u, i + u)
                level(t, 6)
                f_scale(t + 1, 1 - u)
                tail(t, u, mc, False)

            def end():
                grams(NT, 0, mcs, True)
                level(NT, 1, LEVELS_S - 1)
                level(NT, 2, LEVELS_S - 1)
                tail(NT, 0, mcs, True)
                sampled_states(NT, 0, mcs)

            tiles(dve, start, body, end)

        @block.gpsimd
        def _(pool):
            tt = nc.gpsimd.tensor_tensor

            def f_rn(t):
                pool.wait_ge(kk_d.sem, kk_d.at(t, 3))
                tt(rn[:], ss[:], halves[:, 0:HA], ALU.pow).then_inc(rn_g.sem, 1)

            def first(t, c):
                m0 = c[:, MC_LVL:MC_LVL + P].unsqueeze(1).broadcast_to([P, 4, P])
                for g in range(2):
                    pool.wait_ge(gram_d.sem, gram_d.at(t, 4 * g + 4))
                    tt(MT[g][:], G[:, 4 * g:4 * g + 4, 0], m0, ALU.mult).then_inc(mt0_g.sem, 1)
                    pool.wait_ge(mt0_g.sem, mt0_g.at(t, 2 * g + 1))
                    tt(MT[g][:], MT[g][:], ident[:].unsqueeze(1).broadcast_to([P, 4, P]), ALU.add).then_inc(mt0_g.sem, 1)

            def level(t, j, c):
                m = c[:, MC_LVL + j * P:MC_LVL + (j + 1) * P].unsqueeze(1).broadcast_to([P, 4, P])
                for g in range(2):
                    n = 2 * (j - 1) + g + 1
                    if j > 1:
                        pool.wait_ge(x_p.sem, x_p.at(t, n - 2))
                    tt(ET[g][:], G[:, 4 * g:4 * g + 4, 0], m, ALU.mult).then_inc(et_g.sem, 1)

            def tail(t, u):
                pool.wait_ge(sil_a.sem, sil_a.at(t))
                tt(sg[:], sg[:], one[:].broadcast_to([P, WA]), ALU.add).then_inc(sil1_g.sem, 1)
                pool.wait_ge(sil1_g.sem, sil1_g.at(t))
                tt(sg[:], sg[:], curB[u][:, 1024:1536], ALU.mult).then_inc(sil_g.sem, 1)
                pool.wait_ge(yb_d.sem, yb_d.at(t, 5))
                tt(rs[:, HA:], var[:, HA:], halves[:, 0:HB], ALU.pow).then_inc(rs_g.sem, 1)
                pool.wait_ge(ya_d.sem, ya_d.at(t, 5))
                tt(rs[:, 0:HA], var[:, 0:HA], halves[:, 0:HA], ALU.pow).then_inc(rs_g.sem, 1)

            def start():
                nc.gpsimd.memset(halves[:], -0.5).then_inc(half_set.sem, 1)
                nc.gpsimd.memset(one[:], 1.0).then_inc(half_set.sem, 1)
                pool.wait_ge(half_set.sem, 2)
                pool.wait_ge(const_in.sem, 16 * NCONST)
                f_rn(0)

            def body(t, u, i):
                first(t, mc)
                level(t, 1, mc)
                level(t, 2, mc)
                level(t, 3, mc)
                f_rn(t + 1)
                level(t, 4, mc)
                level(t, 5, mc)
                level(t, 6, mc)
                tail(t, u)

            def end():
                first(NT, mcs)
                level(NT, 1, mcs)
                level(NT, 2, mcs)
                tail(NT, 0)

            tiles(pool, start, body, end)

        ex.close()



def normalize(dve, s, t, base, x, stats, mv, rs, rs_done, out, g, b):
    for half in range(2):
        dve.bn_stats(stats[:, 6 * half:6 * half + 6], x[:, 512 * half:512 * half + 512]).then_inc(s.sem, 1)
    dve.wait_ge(s.sem, s.at(t, base + 2))
    dve.memset(mv[:, 3:4], 0.0)
    dve.bn_aggr(mv[:, 0:2], stats[:]).then_inc(s.sem, 1)
    dve.wait_ge(s.sem, s.at(t, base + 3))
    dve.tensor_scalar(mv[:, 2:3], mv[:, 1:2], LN_EPS, None, ALU.add).then_inc(s.sem, 1)
    dve.wait_ge(rs_done.sem, rs_done.at(t, 1))
    dve.tensor_scalar(out, x, mv[:, 0:1], rs, ALU.subtract, ALU.mult).then_inc(s.sem, 1)
    dve.wait_ge(s.sem, s.at(t, base + 5))
    dve.tensor_tensor(out, out, g, ALU.mult).then_inc(s.sem, 1)
    dve.wait_ge(s.sem, s.at(t, base + 6))
    dve.tensor_tensor(out, out, b, ALU.add).then_inc(s.sem, 1)


def merge(nc, x_rows, shift_p, shift_s, yT_d, w_out, w_router, vec2, ident_d, h_rows, logits):
    with ExitStack() as ctx:
        def sb(name, shape):
            return ctx.enter_context(nc.sbuf_tensor("mg_" + name, shape, F32))

        def two(name, shape):
            return [sb(f"{name}{u}", shape) for u in range(2)]

        def sig(name, per, by=1):
            return Signal(nc, ctx, "mg_" + name, per, by)

        wo = sb("wo", [P, KD, D])
        wr = sb("wr", [P, KD, NG + NE])
        gb = sb("gb", [P, 2 * D + NG + NE])
        ident = sb("ident", [P, P])
        yT, x, h, hs = two("yT", [P, KD, P]), two("x", [P, D]), two("h", [P, D]), two("hs", [P, KD, P])
        stats, mv, rs = sb("stats", [P, 12]), sb("mv", [P, 4]), sb("rs", [P, 1])
        halves = sb("halves", [P, 1])
        B = [ctx.enter_context(nc.psum_tensor(f"mg_ps{b}", [P, 512], F32)) for b in range(8)]

        half_set = sig("half_set", 1)
        shift_out = sig("shift_out", 2, 16)
        const_in = sig("const_in", 5, 16)
        yT_in = [sig(f"yT_in{u}", 1, 16) for u in range(2)]
        x_in = [sig(f"x_in{u}", 1, 16) for u in range(2)]
        mix_p = sig("mix_p", 2)
        h_d = sig("h_d", 9)
        rs_g = sig("rs_g", 1)
        turn_p = sig("turn_p", 2)
        rows_a = sig("rows_a", 1)
        turn_a = sig("turn_a", 2)
        router_p = sig("router_p", 1)
        logit_d = sig("logit_d", 1)

        with nc.Block() as block:

            def loop(eng, f, last=None):
                with eng.Fori(0, NT // 2) as i:
                    f(2 * i, 0, i)
                    f(2 * i + 1, 1, i)
                f(NT, 0, NT // 2)

            @block.sync
            def _(sp):
                for dst, src in ((gb, vec2.broadcast_to([P, 2 * D + NG + NE])), (ident, ident_d), (wr, w_router)):
                    sp.dma_start(dst[:], src).then_inc(const_in.sem, 16)
                for half in range(2):
                    sp.dma_start(wo[:, :, 512 * half:512 * half + 512], w_out[:, :, 512 * half:512 * half + 512]).then_inc(const_in.sem, 16)

                sp.dma_start(shift_p, x_rows[SEQ:SEQ + 1]).then_inc(shift_out.sem, 16)
                last = x_rows[SAMPLE0:SAMPLE0 + DB * (DS + 1)].rearrange("(b t) c -> b t c", b=DB)[:, DS]
                sp.dma_start(shift_s, last).then_inc(shift_out.sem, 16)
                sp.wait_ge(shift_out.sem, 32)

            @block.gpsimd
            def _(pool):
                nc.gpsimd.memset(halves[:], -0.5).then_inc(half_set.sem, 1)
                pool.wait_ge(half_set.sem, 1)

                def load(t, u):
                    if isinstance(t, int) and t == NT:
                        pool.dma_start(x[u][0:TS], x_rows[SAMPLE0:SAMPLE0 + DB * (DS + 1)].rearrange("(b t) c -> b t c", b=DB)[:, 1:]).then_inc(x_in[u].sem, 16)
                    else:
                        pool.dma_start(x[u][:], x_rows[1:1 + SEQ].rearrange("(n p) c -> n p c", p=P)[t]).then_inc(x_in[u].sem, 16)
                    pool.dma_start(yT[u][:], yT_d[t]).then_inc(yT_in[u].sem, 16)

                def power(t):
                    pool.wait_ge(h_d.sem, h_d.at(t, 6))
                    nc.gpsimd.tensor_tensor(rs[:], mv[:, 2:3], halves[:], ALU.pow).then_inc(rs_g.sem, 1)

                load(0, 0)
                load(1, 1)
                with pool.Fori(0, NT // 2 - 1) as i:
                    for u in range(2):
                        power(2 * i + u)
                        load(2 * i + u + 2, u)
                power(NT - 2)
                load(NT, 0)
                power(NT - 1)
                power(NT)

            @block.tensor
            def _(pe):
                pe.wait_ge(const_in.sem, const_in.at(1, 0))

                def mix(t, u, i):
                    pe.wait_ge(yT_in[u].sem, (i + 1) * 16)
                    for half in range(2):
                        for k in range(KD):
                            m = nc.tensor.matmul(B[2 * u + half][:], yT[u][:, k], wo[:, k, 512 * half:512 * half + 512], start=(k == 0), stop=(k == KD - 1))
                        m.then_inc(mix_p.sem, 1)

                def turn(t, u):
                    pe.wait_ge(h_d.sem, h_d.at(t))
                    for half in range(2):
                        pe.wait_ge(turn_a.sem, turn_a.at(t, 0))
                        for q in range(4):
                            k = 4 * half + q
                            m = nc.tensor.transpose(B[4 + half][:, q * P:(q + 1) * P], h[u][:, k * P:(k + 1) * P], ident[:])
                        m.then_inc(turn_p.sem, 1)

                def router(t, u):
                    pe.wait_ge(turn_a.sem, turn_a.at(t))
                    pe.wait_ge(logit_d.sem, logit_d.at(t, 0))
                    for k in range(KD):
                        m = nc.tensor.matmul(B[6][:, 0:NG + NE], hs[u][:, k], wr[:, k], start=(k == 0), stop=(k == KD - 1))
                    m.then_inc(router_p.sem, 1)

                mix(0, 0, 0)
                with pe.Fori(0, NT // 2) as i:
                    mix(2 * i + 1, 1, i)
                    turn(2 * i, 0)
                    router(2 * i, 0)
                    mix(2 * i + 2, 0, i + 1)
                    turn(2 * i + 1, 1)
                    router(2 * i + 1, 1)
                turn(NT, 0)
                router(NT, 0)

            @block.scalar
            def _(act):
                def tile(t, u, i):
                    act.wait_ge(h_d.sem, h_d.at(t))
                    nc.scalar.copy(h_rows[:, t], h[u][:]).then_inc(rows_a.sem, 1)
                    act.wait_ge(router_p.sem, router_p.at(t, 0))
                    for half in range(2):
                        act.wait_ge(turn_p.sem, turn_p.at(t, half + 1))
                        nc.scalar.copy(hs[u][:, 4 * half:4 * half + 4], B[4 + half][:].rearrange("p (k t) -> p k t", t=P)).then_inc(turn_a.sem, 1)
                loop(act, tile)

            @block.vector
            def _(dve):
                dve.wait_ge(const_in.sem, const_in.at(1, 0))

                def tile(t, u, i):
                    dve.wait_ge(x_in[u].sem, (i + 1) * 16)
                    dve.wait_ge(turn_a.sem, turn_a.at(t, 0))
                    for half in range(2):
                        c = slice(512 * half, 512 * half + 512)
                        dve.wait_ge(mix_p.sem, mix_p.at(t, half + 1))
                        nc.vector.scalar_tensor_tensor(h[u][:, c], x[u][:, c], ALPHA, B[2 * u + half][:], ALU.mult, ALU.add).then_inc(h_d.sem, 1)
                    dve.wait_ge(h_d.sem, h_d.at(t, 2))
                    normalize(nc.vector, h_d, t, 2, h[u][:], stats, mv, rs[:], rs_g, h[u][:], gb[:, 0:D], gb[:, D:2 * D])
                    dve.wait_ge(router_p.sem, router_p.at(t))
                    nc.vector.tensor_tensor(logits[:, t], B[6][:, 0:NG + NE], gb[:, 2 * D:], ALU.add).then_inc(logit_d.sem, 1)
                loop(dve, tile)



def route(nc, logits, h_rows, rconst, slot_u, weight, tile_expert, sorted_h):
    n = TILES
    with ExitStack() as ctx:
        def sb(name, shape, dt=F32):
            return ctx.enter_context(nc.sbuf_tensor("rt_" + name, shape, dt))

        rc = sb("rc", [P, RC_N])
        ones = sb("ones", [P, P])
        cmax, z, gp, pm, v1, v2, e, w1 = (sb(x, [P, n]) for x in ("cmax", "z", "gp", "pm", "v1", "v2", "e", "w1"))
        c, ex, pr, oh, f4, oh1, oh2, d = (sb(x, [P, n, 4]) for x in ("c", "ex", "pr", "oh", "f4", "oh1", "oh2", "d"))
        prod = sb("prod", [P, n, 4, 4])
        E = sb("E", [P, 2, n, NG, EPG])
        O = sb("O", [P, n, NE])
        pre = sb("pre", [P, n + 1, NE])
        slot = sb("slot", [P, n, NE])
        hit = sb("hit", [P, n, NE])
        slot_f = sb("slot_f", [P, 2, n])
        cmp = sb("cmp", [P, NE, n])
        ntl, tb, tend = sb("ntl", [P, NE]), sb("tb", [P, NE]), sb("tend", [P, NE])
        tri16 = sb("tri16", [P, NE, NE])
        cmp2 = sb("cmp2", [P, SLOTS // P, NE])
        te = sb("te", [P, SLOTS // P])
        ps = [ctx.enter_context(nc.psum_tensor(f"rt_ps{b}", [P, 512], F32)) for b in range(2)]
        const_in = Signal(nc, ctx, "rt_const_in", 1, 16)
        step = Signal(nc, ctx, "rt_step", 1)
        exp_a = Signal(nc, ctx, "rt_exp_a", 1)
        count_p = Signal(nc, ctx, "rt_count_p", 1)
        slots_d = Signal(nc, ctx, "rt_slots_d", 1)
        scattered = Signal(nc, ctx, "rt_scattered", 2 * n, 16)
        prio = rc[:, RC_PRIO:RC_PRIO + 4]

        def over(x):
            return x.unsqueeze(2).broadcast_to([P, n, 4])

        with nc.Block() as block:

            @block.sync
            def _(sp):
                sp.dma_start(rc[:], rconst).then_inc(const_in.sem, 16)

            @block.scalar
            def _(act):
                act.wait_ge(step.sem, C_READY)
                nc.scalar.activation(ex[:], c[:], ACT.Exp).then_inc(exp_a.sem, 1)
                act.wait_ge(step.sem, V2_READY)
                nc.scalar.activation(e[:], v2[:], ACT.Exp).then_inc(exp_a.sem, 1)

            @block.tensor
            def _(pe):
                pe.wait_ge(step.sem, O_READY)
                rows = O[:].rearrange("p n e -> p (n e)")
                nc.tensor.matmul(ps[0][:, 0:n * NE], rc[:, RC_TRI:RC_TRI + P], rows, start=True, stop=True).then_inc(count_p.sem, 1)
                nc.tensor.matmul(ps[1][:, 0:n * NE], ones[:], rows, start=True, stop=True).then_inc(count_p.sem, 1)

            @block.gpsimd
            def _(pool):
                pool.wait_ge(slots_d.sem, 1)
                for t in range(n):
                    rows = P if t < NT else TS
                    for k in range(2):
                        where = bass.IndirectOffsetOnAxis(ap=slot_u[0:rows, k, t:t + 1], axis=0)
                        pool.indirect_dma_start(out=sorted_h, out_offset=where, in_=h_rows[0:rows, t], in_offset=None).then_inc(scattered.sem, 16)
                pool.wait_ge(scattered.sem, scattered.at(1, 0))

            @block.vector
            def _(dve):
                tt, ts, red = nc.vector.tensor_tensor, nc.vector.tensor_scalar, nc.vector.tensor_reduce
                done = [0]

                def then(ins):
                    done[0] += 1
                    ins.then_inc(step.sem, 1)
                    dve.wait_ge(step.sem, done[0])

                def first_max(out, x, floor):
                    then(tt(pr[:], x, floor, ALU.is_ge))
                    then(tt(pr[:], pr[:], prio.unsqueeze(1).broadcast_to([P, n, 4]), ALU.mult))
                    then(red(pm[:], pr[:], AX, ALU.max))
                    then(tt(out, pr[:], over(pm[:]), ALU.is_equal))

                dve.wait_ge(const_in.sem, 16)
                coarse = logits[:, :, 0:NG]
                fine = logits[:, :, NG:].rearrange("p n (g j) -> p n g j", g=NG)
                then(red(cmax[:], coarse, AX, ALU.max))
                then(tt(c[:], coarse, over(cmax[:]), ALU.subtract))
                assert done[0] == C_READY
                first_max(oh[:], coarse, over(cmax[:]))
                then(tt(prod[:], fine, oh[:].unsqueeze(3).broadcast_to([P, n, 4, 4]), ALU.mult))
                then(red(f4[:], prod[:].rearrange("p n g j -> p n j g"), AX, ALU.add))
                then(red(v1[:], f4[:], AX, ALU.max))
                first_max(oh1[:], f4[:], over(v1[:]))
                then(tt(d[:], f4[:], over(v1[:]), ALU.subtract))
                then(nc.vector.scalar_tensor_tensor(d[:], oh1[:], -3e38, d[:], ALU.mult, ALU.add))
                then(red(v2[:], d[:], AX, ALU.max))
                assert done[0] == V2_READY
                first_max(oh2[:], d[:], over(v2[:]))
                for k, o in enumerate((oh1, oh2)):
                    then(tt(E[:, k], oh[:].unsqueeze(3).broadcast_to([P, n, 4, 4]), o[:].unsqueeze(2).broadcast_to([P, n, 4, 4]), ALU.mult))
                flat = [E[:, k].rearrange("p n g j -> p n (g j)") for k in range(2)]
                then(tt(O[:], flat[0], flat[1], ALU.add))
                then(tt(O[:], O[:], rc[:, RC_VALID:RC_VALID + n].unsqueeze(2).broadcast_to([P, n, NE]), ALU.mult))
                then(nc.vector.memset(ones[:], 1.0))
                assert done[0] == O_READY
                then(nc.vector.memset(pre[:, 0], 0.0))
                dve.wait_ge(count_p.sem, 2)
                for t in range(n):
                    then(tt(pre[:, t + 1], ps[1][:, t * NE:(t + 1) * NE], pre[:, t], ALU.add))
                thr = rc[:, RC_THR:RC_THR + n].unsqueeze(1).broadcast_to([P, NE, n])
                then(tt(cmp[:], pre[:, n].unsqueeze(2).broadcast_to([P, NE, n]), thr, ALU.is_gt))
                then(red(ntl[:], cmp[:], AX, ALU.add))
                before = rc[:, RC_LT:RC_LT + NE * NE].rearrange("p (a b) -> p a b", a=NE)
                then(tt(tri16[:], before, ntl[:].unsqueeze(1).broadcast_to([P, NE, NE]), ALU.mult))
                then(red(tb[:], tri16[:], AX, ALU.add))
                then(tt(tend[:], tb[:], ntl[:], ALU.add))
                then(ts(tb[:], tb[:], float(P), None, ALU.mult))
                then(tt(slot[:], ps[0][:, 0:n * NE].rearrange("p (n e) -> p n e", n=n), pre[:, 0:n], ALU.add))
                then(tt(slot[:], slot[:], tb[:].unsqueeze(1).broadcast_to([P, n, NE]), ALU.add))
                for k in range(2):
                    then(tt(hit[:], slot[:], flat[k], ALU.mult))
                    then(red(slot_f[:, k], hit[:], AX, ALU.add))
                then(nc.vector.tensor_copy(slot_u[:], slot_f[:]))
                nc.vector.nop().then_inc(slots_d.sem, 1)
                tiles_at = rc[:, RC_TILE:RC_TILE + SLOTS // P].unsqueeze(2).broadcast_to([P, SLOTS // P, NE])
                then(tt(cmp2[:], tiles_at, tend[:].unsqueeze(1).broadcast_to([P, SLOTS // P, NE]), ALU.is_ge))
                then(red(te[:], cmp2[:], AX, ALU.add))
                then(ts(te[:], te[:], float(NE - 1), None, ALU.min))
                then(nc.vector.tensor_copy(tile_expert[:], te[:]))
                dve.wait_ge(exp_a.sem, 2)
                then(red(z[:], ex[:], AX, ALU.add))
                then(nc.vector.reciprocal(gp[:], z[:]))
                then(ts(w1[:], e[:], 1.0, None, ALU.add))
                then(nc.vector.reciprocal(w1[:], w1[:]))
                then(nc.vector.scalar_tensor_tensor(weight[:, 0], w1[:], 0.5, gp[:], ALU.mult, ALU.mult))
                then(tt(weight[:, 1], e[:], weight[:, 0], ALU.mult))


def experts(nc, w13_d, w2_d, ident_d, tile_expert, sorted_h, sorted_y):
    NJ = SLOTS // P
    NF = FE // P
    sh, sy = (x.rearrange("(j p) d -> j p d", p=P) for x in (sorted_h, sorted_y))
    with ExitStack() as ctx:
        def two(name, shape):
            return [ctx.enter_context(nc.sbuf_tensor(f"ex_{name}{u}", shape, F32)) for u in range(2)]

        def sig(name, per, by=1):
            return Signal(nc, ctx, "ex_" + name, per, by)

        w13, w2 = two("w13", [P, KD, 2 * FE]), two("w2", [P, NF, D])
        x, xT, th, hid, hidT, y = (two("x", [P, D]), two("xT", [P, KD, P]), two("th", [P, FE]), two("hid", [P, FE]),
                                   two("hidT", [P, NF, P]), two("y", [P, D]))
        ident = ctx.enter_context(nc.sbuf_tensor("ex_ident", [P, P], F32))
        B = [ctx.enter_context(nc.psum_tensor(f"ex_ps{b}", [P, 512], F32)) for b in range(7)]
        ident_in = sig("ident_in", 1, 16)
        w13_in = [sig(f"w13_in{u}", 1, 16) for u in range(2)]
        w2_in = [sig(f"w2_in{u}", 1, 16) for u in range(2)]
        x_in = [sig(f"x_in{u}", 1, 16) for u in range(2)]
        y_out = [sig(f"y_out{u}", 1, 16) for u in range(2)]
        turn_p = sig("turn_p", 2)
        turn_a = sig("turn_a", 2)
        up_p = sig("up_p", 1)
        th_a = sig("th_a", 1)
        hid_d = sig("hid_d", 2)
        hidT_p = sig("hidT_p", 1)
        hidT_a = sig("hidT_a", 1)
        down_p = sig("down_p", 2)
        y_a = sig("y_a", 1)
        y_d = sig("y_d", 1)

        with nc.Block() as block:

            def tiles(eng, step):
                step(0, 0, 0)
                with eng.Fori(0, NJ // 2 - 1) as i:
                    step(2 * i + 1, 1, i)
                    step(2 * i + 2, 0, i + 1)
                step(NJ - 1, 1, NJ // 2 - 1)

            @block.sync
            def _(sp):
                def expert_of(j):
                    row = tile_expert[0:1, j:j + 1] if isinstance(j, int) else tile_expert[0:1, bass.ds(j, 1)]
                    return sp.value_load(row, min_val=0, max_val=NE - 1)

                def load13(expert, u):
                    sp.dma_start(w13[u][:], w13_d[expert]).then_inc(w13_in[u].sem, 16)

                def load2(expert, u):
                    sp.dma_start(w2[u][:], w2_d[expert]).then_inc(w2_in[u].sem, 16)

                for u in range(2):
                    expert = expert_of(u)
                    load13(expert, u)
                    load2(expert, u)
                with sp.Fori(0, NJ // 2 - 1) as i:
                    for u in range(2):
                        expert = expert_of(2 * i + u + 2)
                        sp.wait_ge(up_p.sem, up_p.at(2 * i + u))
                        load13(expert, u)
                        sp.wait_ge(down_p.sem, down_p.at(2 * i + u))
                        load2(expert, u)

            @block.gpsimd
            def _(pool):
                def load(j, u):
                    pool.dma_start(x[u][:], sh[j]).then_inc(x_in[u].sem, 16)

                def store(j, u):
                    pool.wait_ge(y_a.sem, y_a.at(j))
                    pool.wait_ge(y_d.sem, y_d.at(j))
                    pool.dma_start(sy[j], y[u][:]).then_inc(y_out[u].sem, 16)

                pool.dma_start(ident[:], ident_d).then_inc(ident_in.sem, 16)
                load(0, 0)
                load(1, 1)
                with pool.Fori(0, NJ // 2 - 1) as i:
                    for u in range(2):
                        pool.wait_ge(turn_p.sem, turn_p.at(2 * i + u))
                        load(2 * i + u + 2, u)
                        store(2 * i + u, u)
                store(NJ - 2, 0)
                store(NJ - 1, 1)
                for u in range(2):
                    pool.wait_ge(y_out[u].sem, 16 * (NJ // 2))

            @block.tensor
            def _(pe):
                mm = nc.tensor.matmul

                def turn(j, u, i):
                    pe.wait_ge(x_in[u].sem, (i + 1) * 16)
                    for half in range(2):
                        if not (isinstance(j, int) and j == 0):
                            pe.wait_ge(turn_a.sem, turn_a.at(j - 1, half + 1))
                        for q in range(4):
                            k = 4 * half + q
                            m = nc.tensor.transpose(B[2 + half][:, q * P:(q + 1) * P], x[u][:, k * P:(k + 1) * P], ident[:])
                        m.then_inc(turn_p.sem, 1)

                def up(j, u, i):
                    pe.wait_ge(w13_in[u].sem, (i + 1) * 16)
                    pe.wait_ge(turn_a.sem, turn_a.at(j))
                    for k in range(KD):
                        m = mm(B[u][:], xT[u][:, k], w13[u][:, k], start=(k == 0), stop=(k == KD - 1))
                    m.then_inc(up_p.sem, 1)

                def down(j, u, i):
                    pe.wait_ge(w2_in[u].sem, (i + 1) * 16)
                    pe.wait_ge(hidT_a.sem, hidT_a.at(j))
                    for half in range(2):
                        s = (y_a, y_d)[half]
                        pe.wait_ge(s.sem, s.at(j, 0))
                        for f in range(NF):
                            m = mm(B[5 + half][:], hidT[u][:, f], w2[u][:, f, 512 * half:512 * half + 512], start=(f == 0), stop=(f == NF - 1))
                        m.then_inc(down_p.sem, 1)

                def turn_hid(j, u):
                    pe.wait_ge(hid_d.sem, hid_d.at(j))
                    for f in range(NF):
                        m = nc.tensor.transpose(B[4][:, f * P:(f + 1) * P], hid[u][:, f * P:(f + 1) * P], ident[:])
                    m.then_inc(hidT_p.sem, 1)

                pe.wait_ge(ident_in.sem, 16)
                turn(0, 0, 0)
                up(0, 0, 0)
                turn(1, 1, 0)
                turn_hid(0, 0)
                with pe.Fori(0, NJ // 2 - 1) as i:
                    for u in (1, 0):
                        j = 2 * i + 2 - u
                        up(j, u, i + 1 - u)
                        turn(j + 1, 1 - u, i + 1)
                        down(j - 1, 1 - u, i)
                        turn_hid(j, u)
                up(NJ - 1, 1, NJ // 2 - 1)
                down(NJ - 2, 0, NJ // 2 - 1)
                turn_hid(NJ - 1, 1)
                down(NJ - 1, 1, NJ // 2 - 1)

            @block.scalar
            def _(act):
                def turned(j, u):
                    for half in range(2):
                        act.wait_ge(turn_p.sem, turn_p.at(j, half + 1))
                        nc.scalar.copy(xT[u][:, 4 * half:4 * half + 4], B[2 + half][:].rearrange("p (k t) -> p k t", t=P)).then_inc(turn_a.sem, 1)

                def hidden(j, u):
                    act.wait_ge(up_p.sem, up_p.at(j))
                    nc.scalar.activation(th[u][:], B[u][:, 0:FE], ACT.Tanh, scale=0.5).then_inc(th_a.sem, 1)

                def hid_turned(j, u):
                    act.wait_ge(hidT_p.sem, hidT_p.at(j))
                    nc.scalar.copy(hidT[u][:], B[4][:, 0:FE].rearrange("p (f t) -> p f t", t=P)).then_inc(hidT_a.sem, 1)

                def out(j, u, i):
                    act.wait_ge(y_out[u].sem, i * 16)
                    act.wait_ge(down_p.sem, down_p.at(j, 1))
                    nc.scalar.copy(y[u][:, 0:512], B[5][:]).then_inc(y_a.sem, 1)

                turned(0, 0)
                hidden(0, 0)
                turned(1, 1)
                hid_turned(0, 0)
                with act.Fori(0, NJ // 2 - 1) as i:
                    for u in (1, 0):
                        j = 2 * i + 2 - u
                        hidden(j, u)
                        turned(j + 1, 1 - u)
                        out(j - 1, 1 - u, i)
                        hid_turned(j, u)
                hidden(NJ - 1, 1)
                out(NJ - 2, 0, NJ // 2 - 1)
                hid_turned(NJ - 1, 1)
                out(NJ - 1, 1, NJ // 2 - 1)

            @block.vector
            def _(dve):
                def hidden(j, u):
                    dve.wait_ge(th_a.sem, th_a.at(j))
                    nc.vector.scalar_tensor_tensor(th[u][:], th[u][:], 1.0, B[u][:, 0:FE], ALU.add, ALU.mult).then_inc(hid_d.sem, 1)
                    dve.wait_ge(hid_d.sem, hid_d.at(j, 1))
                    nc.vector.tensor_tensor(hid[u][:], th[u][:], B[u][:, FE:], ALU.mult).then_inc(hid_d.sem, 1)

                def out(j, u, i):
                    dve.wait_ge(y_out[u].sem, i * 16)
                    dve.wait_ge(down_p.sem, down_p.at(j, 2))
                    nc.vector.tensor_copy(y[u][:, 512:], B[6][:]).then_inc(y_d.sem, 1)

                hidden(0, 0)
                with dve.Fori(0, NJ // 2 - 1) as i:
                    for u in (1, 0):
                        hidden(2 * i + 2 - u, u)
                        out(2 * i + 1 - u, 1 - u, i)
                hidden(NJ - 1, 1)
                out(NJ - 2, 0, NJ // 2 - 1)
                out(NJ - 1, 1, NJ // 2 - 1)


def finish(nc, h_rows, slot_u, weight, sorted_y, pT_d, w_ple, w_pgate, vec3, ident_d, out_d):
    with ExitStack() as ctx:
        def sb(name, shape):
            return ctx.enter_context(nc.sbuf_tensor("fi_" + name, shape, F32))

        def two(name, shape):
            return [sb(f"{name}{u}", shape) for u in range(2)]

        def sig(name, per, by=1):
            return Signal(nc, ctx, "fi_" + name, per, by)

        KP = D_PLE // P
        wp, wg = sb("wp", [P, KP, D]), sb("wg", [P, KD, D])
        gb = sb("gb", [P, 3 * D])
        ident = sb("ident", [P, P])
        pT, h, hs, q = two("pT", [P, KP, P]), two("h", [P, D]), two("hs", [P, KD, P]), two("q", [P, D])
        junk = sb("junk", [P, D])
        y0, y1 = two("y0", [P, D]), two("y1", [P, D])
        stats, mv, rs, rr = sb("stats", [P, 12]), sb("mv", [P, 4]), sb("rs", [P, 1]), sb("rr", [P, 1])
        ssq = two("ssq", [P, 1])
        var2 = sb("var2", [P, 1])
        halves = sb("halves", [P, 1])
        B = [ctx.enter_context(nc.psum_tensor(f"fi_ps{b}", [P, 512], F32)) for b in range(8)]
        half_set = sig("half_set", 1)
        const_in = sig("const_in", 5, 16)
        pT_in = [sig(f"pT_in{u}", 1, 16) for u in range(2)]
        y_in = [sig(f"y_in{u}", 2, 16) for u in range(2)]
        h_d = sig("h_d", 10)
        rs_g = sig("rs_g", 1)
        turn_p = sig("turn_p", 2)
        turn_a = sig("turn_a", 2)
        gate_p = sig("gate_p", 2)
        ple_p = sig("ple_p", 2)
        tanh_a = sig("tanh_a", 2)
        sq_a = sig("sq_a", 1)
        q_d = sig("q_d", 6)
        rr_g = sig("rr_g", 1)
        out_s = [sig(f"out_s{u}", 1, 16) for u in range(2)]

        with nc.Block() as block:

            @block.sync
            def _(sp):
                for dst, src in ((gb, vec3.broadcast_to([P, 3 * D])), (ident, ident_d), (wp, w_ple)):
                    sp.dma_start(dst[:], src).then_inc(const_in.sem, 16)
                for half in range(2):
                    sp.dma_start(wg[:, :, 512 * half:512 * half + 512], w_pgate[:, :, 512 * half:512 * half + 512]).then_inc(const_in.sem, 16)

                def store(t, u):
                    sp.wait_ge(q_d.sem, q_d.at(t))
                    sp.dma_start(out_d[t], q[u][:]).then_inc(out_s[u].sem, 16)
                with sp.Fori(0, NT // 2) as i:
                    store(2 * i, 0)
                    store(2 * i + 1, 1)
                store(NT, 0)
                sp.wait_ge(out_s[0].sem, 16 * (NT // 2 + 1))
                sp.wait_ge(out_s[1].sem, 16 * (NT // 2))

            @block.gpsimd
            def _(pool):
                nc.gpsimd.memset(halves[:], -0.5).then_inc(half_set.sem, 1)
                pool.wait_ge(half_set.sem, 1)

                def load(t, u):
                    rows = TS if t == NT else P
                    pool.dma_start(pT[u][:], pT_d[t]).then_inc(pT_in[u].sem, 16)
                    for k, y in enumerate((y0, y1)):
                        where = bass.IndirectOffsetOnAxis(ap=slot_u[0:rows, k, t:t + 1], axis=0)
                        pool.indirect_dma_start(out=y[u][0:rows], out_offset=None, in_=sorted_y, in_offset=where).then_inc(y_in[u].sem, 16)

                def power(t):
                    pool.wait_ge(h_d.sem, h_d.at(t, 7))
                    nc.gpsimd.tensor_tensor(rs[:], mv[:, 2:3], halves[:], ALU.pow).then_inc(rs_g.sem, 1)

                def power2(t):
                    pool.wait_ge(q_d.sem, q_d.at(t, 3))
                    nc.gpsimd.tensor_tensor(rr[:], var2[:], halves[:], ALU.pow).then_inc(rr_g.sem, 1)

                load(0, 0)
                load(1, 1)
                power(0)
                for t in range(TILES):
                    if t + 1 < TILES:
                        power(t + 1)
                    power2(t)
                    if t + 2 < TILES:
                        load(t + 2, t % 2)

            @block.tensor
            def _(pe):
                pe.wait_ge(const_in.sem, const_in.at(1, 0))

                def tile(t, u, i):
                    pe.wait_ge(h_d.sem, h_d.at(t))
                    pe.wait_ge(turn_a.sem, turn_a.at(t, 0))
                    for half in range(2):
                        for c in range(4):
                            k = 4 * half + c
                            m = nc.tensor.transpose(B[half][:, c * P:(c + 1) * P], h[u][:, k * P:(k + 1) * P], ident[:])
                        m.then_inc(turn_p.sem, 1)
                    pe.wait_ge(pT_in[u].sem, (i + 1) * 16)
                    for half in range(2):
                        pe.wait_ge(q_d.sem, q_d.at(t, 0))
                        for k in range(KP):
                            m = nc.tensor.matmul(B[4 + half][:], pT[u][:, k], wp[:, k, 512 * half:512 * half + 512], start=(k == 0), stop=(k == KP - 1))
                        m.then_inc(ple_p.sem, 1)
                    pe.wait_ge(turn_a.sem, turn_a.at(t))
                    for half in range(2):
                        for k in range(KD):
                            m = nc.tensor.matmul(B[2 + half][:], hs[u][:, k], wg[:, k, 512 * half:512 * half + 512], start=(k == 0), stop=(k == KD - 1))
                        m.then_inc(gate_p.sem, 1)
                with pe.Fori(0, NT // 2) as i:
                    tile(2 * i, 0, i)
                    tile(2 * i + 1, 1, i)
                tile(NT, 0, NT // 2)

            @block.scalar
            def _(act):
                def tile(t, u, i):
                    for half in range(2):
                        act.wait_ge(turn_p.sem, turn_p.at(t, half + 1))
                        nc.scalar.copy(hs[u][:, 4 * half:4 * half + 4], B[half][:].rearrange("p (k t) -> p k t", t=P)).then_inc(turn_a.sem, 1)
                    act.wait_ge(out_s[u].sem, i * 16)
                    for half in range(2):
                        act.wait_ge(gate_p.sem, gate_p.at(t, half + 1))
                        nc.scalar.activation(q[u][:, 512 * half:512 * half + 512], B[2 + half][:], ACT.Tanh, scale=0.5).then_inc(tanh_a.sem, 1)
                    act.wait_ge(q_d.sem, q_d.at(t, 2))
                    nc.scalar.activation(junk[:], q[u][:], ACT.Square, accum_out=ssq[u][:]).then_inc(sq_a.sem, 1)
                with act.Fori(0, NT // 2) as i:
                    tile(2 * i, 0, i)
                    tile(2 * i + 1, 1, i)
                tile(NT, 0, NT // 2)

            @block.vector
            def _(dve):
                tt, stt = nc.vector.tensor_tensor, nc.vector.scalar_tensor_tensor
                dve.wait_ge(const_in.sem, const_in.at(1, 0))

                def norm(t, u, i):
                    if not isinstance(t, int):
                        dve.wait_ge(q_d.sem, q_d.at(t - 1, 0))
                    dve.wait_ge(y_in[u].sem, (i + 1) * 32)
                    nc.vector.tensor_scalar(y0[u][:], y0[u][:], weight[:, 0, t:t + 1] if isinstance(t, int) else weight[:, 0, bass.ds(t, 1)], None, ALU.mult).then_inc(h_d.sem, 1)
                    dve.wait_ge(h_d.sem, h_d.at(t, 1))
                    stt(y0[u][:], y1[u][:], weight[:, 1, t:t + 1] if isinstance(t, int) else weight[:, 1, bass.ds(t, 1)], y0[u][:], ALU.mult, ALU.add).then_inc(h_d.sem, 1)
                    dve.wait_ge(h_d.sem, h_d.at(t, 2))
                    stt(y0[u][:], h_rows[:, t], ALPHA, y0[u][:], ALU.mult, ALU.add).then_inc(h_d.sem, 1)
                    dve.wait_ge(h_d.sem, h_d.at(t, 3))
                    normalize(nc.vector, h_d, t, 3, y0[u][:], stats, mv, rs[:], rs_g, h[u][:], gb[:, 0:D], gb[:, D:2 * D])

                def embed(t, u):
                    for half in range(2):
                        c = slice(512 * half, 512 * half + 512)
                        dve.wait_ge(tanh_a.sem, tanh_a.at(t, half + 1))
                        stt(q[u][:, c], q[u][:, c], 1.0, B[4 + half][:], ALU.add, ALU.mult).then_inc(q_d.sem, 1)
                    dve.wait_ge(sq_a.sem, sq_a.at(t))
                    nc.vector.tensor_scalar(var2[:], ssq[u][:], 0.25 / D, LN_EPS, ALU.mult, ALU.add).then_inc(q_d.sem, 1)
                    dve.wait_ge(rr_g.sem, rr_g.at(t))
                    nc.vector.tensor_scalar(q[u][:], q[u][:], rr[:], 0.5, ALU.mult, ALU.mult).then_inc(q_d.sem, 1)
                    dve.wait_ge(q_d.sem, q_d.at(t, 4))
                    tt(q[u][:], q[u][:], gb[:, 2 * D:], ALU.mult).then_inc(q_d.sem, 1)
                    dve.wait_ge(q_d.sem, q_d.at(t, 5))
                    tt(q[u][:], q[u][:], h[u][:], ALU.add).then_inc(q_d.sem, 1)

                norm(0, 0, 0)
                with dve.Fori(0, NT // 2) as i:
                    norm(2 * i + 1, 1, i)
                    embed(2 * i, 0)
                    norm(2 * i + 2, 0, i + 1)
                    embed(2 * i + 1, 1)
                embed(NT, 0)


INPUTS = ["x_all", "x_rows", "w_in", "vecs", "w_lora", "w_gate", "fconst", "mconst", "ident", "s0T", "r0", "w_out", "w_router",
          "vec2", "rconst", "w13", "w2", "pT", "w_ple", "w_pgate", "vec3"]
OUTPUTS = {"out": (TILES, P, D), "shift_p": (1, D), "shift_s": (DB, D), "wkv_p": (P, 4, NA), "ret_p": (P, 2, NV), "wkv_s": (P, DB, 4, NA), "ret_s": (P, DB, 2, NV)}


def program(nc, a, o):
    proj = nc.dram_tensor("proj", (ROWS, IN_W), F32, kind="Internal").ap()
    yT_d = nc.dram_tensor("yT_d", (TILES, P, KD, P), F32, kind="Internal").ap()
    sorted_h = nc.dram_tensor("sorted_h", (SLOTS, D), F32, kind="Internal").ap()
    sorted_y = nc.dram_tensor("sorted_y", (SLOTS, D), F32, kind="Internal").ap()
    project(nc, a["x_all"], a["w_in"], proj, sorted_h)
    mixer(nc, proj, a["vecs"], a["w_lora"], a["w_gate"], a["fconst"], a["mconst"], a["ident"], a["s0T"], a["r0"],
          yT_d, o["wkv_p"], o["ret_p"], o["wkv_s"], o["ret_s"])
    with ExitStack() as ctx:
        h_rows = ctx.enter_context(nc.sbuf_tensor("h_rows", [P, TILES, D], F32))
        logits = ctx.enter_context(nc.sbuf_tensor("logits", [P, TILES, NG + NE], F32))
        weight = ctx.enter_context(nc.sbuf_tensor("weight", [P, 2, TILES], F32))
        slot_u = ctx.enter_context(nc.sbuf_tensor("slot_u", [P, 2, TILES], U32))
        tile_expert = ctx.enter_context(nc.sbuf_tensor("tile_expert", [P, SLOTS // P], I32))
        merge(nc, a["x_rows"], o["shift_p"], o["shift_s"], yT_d, a["w_out"], a["w_router"], a["vec2"], a["ident"], h_rows, logits)
        route(nc, logits, h_rows, a["rconst"], slot_u, weight, tile_expert, sorted_h)
        experts(nc, a["w13"], a["w2"], a["ident"], tile_expert, sorted_h, sorted_y)
        finish(nc, h_rows, slot_u, weight, sorted_y, a["pT"], a["w_ple"], a["w_pgate"], a["vec3"], a["ident"], o["out"])


def layout(inputs):
    z = {n: np.asarray(a) for n, a in inputs.items()}
    out = {}
    rows = np.zeros((ROWS, D), np.float32)
    rows[1:1 + SEQ] = z["x_prompt"][0]
    tail = rows[SAMPLE0:SAMPLE0 + DB * (DS + 1)].reshape(DB, DS + 1, D)
    tail[:, 0] = z["state_shift"][0]
    tail[:, 1:] = z["x_sample"]
    out["x_rows"] = rows
    out["x_all"] = np.ascontiguousarray(rows.reshape(TILES, P, KD, P).transpose(3, 0, 2, 1))
    out["w_in"] = np.ascontiguousarray(z["w_in"][0].reshape(KD, P, NSLICE, SLICE).transpose(2, 1, 0, 3))
    out["vecs"] = np.concatenate([z[n][0].reshape(-1) for n in VEC])[None]
    out["w_lora"] = np.concatenate([z["w_decay_up"][0], z["w_aaa_up"][0]])
    out["w_gate"] = z["w_gate_up"][0]
    out["s0T"] = z["state_wkv"][0].reshape(DB, 4, 2, NA, NA).transpose(2, 4, 0, 1, 3).reshape(P, DB, 4, NA)
    out["r0"] = z["state_ret"][0].reshape(DB, 2, 2, NK, NV).transpose(2, 3, 0, 1, 4).reshape(P, DB, 2, NV)
    out["w_out"] = z["w_out"][0].reshape(KD, P, D).transpose(1, 0, 2)
    out["w_router"] = np.concatenate([z["router_coarse_w"][0], z["router_fine_w"][0]], 1).reshape(KD, P, NG + NE).transpose(1, 0, 2)
    out["vec2"] = np.concatenate([z[n][0] for n in ("ln1_g", "ln1_b", "router_coarse_b", "router_fine_b")])[None]
    out["w13"] = np.stack([z["expert_" + n][0].reshape(NE, KD, P, FE) for n in ("w1", "w3")], 3).transpose(0, 2, 1, 3, 4).reshape(NE, P, KD, 2 * FE)
    out["w2"] = z["expert_w2"][0].reshape(NE, FE // P, P, D).transpose(0, 2, 1, 3)
    p = np.zeros((ROWS, D_PLE), np.float32)
    p[:SEQ] = z["p_prompt"][0, 0]
    p[SEQ:SEQ + TS] = z["p_sample"][0].reshape(TS, D_PLE)
    out["pT"] = p.reshape(TILES, P, D_PLE // P, P).transpose(0, 3, 2, 1)
    out["w_ple"] = z["w_ple"][0].reshape(D_PLE // P, P, D).transpose(1, 0, 2)
    out["w_pgate"] = z["w_ple_gate"][0].reshape(KD, P, D).transpose(1, 0, 2)
    out["vec3"] = np.concatenate([z[n][0] for n in ("ln2_g", "ln2_b", "ple_norm_g")])[None]
    out["fconst"], out["mconst"], out["rconst"] = shape_constants()
    out["ident"] = np.eye(P, dtype=np.float32)
    return out


def kernel(**inputs):
    import concourse.bacc as bacc
    from concourse.bass_utils import run_bass_kernel_spmd as run

    laid = layout(inputs)
    nc = bacc.Bacc("TRN2", target_bir_lowering=False, num_devices=1)
    arrays, a, o = {}, {}, {}
    for name in INPUTS:
        arrays["in_" + name] = np.ascontiguousarray(laid[name])
        a[name] = nc.dram_tensor("in_" + name, arrays["in_" + name].shape, F32, kind="ExternalInput").ap()
    for name, shape in OUTPUTS.items():
        o[name] = nc.dram_tensor("out_" + name, shape, F32, kind="ExternalOutput").ap()
    program(nc, a, o)
    got = run(nc, [arrays], core_ids=[0]).results[0]
    y = np.asarray(got["out_out"]).reshape(ROWS, D)
    wkv_p = np.asarray(got["out_wkv_p"]).reshape(2, NA, 4, NA).transpose(2, 0, 3, 1).reshape(1, 1, HA, NA, NA)
    ret_p = np.asarray(got["out_ret_p"]).reshape(2, NK, 2, NV).transpose(2, 0, 1, 3).reshape(1, 1, HB, NK, NV)
    wkv_s = np.asarray(got["out_wkv_s"]).reshape(2, NA, DB, 4, NA).transpose(2, 3, 0, 4, 1).reshape(1, DB, HA, NA, NA)
    ret_s = np.asarray(got["out_ret_s"]).reshape(2, NK, DB, 2, NV).transpose(2, 3, 0, 1, 4).reshape(1, DB, HB, NK, NV)
    shift_p = np.asarray(got["out_shift_p"]).reshape(1, 1, D)
    shift_s = np.asarray(got["out_shift_s"]).reshape(1, DB, D)
    return (y[:SEQ].reshape(1, SEQ, D), y[SEQ:SEQ + TS].reshape(DB, DS, D), wkv_p, shift_p, ret_p, wkv_s, shift_s, ret_s)
```

```python
from contextlib import ExitStack

import numpy as np

import concourse.bass as bass
from concourse import mybir

F32 = mybir.dt.float32
F16 = mybir.dt.float16
U32 = mybir.dt.uint32
I32 = mybir.dt.int32
ALU = mybir.AluOpType
ACT = mybir.ActivationFunctionType
AX = mybir.AxisListType.X

P = 128
D = 1024
KD = D // P
SEQ = 1024
DB, DS = 8, 8
PAST = 8192
D_PLE = 256
HA, NA = 8, 64
WA = HA * NA
HB, NK, NV = 4, 64, 128
SHIFT_W = 3 * WA + 64 + 64 + 128
IN_W = SHIFT_W + 2 * HB * NK + 2 * HB * NV
NG, EPG = 4, 4
NE = NG * EPG
FE = 256
ALPHA = 2 ** 0.25
LN_EPS = 1e-5
GN_EPS_A = 64e-5
GN_EPS_B = 1e-5

NT = SEQ // P
TILES = NT + 1
TS = DB * DS
ROWS = TILES * P
SAMPLE0 = 1 + SEQ
LEVELS = 7
LEVELS_S = 3
SLICE = 416
NSLICE = IN_W // SLICE
W_CONST = -float(np.exp(-0.5))
FC_TI, FC_TE, FC_SEL, FC_COS, FC_SIN, FC_CROSS, FC_KDEC, FC_N = 0, 128, 256, 264, 296, 328, 332, 336
MC_GRAM, MC_D, MC_M0, MC_LVL, MC_CDEC, MC_BLK, MC_N = 0, 512, 1024, 1152, 1152 + 7 * 128, 1152 + 7 * 128 + 2, 1152 + 7 * 128 + 10
VEC = ["mu_shift", "decay_base", "aaa_base", "k_k", "k_a", "r_k", "lnx_g", "lnx_b", "ret_gn_g", "ret_gn_b"]
VEC_OFF = dict(zip(VEC, np.cumsum([0, SHIFT_W] + [WA] * 8).tolist()))
VEC_N = SHIFT_W + WA * 9
SLOTS = (2 * (SEQ + TS) + NE * (P - 1)) // P * P
RC_PRIO, RC_THR, RC_LT, RC_TILE, RC_VALID, RC_TRI = 0, 4, 16, 16 + NE * NE, 48 + NE * NE, 60 + NE * NE
RC_SLOT, RC_OWN = RC_TRI + P, RC_TRI + P + NE
RC_N = RC_OWN + SLOTS // P
C_READY, V2_READY, O_READY = 2, 16, 25


def shape_constants():
    lg = np.log1p(-np.exp2(-5.0 - np.arange(HB)))
    half = NK // 2
    inv = (10000.0 ** (-np.arange(half) / half)).astype(np.float32)
    fc = np.zeros((TILES, P, FC_N), np.float32)
    s, t = np.arange(P)[:, None], np.arange(P)[None, :]
    for n in range(TILES):
        if n < NT:
            pos = np.arange(P) + n * P
            idx, chunk = np.arange(P), P
            mid = (s < P // 2) * np.ones((1, P))
            fc[n, :, FC_TI:FC_TI + P] = (s <= t) - mid
            fc[n, :, FC_TE:FC_TE + P] = (s < t) - mid
            fc[n, :, FC_SEL] = np.arange(P) < P // 2
            fc[n, :, FC_SEL + 1] = np.arange(P) >= P // 2
        else:
            pos = PAST + np.arange(P) % DS
            idx, chunk = np.arange(P) % DS, DS
            same = (s // DS == t // DS) & (s < TS) & (t < TS)
            fc[n, :, FC_TI:FC_TI + P] = same & (s <= t)
            fc[n, :, FC_TE:FC_TE + P] = same & (s < t)
            fc[n, :, FC_SEL:FC_SEL + DB] = (np.arange(P)[:, None] // DS == np.arange(DB))
        ang = pos.astype(np.float32)[:, None] * inv[None, :]
        fc[n, :, FC_COS:FC_COS + half] = np.cos(ang)
        fc[n, :, FC_SIN:FC_SIN + half] = np.sin(ang)
        fc[n, :, FC_CROSS:FC_CROSS + HB] = np.exp(lg[None] * (idx[:, None] + 1.0))
        fc[n, :, FC_KDEC:FC_KDEC + HB] = np.exp(lg[None] * (chunk - 1.0 - idx[:, None])) * NK ** -0.5
    mc = np.zeros((2, P, MC_N), np.float32)
    for kind in range(2):
        ok = np.ones((P, P), bool) if kind == 0 else (s // DS == t // DS) & (s < TS) & (t < TS)
        for q in range(4):
            mc[kind, :, MC_GRAM + q * P:MC_GRAM + (q + 1) * P] = ok & ((s < t) if q % 2 == 0 else (s <= t))
        for h in range(HB):
            dec = np.where(s <= t, np.exp(lg[h] * np.maximum(t - s, 0)), 0.0) * NK ** -0.5
            at = MC_D + (h % 2 * 2 + h // 2) * P
            mc[kind, :, at:at + P] = dec * ok
        for j in range(LEVELS):
            b = 1 << j
            up = ok & (s // (2 * b) == t // (2 * b)) & (s // b % 2 == 0) & (t // b % 2 == 1)
            mc[kind, :, MC_LVL + j * P:MC_LVL + (j + 1) * P] = up
            if j == 0:
                mc[kind, :, MC_M0:MC_M0 + P] = up.T
        cd = np.exp(lg * (P if kind == 0 else DS))
        for pair in range(2):
            mc[kind, :64, MC_CDEC + pair] = cd[2 * pair]
            mc[kind, 64:, MC_CDEC + pair] = cd[2 * pair + 1]
        mc[kind, :, MC_BLK:MC_BLK + DB] = (np.arange(P)[:, None] // DS == np.arange(DB))
    rc = np.zeros((P, RC_N), np.float32)
    rc[:, RC_PRIO:RC_PRIO + 4] = np.arange(4, 0, -1)
    rc[:, RC_THR:RC_THR + TILES] = P * np.arange(TILES)
    rc[:, RC_THR] = 1e9
    rc[:, RC_SLOT:RC_SLOT + NE] = P * np.arange(NE)
    rc[:, RC_OWN:RC_OWN + NE] = np.arange(NE)
    rc[:, RC_LT:RC_LT + NE * NE] = (np.arange(NE)[None, :] < np.arange(NE)[:, None]).reshape(-1)
    rc[:, RC_TILE:RC_TILE + SLOTS // P] = np.arange(SLOTS // P)
    rc[:, RC_VALID:RC_VALID + TILES] = (np.arange(TILES) < NT) | (np.arange(P)[:, None] < TS)
    rc[:, RC_TRI:RC_TRI + P] = s < t
    return fc, mc, rc


W_SCALE = 64.0


class Signal:

    def __init__(self, nc, ctx, name, per, by=1, primed=False):
        self.sem = ctx.enter_context(nc.semaphore(name)) if ctx is not None else nc.alloc_semaphore(name)
        self.per, self.by, self.primed = per, by, primed

    def prime(self, eng):
        assert self.primed
        eng.sem_inc(self.sem, self.by)

    def at(self, t, j=None):
        return (t * self.per + (self.per if j is None else j) + (1 if self.primed else 0)) * self.by


def split_hi(act, hi, x, scale):
    return act.activation(hi, x, ACT.Copy, scale=scale)


def split_lo(dve, lo, x, scale, hi):
    return dve.scalar_tensor_tensor(lo, x, scale, hi, ALU.mult, ALU.subtract)


def project(nc, soft, x_all, w_in, proj, sorted_h, load_next):
    nb = 6
    per = 2 * TILES
    pieces = 4
    kp = KD // pieces
    assert per % nb == 0 and nb % 2 == 0 and TILES // 2 >= pieces
    with ExitStack() as ctx:
        def sb(name, shape, dt=F32):
            return ctx.enter_context(nc.sbuf_tensor("pj_" + name, shape, dt))

        def sem(name):
            return ctx.enter_context(nc.semaphore("pj_" + name))

        xT = sb("xT", [P, TILES, KD, P])
        xh, xl = sb("xh", [P, TILES, KD, P], F16), sb("xl", [P, TILES, KD, P], F16)
        w = [sb(f"w{u}", [P, KD, SLICE]) for u in range(2)]
        wh, wl = ([sb(f"{n}{u}", [P, KD, SLICE], F16) for u in range(2)] for n in ("wh", "wl"))
        stage = [sb(f"out{b}", [P, SLICE]) for b in range(nb)]
        bank = [ctx.enter_context(nc.psum_tensor(f"pj_ps{b}", [P, 512], F32)) for b in range(nb)]
        x_loaded = [sem(f"x_loaded{g}") for g in range(3)]
        w_loaded = [sem(f"w_loaded{u}") for u in range(2)]
        x_hi, x_lo = sem("x_hi"), sem("x_lo")
        w_hi, w_lo = sem("w_hi"), sem("w_lo")
        summed = sem("summed")
        bank_free = [sem(f"bank_free{e}") for e in range(2)]
        stored = [sem(f"stored{b}") for b in range(nb)]
        zero = sb("zero", [P, D])
        zero_set = sem("zero_set")
        zeroed = soft.enter_context(nc.semaphore("pj_zeroed"))
        with nc.Block() as block:

            @block.sync
            def _(sp):
                for g in range(3):
                    sp.dma_start(xT[:, 3 * g:3 * g + 3], x_all[:, 3 * g:3 * g + 3]).then_inc(x_loaded[g], 16)
                    if g == 0:
                        sp.dma_start(w[0][:], w_in[0]).then_inc(w_loaded[0], 16)
                sp.dma_start(w[1][:], w_in[1]).then_inc(w_loaded[1], 16)
                load_next(sp)
                for b in range(nb):
                    sp.sem_inc(stored[b], 16)

                def two_slices(i, more):
                    for q in range(per):
                        b = q % nb
                        sp.wait_ge(bank_free[q % 2], i * TILES + q // 2 + 1 + nb // 2)
                        rows = proj[P * (q % TILES):P * (q % TILES) + P]
                        cols = rows.rearrange("p (s c) -> s p c", c=SLICE)[2 * i + q // TILES]
                        sp.dma_start(cols, stage[b][:]).then_inc(stored[b], 16)
                        if more and q % TILES == 0:
                            u = q // TILES
                            sp.wait_ge(w_lo, (2 * i + u + 1) * pieces)
                            sp.dma_start(w[u][:], w_in[2 * i + 2 + u]).then_inc(w_loaded[u], 16)

                with sp.Fori(0, NSLICE // 2 - 1) as i:
                    two_slices(i, True)
                two_slices(NSLICE // 2 - 1, False)
                for b in range(nb):
                    sp.wait_ge(stored[b], 16 * ((NSLICE // 2) * (per // nb) + 1))

            @block.tensor
            def _(pe):
                with pe.Fori(0, NSLICE // 2) as i:
                    for q in range(per):
                        u, m, b = q // TILES, q % TILES, q % nb
                        if u == 0 and m % 3 == 0:
                            pe.wait_ge(x_lo, m // 3 + 1)
                        pe.wait_ge(bank_free[q % 2], i * TILES + q // 2 + 1)
                        for k in range(KD):
                            if m == 0 and k % kp == 0:
                                pe.wait_ge(w_lo, (2 * i + u) * pieces + k // kp + 1)
                            for n, (x, y) in enumerate(((xh, wh[u]), (xh, wl[u]), (xl, wh[u]))):
                                mm = nc.tensor.matmul(bank[b][:, 0:SLICE], x[:, m, k], y[:, k], start=(k == 0 and n == 0), stop=(k == KD - 1 and n == 2))
                        mm.then_inc(summed, 1)

            @block.gpsimd
            def _(pool):
                nc.gpsimd.memset(zero[:], 0.0).then_inc(zero_set, 1)
                pool.wait_ge(zero_set, 1)
                with pool.Fori(0, SLOTS // P) as j:
                    pool.wait_ge(summed, NSLICE * TILES * P // SLOTS * (j + 1))
                    pool.dma_start(sorted_h.rearrange("(j p) d -> j p d", p=P)[j], zero[:]).then_inc(zeroed, 16)
                pool.wait_ge(zeroed, 16 * (SLOTS // P))

            def slices(eng, e, copy, split_x, split_w):
                eng.sem_inc(bank_free[e], nb // 2)
                split_x(0)
                for c in range(pieces):
                    split_w(0, 0, 0, c)
                split_x(1)
                split_x(2)

                def two(i, more):
                    for q in range(e, per, 2):
                        b, u = q % nb, q // TILES
                        eng.wait_ge(summed, i * per + q + 1)
                        eng.wait_ge(stored[b], (i * (per // nb) + q // nb + 1) * 16)
                        copy(stage[b][:], bank[b][:, 0:SLICE]).then_inc(bank_free[e], 1)
                        c = q % TILES // 2
                        if c < pieces and (more or u == 0):
                            split_w(2 * i + u + 1, 1 - u, i + u, c)

                with eng.Fori(0, NSLICE // 2 - 1) as i:
                    two(i, True)
                two(NSLICE // 2 - 1, False)

            @block.scalar
            def _(act):
                def split_x(g):
                    act.wait_ge(x_loaded[g], 16)
                    split_hi(nc.scalar, xh[:, 3 * g:3 * g + 3], xT[:, 3 * g:3 * g + 3], 1.0).then_inc(x_hi, 1)

                def split_w(s, u, k, c):
                    act.wait_ge(w_loaded[u], (k + 1) * 16)
                    r = slice(kp * c, kp * c + kp)
                    split_hi(nc.scalar, wh[u][:, r], w[u][:, r], W_SCALE).then_inc(w_hi, 1)

                slices(act, 0, lambda out, x: nc.scalar.activation(out, x, ACT.Copy, scale=1.0 / W_SCALE), split_x, split_w)

            @block.vector
            def _(dve):
                def split_x(g):
                    dve.wait_ge(x_hi, g + 1)
                    split_lo(nc.vector, xl[:, 3 * g:3 * g + 3], xT[:, 3 * g:3 * g + 3], 1.0, xh[:, 3 * g:3 * g + 3]).then_inc(x_lo, 1)

                def split_w(s, u, k, c):
                    dve.wait_ge(w_hi, s * pieces + c + 1)
                    r = slice(kp * c, kp * c + kp)
                    split_lo(nc.vector, wl[u][:, r], w[u][:, r], W_SCALE, wh[u][:, r]).then_inc(w_lo, 1)

                slices(dve, 1, lambda out, x: nc.vector.tensor_scalar(out, x, 1.0 / W_SCALE, None, ALU.mult), split_x, split_w)


class MixerConstants:

    def __init__(self, nc, ctx):
        def sb(name, shape):
            return ctx.enter_context(nc.sbuf_tensor("mx_" + name, shape, F32))

        self.vec = sb("vec", [P, VEC_N])
        self.wlo = sb("wlo", [P, WA])
        self.wga = sb("wga", [P, WA])
        self.mc, self.mcs = sb("mc", [P, MC_N]), sb("mcs", [P, MC_N])
        self.ident = sb("ident", [P, P])
        self.loaded = ctx.enter_context(nc.semaphore("mx_loaded"))

    def load(self, eng, vecs, w_lora, w_gate, mconst, ident_d):
        for dst, src in ((self.vec, vecs.broadcast_to([P, VEC_N])), (self.wlo, w_lora), (self.wga, w_gate),
                         (self.mc, mconst[0]), (self.mcs, mconst[1]), (self.ident, ident_d)):
            eng.dma_start(dst[:], src).then_inc(self.loaded, 16)

    def wait(self, eng):
        eng.wait_ge(self.loaded, 6 * 16)


def mixer(nc, const, proj, fconst, s0T_d, r0_d, yT_d, wkv_p, ret_p, wkv_s, ret_s):
    signals = []
    with ExitStack() as ctx:
        def sb(name, shape):
            return ctx.enter_context(nc.sbuf_tensor("mx_" + name, shape, F32))

        def two(name, shape):
            return [sb(f"{name}{u}", shape) for u in range(2)]

        def sig(name, per, by=1, primed=False):
            signals.append(Signal(nc, None, "mx_" + name, per, by, primed))
            return signals[-1]

        vec, wlo, wga, mc, mcs, ident = const.vec, const.wlo, const.wga, const.mc, const.mcs, const.ident
        halves = sb("halves", [P, 8])
        one = sb("one", [P, 1])
        fc = two("fc", [P, FC_N])
        cur = sb("cur", [P, SHIFT_W])
        sh = two("sh", [P, SHIFT_W])
        curB = two("curB", [P, IN_W - SHIFT_W])
        loraT = sb("loraT", [P, 2 * P])
        lw = sb("lw", [P, WA])
        ga = sb("ga", [P, WA])
        gate = two("gate", [P, WA])
        kk = sb("kk", [P, WA])
        kp = sb("kp", [P, WA])
        t1 = sb("t1", [P, WA])
        t3 = sb("t3", [P, WA])
        e1 = sb("e1", [P, WA])
        e2 = sb("e2", [P, WA])
        e3 = sb("e3", [P, WA])
        ss = sb("ss", [P, HA])
        rn = sb("rn", [P, HA])
        em = two("em", [P, HA // 2, DB])
        bt = two("bt", [P, WA])
        kt = two("kt", [P, WA])
        bonus = two("bonus", [P, HA])
        rot = sb("rot", [P, 2 * HB * NK])
        qh = sb("qh", [P, HB * NK])
        kh = two("kh", [P, HB * NK])
        arT = sb("arT", [P, HA // 2, 2, P])
        bT = sb("bT", [P, HA // 2, P])
        kT = sb("kT", [P, HA // 2, P])
        qT = sb("qT", [P, 4, P])
        kTr = sb("kTr", [P, 2, P])
        G = sb("G", [P, HA, 4, P])
        scT = sb("scT", [P, HB, P])
        ET = two("ET", [P, 4, P])
        M = two("M", [P, 4, P])
        MT = two("MT", [P, 4, P])
        X = two("X", [P, 4, P])
        wsb = sb("wsb", [P, HA, NA])
        usb = sb("usb", [P, HA, NA])
        S = sb("S", [P, HA // 2, NA])
        S0 = sb("S0", [P, HA // 2, 2, NA])
        R = sb("R", [P, HB // 2, 2, NV])
        t2 = sb("t2", [P, WA])
        y = sb("y", [P, HA + HB * 2, NA])
        sq = sb("sq", [P, WA])
        sg = sb("sg", [P, WA])
        mean = sb("mean", [P, HA + HB])
        var = sb("var", [P, HA + HB])
        rs = sb("rs", [P, HA + HB])
        yT = sb("yT", [P, KD, P])
        s0T = sb("s0T", [P, DB, 4, NA])
        r0 = sb("r0", [P, DB, 2, NV])
        wTs = sb("wTs", [64, 2, 4, 2, TS])
        oTs = sb("oTs", [P, 2, 2, TS])
        B = [ctx.enter_context(nc.psum_tensor(f"mx_ps{b}", [P, 512], F32)) for b in range(8)]

        def v(name, width=WA):
            return vec[:, VEC_OFF[name]:VEC_OFF[name] + width]

        def heads(x, n):
            return x.rearrange("p (h d) -> p h d", h=n)

        def over(x, n):
            return x.unsqueeze(2).broadcast_to([P, x.shape[1], n])

        half_set = sig("half_set", 1)
        s_zero = sig("s_zero", 1)
        rwkv_in = [sig(f"rwkv_in{u}", 2, 16) for u in range(2)]
        ret_in = [sig(f"ret_in{u}", 2, 16) for u in range(2)]
        mix_d = sig("mix_d", 3)
        lora_d = sig("lora_d", 1)
        z_d = sig("z_d", 2)
        lwa_d = sig("lwa_d", 2)
        kk_d = sig("kk_d", 7)
        scaled_d = sig("scaled_d", 4)
        bonus_d = sig("bonus_d", 3)
        rot_d = sig("rot_d", 6)
        gram_d = sig("gram_d", HA)
        sc_d = sig("sc_d", 2)
        s0_d = sig("s0_d", 2)
        m0_d = sig("m0_d", 4)
        m_d = sig("m_d", 2 * (LEVELS - 2))
        mt_d = sig("mt_d", 2 * (LEVELS - 1))
        state_d = sig("state_d", 7, primed=True)
        ya_d = sig("ya_d", 11, primed=True)
        yb_d = sig("yb_d", 9)
        lora_a = sig("lora_a", 2)
        loraT_a = sig("loraT_a", 1)
        tz_a = sig("tz_a", 2)
        gate_a = sig("gate_a", 1)
        kksq_a = sig("kksq_a", 1)
        exp_a = sig("exp_a", 4)
        turn_a = sig("turn_a", 6)
        x_a = sig("x_a", 2 * (LEVELS - 1))
        w_a = sig("w_a", 1)
        u_a = sig("u_a", 1)
        sil_a = sig("sil_a", 1)
        sq_a = sig("sq_a", 2)
        yT_a = sig("yT_a", 2, primed=True)
        rn_g = sig("rn_g", 1)
        mt0_g = sig("mt0_g", 4)
        et_g = sig("et_g", 2 * (LEVELS - 1))
        rs_g = sig("rs_g", 2)
        sil1_g = sig("sil1_g", 1)
        sil_g = sig("sil_g", 1)
        loraT_p = sig("loraT_p", 1)
        z_p = sig("z_p", 3)
        cum_p = sig("cum_p", 3)
        turn_p = sig("turn_p", 6)
        gram_p = sig("gram_p", HA)
        sc_p = sig("sc_p", 1)
        l0_p = sig("l0_p", 2)
        x_p = sig("x_p", 2 * (LEVELS - 1))
        m_p = sig("m_p", 2 * (LEVELS - 2))
        mt_p = sig("mt_p", 2 * (LEVELS - 1))
        w_p = sig("w_p", 1)
        u_p = sig("u_p", 1)
        y_p = sig("y_p", 1)
        ds_p = sig("ds_p", 1)
        o_p = sig("o_p", 1)
        dr_p = sig("dr_p", 1)
        yT_p = sig("yT_p", 2)
        yT_out = sig("yT_out", 1, 16, primed=True)
        s0T_in = sig("s0T_in", 1, 16)
        blk_d = sig("blk_d", 8)
        sum_d = sig("sum_d", 4)
        new_d = sig("new_d", 8)
        new_p = sig("new_p", 8)
        sw_p = sig("sw_p", 1)
        sw_a = sig("sw_a", 4)
        st_out = sig("st_out", 1, 16)

        ex = ctx.enter_context(ExitStack())
        block = ex.enter_context(nc.Block())

        def tiles(eng, prologue, body, epilogue):
            prologue()
            body(0, 0, 0)
            with eng.Fori(0, NT // 2 - 1) as i:
                body(2 * i + 1, 1, i)
                body(2 * i + 2, 0, i + 1)
            body(NT - 1, 1, NT // 2 - 1)
            epilogue()

        def later(t, n):
            return not isinstance(t, int) or t >= n

        @block.sync
        def _(sp):
            def load(t, u, k, sample=False):
                if later(t, 2):
                    sp.wait_ge(ya_d.sem, ya_d.at(t - 2, 4))
                sp.wait_ge(mix_d.sem, mix_d.at(t, 0))
                if sample:
                    rows = proj[SAMPLE0:SAMPLE0 + DB * (DS + 1)].rearrange("(b t) c -> b t c", b=DB)
                    sp.dma_start(cur[0:TS, :], rows[:, 1:, 0:SHIFT_W]).then_inc(rwkv_in[u].sem, 16)
                    sp.dma_start(sh[u][0:TS, :], rows[:, :DS, 0:SHIFT_W]).then_inc(rwkv_in[u].sem, 16)
                    sp.dma_start(curB[u][0:TS, :], rows[:, 1:, SHIFT_W:]).then_inc(ret_in[u].sem, 16)
                else:
                    own = proj[1:1 + SEQ].rearrange("(n p) c -> n p c", p=P)[t]
                    sp.dma_start(cur[:], own[:, 0:SHIFT_W]).then_inc(rwkv_in[u].sem, 16)
                    sp.dma_start(sh[u][:], proj[0:SEQ].rearrange("(n p) c -> n p c", p=P)[t, :, 0:SHIFT_W]).then_inc(rwkv_in[u].sem, 16)
                    sp.dma_start(curB[u][:], own[:, SHIFT_W:]).then_inc(ret_in[u].sem, 16)
                sp.dma_start(fc[u][:], fconst[t]).then_inc(ret_in[u].sem, 16)

            def store(t):
                sp.wait_ge(yT_a.sem, yT_a.at(t))
                sp.dma_start(yT_d[t], yT[:]).then_inc(yT_out.sem, 16)

            yT_out.prime(sp)
            load(0, 0, 0)
            sp.dma_start(s0T[:], s0T_d).then_inc(s0T_in.sem, 16)
            sp.dma_start(r0[:], r0_d).then_inc(s0T_in.sem, 16)
            load(1, 1, 0)
            with sp.Fori(0, NT // 2 - 1) as i:
                for u in range(2):
                    load(2 * i + u + 2, u, i + 1)
                    store(2 * i + u)
            load(NT, 0, NT // 2, sample=True)
            store(NT - 2)
            store(NT - 1)
            sp.wait_ge(state_d.sem, state_d.at(NT - 1))
            sp.dma_start(wkv_p, S[:]).then_inc(st_out.sem, 16)
            for o in range(2):
                r = slice(64 * o, 64 * o + 64)
                sp.dma_start(ret_p[r], R[r, :, o]).then_inc(st_out.sem, 16)
            store(NT)
            sp.wait_ge(new_d.sem, 4)
            sp.dma_start(wkv_s, s0T[:]).then_inc(st_out.sem, 16)
            sp.wait_ge(new_d.sem, 8)
            sp.dma_start(ret_s, r0[:]).then_inc(st_out.sem, 16)
            sp.wait_ge(yT_out.sem, yT_out.at(NT))
            sp.wait_ge(st_out.sem, 16 * 5)

        @block.tensor
        def _(pe):
            mm = nc.tensor.matmul

            def f_loraT(t, u):
                pe.wait_ge(lora_d.sem, lora_d.at(t))
                pe.wait_ge(exp_a.sem, exp_a.at(t, 0))
                if later(t, 2):
                    pe.wait_ge(yT_a.sem, yT_a.at(t - 3))
                nc.tensor.transpose(B[0][:, 0:P], sh[u][:, 3 * WA:3 * WA + P], ident[:])
                nc.tensor.transpose(B[0][:, P:2 * P], sh[u][:, 3 * WA + P:3 * WA + 2 * P], ident[:]).then_inc(loraT_p.sem, 1)

            def f_z(t, u):
                pe.wait_ge(loraT_a.sem, loraT_a.at(t))
                mm(B[1][:], loraT[0:64, 0:P], wlo[0:64, :], start=True, stop=True).then_inc(z_p.sem, 1)
                mm(B[0][:], loraT[64:128, 0:P], wlo[64:128, :], start=True, stop=True).then_inc(z_p.sem, 1)
                pe.wait_ge(z_d.sem, z_d.at(t, 1))
                mm(B[1][:], loraT[:, P:2 * P], wga[:], start=True, stop=True).then_inc(z_p.sem, 1)

            def f_cum(t, u):
                pe.wait_ge(lwa_d.sem, lwa_d.at(t, 1))
                mm(B[0][:], fc[u][:, FC_TI:FC_TI + P], lw[:], start=True, stop=True).then_inc(cum_p.sem, 1)
                pe.wait_ge(gate_a.sem, gate_a.at(t))
                mm(B[1][:], fc[u][:, FC_TE:FC_TE + P], lw[:], start=True, stop=True).then_inc(cum_p.sem, 1)
                pe.wait_ge(exp_a.sem, exp_a.at(t, 2))
                for q in range(HA // 2):
                    m = mm(B[0][:, q * DB:(q + 1) * DB], lw[:, q * P:(q + 1) * P], fc[u][:, FC_SEL:FC_SEL + DB], start=True, stop=True)
                m.then_inc(cum_p.sem, 1)

            def turn(t, u):
                srcs = [(e2, scaled_d, 4), (bt[u], scaled_d, 1), (e1, scaled_d, 3), (kt[u], scaled_d, 2)]
                for n, (src, s, j) in enumerate(srcs):
                    pe.wait_ge(s.sem, s.at(t, j))
                    if n >= 2:
                        pe.wait_ge(turn_a.sem, turn_a.at(t, n - 1))
                    for q in range(4):
                        m = nc.tensor.transpose(B[2 + n % 2][:, q * P:(q + 1) * P], src[:, q * P:(q + 1) * P], ident[:])
                    m.then_inc(turn_p.sem, 1)
                pe.wait_ge(rot_d.sem, rot_d.at(t))
                pe.wait_ge(turn_a.sem, turn_a.at(t, 3))
                for q in range(4):
                    src = rot[:, q * P:(q + 1) * P] if q < 2 else qh[:, (q - 2) * P:(q - 1) * P]
                    m = nc.tensor.transpose(B[2][:, q * P:(q + 1) * P], src, ident[:])
                m.then_inc(turn_p.sem, 1)
                pe.wait_ge(turn_a.sem, turn_a.at(t, 4))
                for q in range(2):
                    m = nc.tensor.transpose(B[3][:, q * P:(q + 1) * P], rot[:, (q + 2) * P:(q + 3) * P], ident[:])
                m.then_inc(turn_p.sem, 1)

            def grams(t):
                pe.wait_ge(turn_a.sem, turn_a.at(t, 4))
                pe.wait_ge(state_d.sem, state_d.at(t, 0))
                if later(t, 1):
                    pe.wait_ge(yb_d.sem, yb_d.at(t - 1, 3))
                    pe.wait_ge(ya_d.sem, ya_d.at(t - 1, 3))
                def turn_l(g):
                    pe.wait_ge(gram_d.sem, gram_d.at(t, 4 * g + 4))
                    if g == 0:
                        pe.wait_ge(turn_a.sem, turn_a.at(t, 5))
                    else:
                        pe.wait_ge(turn_a.sem, turn_a.at(t, 6))
                    for h in range(4):
                        m = nc.tensor.transpose(B[2 + g][:, h * P:(h + 1) * P], G[:, 4 * g + h, 0], ident[:])
                    m.then_inc(l0_p.sem, 1)

                for h in range(HA):
                    q, r = h // 2, slice(64 * (h % 2), 64 * (h % 2) + 64)
                    if h >= 2:
                        pe.wait_ge(gram_d.sem, gram_d.at(t, h - 1))
                    mm(B[4 + h % 2][:, 0:2 * P], bT[r, q], arT[r, q], start=True, stop=True)
                    mm(B[4 + h % 2][:, 2 * P:], kT[r, q], arT[r, q], start=True, stop=True).then_inc(gram_p.sem, 1)
                    if h == 5:
                        turn_l(0)
                pe.wait_ge(turn_a.sem, turn_a.at(t, 6))
                for h in (0, 2, 1, 3):
                    q, r = h // 2, slice(64 * (h % 2), 64 * (h % 2) + 64)
                    m = mm(B[6 + h % 2][:, q * P:(q + 1) * P], kTr[r, q], qT[r, q], start=True, stop=True)
                m.then_inc(sc_p.sem, 1)
                turn_l(1)

            def level(t, j, last=LEVELS - 1):
                n = 2 * (j - 1)
                for g in range(2):
                    pe.wait_ge(et_g.sem, et_g.at(t, n + g + 1))
                    if j == 1:
                        pe.wait_ge(m0_d.sem, m0_d.at(t, 2 * g + 2))
                    else:
                        pe.wait_ge(m_d.sem, m_d.at(t, n - 2 + g + 1))
                    for h in range(4):
                        m = mm(B[2 + g][:, h * P:(h + 1) * P], ET[g][:, h], M[g][:, h], start=True, stop=True)
                    m.then_inc(x_p.sem, 1)
                for g in range(2):
                    pe.wait_ge(x_a.sem, x_a.at(t, n + g + 1))
                    if j == 1:
                        pe.wait_ge(mt0_g.sem, mt0_g.at(t, 2 * g + 2))
                        pe.wait_ge(gram_d.sem, gram_d.at(t))
                        pe.wait_ge(sc_d.sem, sc_d.at(t))
                    else:
                        pe.wait_ge(mt_d.sem, mt_d.at(t, n - 2 + g + 1))
                    if j < last:
                        for h in range(4):
                            m = mm(B[4 + g][:, h * P:(h + 1) * P], MT[g][:, h], X[g][:, h], start=True, stop=True)
                        m.then_inc(m_p.sem, 1)
                    for h in range(4):
                        m = mm(B[6 + g][:, h * P:(h + 1) * P], X[g][:, h], MT[g][:, h], start=True, stop=True)
                    m.then_inc(mt_p.sem, 1)

            def chunk(t, u, i, sample, last):
                n = TS if sample else P
                vA, vB = sh[u], curB[u]
                pe.wait_ge(mt_d.sem, mt_d.at(t, 2 * last))
                if sample:
                    pe.wait_ge(s0T_in.sem, 32)
                    for par in range(2):
                        r = slice(64 * par, 64 * par + 64)
                        for q in range(4):
                            for b in range(DB):
                                out = B[2 + par][0:64, q * P:(q + 1) * P].rearrange("p (w t) -> p w t", w=2)[:, :, b * DS:(b + 1) * DS]
                                m = mm(out, s0T[r, b, q], arT[r, q, :, b * DS:(b + 1) * DS], start=True, stop=True)
                        m.then_inc(sw_p.sem, 1)
                        for q in range(2):
                            for b in range(DB):
                                m = mm(B[6 + par][:, q * TS + b * DS:q * TS + (b + 1) * DS], r0[r, b, q], qT[r, 2 + q, b * DS:(b + 1) * DS], start=True, stop=True)
                        m.then_inc(sw_p.sem, 1)
                    pe.wait_ge(sw_a.sem, 4)
                else:
                    pe.wait_ge(state_d.sem, state_d.at(t, 0))
                for h in range(HB):
                    q, r = h // 2, slice(64 * (h % 2), 64 * (h % 2) + 64)
                    o = B[6][0:n, h * NV:(h + 1) * NV]
                    if sample:
                        mm(o, oTs[:, h % 2, q], ident[:], start=True, stop=False)
                    elif h % 2 == 0:
                        mm(B[6][:, h * NV:(h + 2) * NV], qT[:, 2 + q], R[:, q], start=True, stop=False)
                    m = mm(o, scT[0:n, h, 0:n], vB[0:n, 512 + h * NV:512 + (h + 1) * NV], start=False, stop=sample or h % 2 == 1)
                m.then_inc(o_p.sem, 1)
                if not sample:
                    for h in range(HB):
                        q, r = h // 2, slice(64 * (h % 2), 64 * (h % 2) + 64)
                        m = mm(B[7][r, q * NV:(q + 1) * NV], kh[u][:, h * NK:(h + 1) * NK], vB[:, 512 + h * NV:512 + (h + 1) * NV], start=True, stop=True)
                    m.then_inc(dr_p.sem, 1)
                    pe.wait_ge(s0_d.sem, s0_d.at(t))
                pe.wait_ge(x_a.sem, x_a.at(t, 2 * last))
                for h in range(HA):
                    q, r = h // 2, slice(64 * (h % 2), 64 * (h % 2) + 64)
                    o = B[2][0:n, h * NA:(h + 1) * NA]
                    if sample:
                        mm(o, wTs[0:64, h % 2, q, 0], ident[0:64, 0:64], start=True, stop=False)
                    elif h % 2 == 0:
                        mm(B[2][:, h * NA:(h + 2) * NA], arT[:, q, 0], S0[:, q], start=True, stop=False)
                    m = mm(o, G[0:n, h, 2, 0:n], vA[0:n, 2 * WA + h * NA:2 * WA + (h + 1) * NA], start=False, stop=sample or h % 2 == 1)
                m.then_inc(w_p.sem, 1)
                if later(t, 1):
                    turn_y(t - 1, 0)
                pe.wait_ge(w_a.sem, w_a.at(t))
                for h in range(HA):
                    m = mm(B[3][0:n, h * NA:(h + 1) * NA], MT[h // 4][0:n, h % 4, 0:n], wsb[0:n, h], start=True, stop=True)
                m.then_inc(u_p.sem, 1)
                if later(t, 1):
                    turn_y(t - 1, 1)
                pe.wait_ge(u_a.sem, u_a.at(t))
                pe.wait_ge(m_d.sem, m_d.at(t, 2 * last - 2))
                if not sample:
                    for q in range(HA // 2):
                        cols, val = slice(q * P, (q + 1) * P), slice(2 * WA + q * P, 2 * WA + (q + 1) * P)
                        mm(B[5][:, cols], bt[u][:, cols], usb[:, 2 * q:2 * q + 2], start=True, stop=False)
                        m = mm(B[5][:, cols], kt[u][:, cols], vA[:, val], start=False, stop=True)
                    m.then_inc(ds_p.sem, 1)
                for h in range(HA):
                    q, r = h // 2, slice(64 * (h % 2), 64 * (h % 2) + 64)
                    o = B[4][0:n, h * NA:(h + 1) * NA]
                    if sample:
                        mm(o, wTs[0:64, h % 2, q, 1], ident[0:64, 0:64], start=True, stop=False)
                    elif h % 2 == 0:
                        mm(B[4][:, h * NA:(h + 2) * NA], arT[:, q, 1], S0[:, q], start=True, stop=False)
                    mm(o, G[0:n, h, 1, 0:n], usb[0:n, h], start=False, stop=False)
                    m = mm(o, G[0:n, h, 3, 0:n], vA[0:n, 2 * WA + h * NA:2 * WA + (h + 1) * NA], start=False, stop=sample or h % 2 == 1)
                m.then_inc(y_p.sem, 1)

            def sampled_states(t, u):
                pe.wait_ge(yT_a.sem, yT_a.at(t))
                for j in range(8):
                    bank = B[5] if j % 2 == 0 else B[0]
                    pe.wait_ge(blk_d.sem, j + 1)
                    if j >= 2:
                        pe.wait_ge(new_d.sem, j - 1)
                    left, right = (X, ET) if j % 2 == 0 else (M, MT)
                    for o in range(2):
                        r = slice(64 * o, 64 * o + 64)
                        if j < 4:
                            cols = slice((2 * j + o) * NA, (2 * j + o + 1) * NA)
                            mm(bank[r, :], bt[u][0:TS, cols], left[o][0:TS], start=True, stop=False)
                            m = mm(bank[r, :], kt[u][0:TS, cols], right[o][0:TS], start=False, stop=True)
                        else:
                            h = 2 * (j % 2) + o
                            m = mm(bank[r, :], kh[u][0:TS, h * NK:(h + 1) * NK], left[o][0:TS], start=True, stop=True)
                    m.then_inc(new_p.sem, 1)

            def turn_y(t, n):
                s, b = ((yb_d, 1), (ya_d, 0))[n]
                if n == 0:
                    pe.wait_ge(exp_a.sem, exp_a.at(NT if later(t, NT - 1) and isinstance(t, int) else t + 2))
                pe.wait_ge(s.sem, s.at(t))
                pe.wait_ge(yT_a.sem, yT_a.at(t, 0))
                for q in range(4):
                    src = y[:, 8 * b + 2 * q:8 * b + 2 * q + 2].rearrange("p h d -> p (h d)")
                    m = nc.tensor.transpose(B[b][:, q * P:(q + 1) * P], src, ident[:])
                m.then_inc(yT_p.sem, 1)

            def start():
                const.wait(pe)
                pe.wait_ge(ret_in[0].sem, 32)
                f_loraT(0, 0)
                f_z(0, 0)
                f_cum(0, 0)

            def body(t, u, i):
                turn(t, u)
                grams(t)
                level(t, 1)
                level(t, 2)
                level(t, 3)
                f_loraT(t + 1, 1 - u)
                level(t, 4)
                f_z(t + 1, 1 - u)
                level(t, 5)
                level(t, 6)
                pe.wait_ge(ret_in[1 - u].sem, (i + 1 + u) * 32)
                f_cum(t + 1, 1 - u)
                chunk(t, u, i, False, LEVELS - 1)

            def end():
                turn(NT, 0)
                grams(NT)
                level(NT, 1, LEVELS_S - 1)
                level(NT, 2, LEVELS_S - 1)
                chunk(NT, 0, NT // 2, True, LEVELS_S - 1)
                turn_y(NT, 0)
                turn_y(NT, 1)
                sampled_states(NT, 0)

            tiles(pe, start, body, end)

        @block.scalar
        def _(act):
            fn = nc.scalar.activation
            cp = nc.scalar.copy

            def f_lora(t, u):
                act.wait_ge(mix_d.sem, mix_d.at(t))
                w, g = sh[u][:, 3 * WA:3 * WA + 64], sh[u][:, 3 * WA + P:3 * WA + 2 * P]
                fn(w, w, ACT.Tanh).then_inc(lora_a.sem, 1)
                fn(g, g, ACT.Tanh, scale=0.5).then_inc(lora_a.sem, 1)

            def f_kksq(t):
                act.wait_ge(kk_d.sem, kk_d.at(t, 1))
                fn(e3[:], kk[:], ACT.Square).then_inc(kksq_a.sem, 1)

            def f_loraT(t):
                act.wait_ge(loraT_p.sem, loraT_p.at(t))
                cp(loraT[:], B[0][:, 0:2 * P]).then_inc(loraT_a.sem, 1)

            def f_z(t, u):
                act.wait_ge(z_d.sem, z_d.at(t, 1))
                fn(lw[:], lw[:], ACT.Tanh, scale=0.5).then_inc(tz_a.sem, 1)
                act.wait_ge(z_d.sem, z_d.at(t, 2))
                fn(ga[:], ga[:], ACT.Tanh, scale=0.5).then_inc(tz_a.sem, 1)

            def f_gate(t, u):
                act.wait_ge(z_p.sem, z_p.at(t, 3))
                if later(t, 2):
                    act.wait_ge(ya_d.sem, ya_d.at(t - 2))
                cp(gate[u][:], B[1][:]).then_inc(gate_a.sem, 1)

            def f_exp(t, u):
                act.wait_ge(cum_p.sem, cum_p.at(t, 1))
                fn(e1[:], B[0][:], ACT.Exp).then_inc(exp_a.sem, 1)
                act.wait_ge(kk_d.sem, kk_d.at(t, 2))
                fn(e3[:], B[0][:], ACT.Exp, scale=-1.0).then_inc(exp_a.sem, 1)
                act.wait_ge(cum_p.sem, cum_p.at(t, 2))
                fn(e2[:], B[1][:], ACT.Exp).then_inc(exp_a.sem, 1)
                act.wait_ge(cum_p.sem, cum_p.at(t, 3))
                fn(em[u][:], B[0][:, 0:HA // 2 * DB].rearrange("p (q b) -> p q b", b=DB), ACT.Exp).then_inc(exp_a.sem, 1)

            def turn(t):
                outs = [(arT[:, :, 0], 2, 512), (bT[:], 3, 512), (arT[:, :, 1], 2, 512), (kT[:], 3, 512), (qT[:], 2, 512), (kTr[:], 3, 256)]
                for n, (out, b, w) in enumerate(outs):
                    act.wait_ge(turn_p.sem, turn_p.at(t, n + 1))
                    cp(out, B[b][:, 0:w].rearrange("p (q t) -> p q t", t=P)).then_inc(turn_a.sem, 1)

            def level(t, j):
                for g in range(2):
                    n = 2 * (j - 1) + g + 1
                    act.wait_ge(x_p.sem, x_p.at(t, n))
                    if j > 1:
                        act.wait_ge(mt_p.sem, mt_p.at(t, n - 2))
                    cp(X[g][:], B[2 + g][:].rearrange("p (h t) -> p h t", t=P)).then_inc(x_a.sem, 1)

            def tail(t, u, n, sample):
                if sample:
                    for par in range(2):
                        act.wait_ge(sw_p.sem, 2 * par + 1)
                        cp(wTs[:, par], B[2 + par][0:64, :].rearrange("p (q w t) -> p q w t", q=4, w=2)).then_inc(sw_a.sem, 1)
                        act.wait_ge(sw_p.sem, 2 * par + 2)
                        cp(oTs[:, par], B[6 + par][:, 0:2 * TS].rearrange("p (q t) -> p q t", q=2)).then_inc(sw_a.sem, 1)
                if later(t, 1):
                    act.wait_ge(yb_d.sem, yb_d.at(t - 1))
                fn(sg[:], curB[u][:, 1024:1536], ACT.Tanh, scale=0.5).then_inc(sil_a.sem, 1)
                act.wait_ge(w_p.sem, w_p.at(t))
                cp(wsb[0:n], B[2][0:n].rearrange("p (h d) -> p h d", h=HA)).then_inc(w_a.sem, 1)
                if later(t, 1):
                    turn_y(t - 1, 0)
                act.wait_ge(u_p.sem, u_p.at(t))
                cp(usb[0:n], B[3][0:n].rearrange("p (h d) -> p h d", h=HA)).then_inc(u_a.sem, 1)
                if later(t, 1):
                    turn_y(t - 1, 1)
                act.wait_ge(yb_d.sem, yb_d.at(t, 3))
                fn(sq[:], y[:, 8:16].rearrange("p h d -> p (h d)"), ACT.Square).then_inc(sq_a.sem, 1)

            def square_a(t):
                act.wait_ge(ya_d.sem, ya_d.at(t, 3))
                fn(t2[:], y[:, 0:8].rearrange("p h d -> p (h d)"), ACT.Square).then_inc(sq_a.sem, 1)

            def turn_y(t, n):
                if n == 0:
                    act.wait_ge(yT_out.sem, yT_out.at(t, 0))
                act.wait_ge(yT_p.sem, yT_p.at(t, n + 1))
                cp(yT[:, 4 - 4 * n:8 - 4 * n], B[1 - n][:].rearrange("p (k t) -> p k t", t=P)).then_inc(yT_a.sem, 1)

            def start():
                yT_a.prime(act)
                f_lora(0, 0)
                f_kksq(0)
                f_loraT(0)
                f_z(0, 0)
                f_gate(0, 0)
                f_exp(0, 0)

            def body(t, u, i):
                turn(t)
                if later(t, 1):
                    square_a(t - 1)
                level(t, 1)
                level(t, 2)
                level(t, 3)
                f_lora(t + 1, 1 - u)
                f_kksq(t + 1)
                f_loraT(t + 1)
                level(t, 4)
                f_z(t + 1, 1 - u)
                level(t, 5)
                f_gate(t + 1, 1 - u)
                level(t, 6)
                f_exp(t + 1, 1 - u)
                tail(t, u, P, False)

            def end():
                turn(NT)
                square_a(NT - 1)
                level(NT, 1)
                level(NT, 2)
                tail(NT, 0, TS, True)
                square_a(NT)
                turn_y(NT, 0)
                turn_y(NT, 1)

            tiles(act, start, body, end)

        @block.vector
        def _(dve):
            tt = nc.vector.tensor_tensor
            ts = nc.vector.tensor_scalar
            stt = nc.vector.scalar_tensor_tensor

            def f_mix1(t, u, k):
                dve.wait_ge(rwkv_in[u].sem, (k + 1) * 32)
                tt(sh[u][:], sh[u][:], cur[:], ALU.subtract).then_inc(mix_d.sem, 1)

            def f_mix2(t, u):
                dve.wait_ge(mix_d.sem, mix_d.at(t, 1))
                tt(sh[u][:], sh[u][:], v("mu_shift", SHIFT_W), ALU.mult).then_inc(mix_d.sem, 1)

            def f_mix3(t, u):
                dve.wait_ge(mix_d.sem, mix_d.at(t, 2))
                tt(sh[u][:], sh[u][:], cur[:], ALU.add).then_inc(mix_d.sem, 1)

            def f_lora(t, u):
                dve.wait_ge(lora_a.sem, lora_a.at(t))
                g = sh[u][:, 3 * WA + P:3 * WA + 2 * P]
                ts(g, g, 0.5, 0.5, ALU.mult, ALU.add).then_inc(lora_d.sem, 1)

            def f_kk1(t, u):
                dve.wait_ge(mix_d.sem, mix_d.at(t))
                tt(kk[:], sh[u][:, WA:2 * WA], v("k_k"), ALU.mult).then_inc(kk_d.sem, 1)
                dve.wait_ge(kksq_a.sem, kksq_a.at(t))
                nc.vector.tensor_reduce(ss[:], heads(e3[:], HA), AX, ALU.add).then_inc(kk_d.sem, 1)
                dve.wait_ge(kk_d.sem, kk_d.at(t, 2))
                ts(ss[:], ss[:], 1e-24, None, ALU.max).then_inc(kk_d.sem, 1)

            def f_z(t):
                dve.wait_ge(z_p.sem, z_p.at(t, 1))
                tt(lw[:], B[1][:], v("decay_base"), ALU.add).then_inc(z_d.sem, 1)
                dve.wait_ge(z_p.sem, z_p.at(t, 2))
                tt(ga[:], B[0][:], v("aaa_base"), ALU.add).then_inc(z_d.sem, 1)

            def f_lwa(t):
                dve.wait_ge(tz_a.sem, tz_a.at(t, 1))
                ts(lw[:], lw[:], 1.0, W_CONST / 2, ALU.add, ALU.mult).then_inc(lwa_d.sem, 1)
                dve.wait_ge(tz_a.sem, tz_a.at(t, 2))
                ts(ga[:], ga[:], 0.5, 0.5, ALU.mult, ALU.add).then_inc(lwa_d.sem, 1)

            def f_kk2(t, u):
                dve.wait_ge(rn_g.sem, rn_g.at(t))
                tt(heads(kk[:], HA), heads(kk[:], HA), over(rn[:], NA), ALU.mult).then_inc(kk_d.sem, 1)
                dve.wait_ge(lwa_d.sem, lwa_d.at(t))
                dve.wait_ge(kk_d.sem, kk_d.at(t, 4))
                tt(bt[u][:], kk[:], ga[:], ALU.mult).then_inc(kk_d.sem, 1)
                if later(t, 2):
                    dve.wait_ge(ya_d.sem, ya_d.at(t - 2))
                stt(t1[:], ga[:], -1.0, v("k_a"), ALU.add, ALU.mult).then_inc(kk_d.sem, 1)
                dve.wait_ge(kk_d.sem, kk_d.at(t, 6))
                stt(kp[:], t1[:], 1.0, sh[u][:, WA:2 * WA], ALU.add, ALU.mult).then_inc(kk_d.sem, 1)

            def f_scale(t, u):
                dve.wait_ge(exp_a.sem, exp_a.at(t, 2))
                dve.wait_ge(kk_d.sem, kk_d.at(t, 7))
                tt(bt[u][:], bt[u][:], e3[:], ALU.mult).then_inc(scaled_d.sem, 1)
                tt(kt[u][:], kp[:], e3[:], ALU.mult).then_inc(scaled_d.sem, 1)
                tt(e1[:], e1[:], sh[u][:, 0:WA], ALU.mult).then_inc(scaled_d.sem, 1)
                dve.wait_ge(exp_a.sem, exp_a.at(t, 3))
                stt(e2[:], kk[:], -1.0, e2[:], ALU.mult, ALU.mult).then_inc(scaled_d.sem, 1)
                dve.wait_ge(rot_d.sem, rot_d.at(t))
                tt(t1[:], sh[u][:, 0:WA], kp[:], ALU.mult).then_inc(bonus_d.sem, 1)
                dve.wait_ge(bonus_d.sem, bonus_d.at(t, 1))
                tt(t1[:], t1[:], v("r_k"), ALU.mult).then_inc(bonus_d.sem, 1)
                dve.wait_ge(bonus_d.sem, bonus_d.at(t, 2))
                nc.vector.tensor_reduce(bonus[u][:], heads(t1[:], HA), AX, ALU.add).then_inc(bonus_d.sem, 1)

            def f_rot(t, u, k):
                dve.wait_ge(ret_in[u].sem, (k + 1) * 32)
                dve.wait_ge(kk_d.sem, kk_d.at(t, 7))
                x = curB[u][:, 0:512].rearrange("p (n d) -> p n d", d=32)
                cos = fc[u][:, FC_COS:FC_COS + 32].unsqueeze(1).broadcast_to([P, 16, 32])
                sin = fc[u][:, FC_SIN:FC_SIN + 32].unsqueeze(1).broadcast_to([P, 16, 32])
                a4, b4 = (z[:].rearrange("p (h two d) -> p h two d", two=2, d=32) for z in (t3, t1))
                r4 = rot[:].rearrange("p (h two d) -> p h two d", two=2, d=32)
                tt(t3[:].rearrange("p (n d) -> p n d", d=32), x, cos, ALU.mult).then_inc(rot_d.sem, 1)
                tt(t1[:].rearrange("p (n d) -> p n d", d=32), x, sin, ALU.mult).then_inc(rot_d.sem, 1)
                dve.wait_ge(rot_d.sem, rot_d.at(t, 2))
                tt(r4[:, :, 0], a4[:, :, 0], b4[:, :, 1], ALU.subtract).then_inc(rot_d.sem, 1)
                tt(r4[:, :, 1], b4[:, :, 0], a4[:, :, 1], ALU.add).then_inc(rot_d.sem, 1)
                dve.wait_ge(rot_d.sem, rot_d.at(t, 4))
                for out, c0, col in ((qh, 0, FC_CROSS), (kh[u], 256, FC_KDEC)):
                    tt(heads(out[:], HB), heads(rot[:, c0:c0 + 256], HB), over(fc[u][:, col:col + HB], NK), ALU.mult).then_inc(rot_d.sem, 1)

            def grams(t, u, c, sample):
                def first(g):
                    dve.wait_ge(l0_p.sem, l0_p.at(t, g + 1))
                    m0 = c[:, MC_M0:MC_M0 + P].unsqueeze(1).broadcast_to([P, 4, P])
                    tt(M[g][:], B[2 + g][:].rearrange("p (h t) -> p h t", t=P), m0, ALU.mult).then_inc(m0_d.sem, 1)
                    dve.wait_ge(m0_d.sem, m0_d.at(t, 2 * g + 1))
                    tt(M[g][:], M[g][:], ident[:].unsqueeze(1).broadcast_to([P, 4, P]), ALU.add).then_inc(m0_d.sem, 1)

                for h in range(HA):
                    dve.wait_ge(gram_p.sem, gram_p.at(t, h + 1))
                    tt(G[:, h].rearrange("p a b -> p (a b)"), B[4 + h % 2][:], c[:, MC_GRAM:MC_GRAM + 512], ALU.mult).then_inc(gram_d.sem, 1)
                    if h == 6:
                        first(0)
                dve.wait_ge(sc_p.sem, sc_p.at(t))
                for o in range(2):
                    dmask = c[:, MC_D + 256 * o:MC_D + 256 * o + 256].rearrange("p (h t) -> p h t", h=2)
                    tt(scT[:, o::2], B[6 + o][:, 0:256].rearrange("p (h t) -> p h t", h=2), dmask, ALU.mult).then_inc(sc_d.sem, 1)
                first(1)
                if not sample:
                    dve.wait_ge(exp_a.sem, exp_a.at(t))
                    dve.wait_ge(state_d.sem, state_d.at(t, 0))
                    for o in range(2):
                        r = slice(64 * o, 64 * o + 64)
                        decay = em[u][r, :, 0].unsqueeze(2).broadcast_to([64, 4, NA])
                        tt(S0[r, :, o], S[r], decay, ALU.mult).then_inc(s0_d.sem, 1)

            def level(t, j, last=LEVELS - 1):
                for g in range(2):
                    n = 2 * (j - 1) + g + 1
                    if j < last:
                        dve.wait_ge(m_p.sem, m_p.at(t, n))
                        tt(M[g][:], B[4 + g][:].rearrange("p (h t) -> p h t", t=P), M[g][:], ALU.add).then_inc(m_d.sem, 1)
                    dve.wait_ge(mt_p.sem, mt_p.at(t, n))
                    tt(MT[g][:], B[6 + g][:].rearrange("p (h t) -> p h t", t=P), MT[g][:], ALU.add).then_inc(mt_d.sem, 1)

            def moments(s, t, off, n, width, bank, dst):
                dve.wait_ge(bank[0].sem, bank[0].at(t))
                src = heads(bank[1][:], n)
                nc.vector.tensor_reduce(mean[:, off:off + n], src, AX, ALU.add).then_inc(s.sem, 1)
                dve.wait_ge(s.sem, s.at(t, 1))
                ts(mean[:, off:off + n], mean[:, off:off + n], 1.0 / width, None, ALU.mult).then_inc(s.sem, 1)
                dve.wait_ge(s.sem, s.at(t, 2))
                tt(dst, src, over(mean[:, off:off + n], width), ALU.subtract).then_inc(s.sem, 1)

            def variance(s, t, step, off, n, width, sqv, sq_step, eps):
                dve.wait_ge(sq_a.sem, sq_a.at(t, sq_step))
                nc.vector.tensor_reduce(var[:, off:off + n], heads(sqv[:], n), AX, ALU.add).then_inc(s.sem, 1)
                dve.wait_ge(s.sem, s.at(t, step))
                ts(var[:, off:off + n], var[:, off:off + n], 1.0 / width, eps, ALU.mult, ALU.add).then_inc(s.sem, 1)

            yA, yB = y[:, 0:8], y[:, 8:16].rearrange("p (h a) d -> p h (a d)", a=2)
            flatB, flatA = y[:, 8:16].rearrange("p h d -> p (h d)"), y[:, 0:8].rearrange("p h d -> p (h d)")

            def tail(t, u, c, sample):
                if later(t, 1):
                    dve.wait_ge(yT_p.sem, yT_p.at(t - 1))
                moments(yb_d, t, HA, HB, NV, (o_p, B[6]), yB)
                if not sample:
                    dve.wait_ge(dr_p.sem, dr_p.at(t))
                    for h in range(HB):
                        q, r = h // 2, slice(64 * (h % 2), 64 * (h % 2) + 64)
                        stt(R[r, q, h % 2], R[r, q, h % 2], c[r, MC_CDEC + q:MC_CDEC + q + 1], B[7][r, q * NV:(q + 1) * NV], ALU.mult, ALU.add).then_inc(state_d.sem, 1)
                    dve.wait_ge(ds_p.sem, ds_p.at(t))
                    for o in range(2):
                        r = slice(64 * o, 64 * o + 64)
                        tt(S[r], B[5][r].rearrange("p (q o d) -> p q o d", q=4, o=2)[:, :, o], S0[r, :, o], ALU.add).then_inc(state_d.sem, 1)
                    dve.wait_ge(state_d.sem, state_d.at(t, 6))
                    tt(S[:], S[:], over(em[u][:, :, 1], NA), ALU.mult).then_inc(state_d.sem, 1)
                moments(ya_d, t, 0, HA, NA, (y_p, B[4]), yA)
                dve.wait_ge(sil_g.sem, sil_g.at(t))
                dve.wait_ge(bonus_d.sem, bonus_d.at(t if sample else t + 1))
                tt(heads(t1[:], HA), heads(sh[u][:, 2 * WA:3 * WA], HA), over(bonus[u][:], NA), ALU.mult).then_inc(ya_d.sem, 1)

            def norms1(t):
                variance(yb_d, t, 4, HA, HB, NV, sq, 1, GN_EPS_B)
                variance(ya_d, t, 5, 0, HA, NA, t2, 2, GN_EPS_A)

            def norms2(t):
                dve.wait_ge(rs_g.sem, rs_g.at(t, 1))
                tt(yB, yB, over(rs[:, HA:HA + HB], NV), ALU.mult).then_inc(yb_d.sem, 1)
                dve.wait_ge(yb_d.sem, yb_d.at(t, 6))
                tt(flatB, flatB, v("ret_gn_g"), ALU.mult).then_inc(yb_d.sem, 1)
                dve.wait_ge(yb_d.sem, yb_d.at(t, 7))
                tt(flatB, flatB, v("ret_gn_b"), ALU.add).then_inc(yb_d.sem, 1)
                dve.wait_ge(yb_d.sem, yb_d.at(t, 8))
                stt(flatB, flatB, 0.5, sg[:], ALU.mult, ALU.mult).then_inc(yb_d.sem, 1)

            def norms3(t, u):
                dve.wait_ge(rs_g.sem, rs_g.at(t, 2))
                tt(yA, yA, over(rs[:, 0:HA], NA), ALU.mult).then_inc(ya_d.sem, 1)
                dve.wait_ge(ya_d.sem, ya_d.at(t, 7))
                tt(flatA, flatA, v("lnx_g"), ALU.mult).then_inc(ya_d.sem, 1)
                dve.wait_ge(ya_d.sem, ya_d.at(t, 8))
                tt(flatA, flatA, v("lnx_b"), ALU.add).then_inc(ya_d.sem, 1)
                dve.wait_ge(ya_d.sem, ya_d.at(t, 9))
                tt(flatA, flatA, t1[:], ALU.add).then_inc(ya_d.sem, 1)
                dve.wait_ge(gate_a.sem, gate_a.at(t))
                dve.wait_ge(ya_d.sem, ya_d.at(t, 10))
                tt(flatA, flatA, gate[u][:], ALU.mult).then_inc(ya_d.sem, 1)

            def sampled_states(t, u, c):
                blk = c[0:TS, MC_BLK:MC_BLK + DB]
                dve.wait_ge(u_a.sem, u_a.at(t))
                dve.wait_ge(exp_a.sem, exp_a.at(t))
                def spread(j):
                    if j >= 2:
                        dve.wait_ge(new_p.sem, j - 1)
                    left, right = (X, ET) if j % 2 == 0 else (M, MT)
                    for o in range(2):
                        if j < 4:
                            h = 2 * j + o
                            for dst, src in ((left[o], usb[0:TS, h]), (right[o], sh[u][0:TS, 2 * WA + h * NA:2 * WA + (h + 1) * NA])):
                                out = dst[0:TS].rearrange("p a (c d) -> p (a c) d", d=NA)
                                m = tt(out, src.unsqueeze(1).broadcast_to([TS, DB, NA]), blk.unsqueeze(2).broadcast_to([TS, DB, NA]), ALU.mult)
                        else:
                            h, half = 2 * (j % 2) + o, (j - 4) // 2
                            src = curB[u][0:TS, 512 + h * NV:512 + (h + 1) * NV].unsqueeze(1).broadcast_to([TS, 4, NV])
                            m = tt(left[o][0:TS], src, blk[:, 4 * half:4 * half + 4].unsqueeze(2).broadcast_to([TS, 4, NV]), ALU.mult)
                    m.then_inc(blk_d.sem, 1)

                spread(0)
                for j in range(8):
                    if j + 1 < 8:
                        spread(j + 1)
                    dve.wait_ge(new_p.sem, j + 1)
                    bank = B[5] if j % 2 == 0 else B[0]
                    if j < 4:
                        st = s0T[:, :, j]
                        tt(st, bank[:].rearrange("p (b d) -> p b d", b=DB), st, ALU.add).then_inc(sum_d.sem, 1)
                        dve.wait_ge(sum_d.sem, j + 1)
                        tt(st, st, over(em[u][:, j], NA), ALU.mult).then_inc(new_d.sem, 1)
                    else:
                        q, half = j % 2, (j - 4) // 2
                        st = r0[:, 4 * half:4 * half + 4, q]
                        stt(st, st, c[:, MC_CDEC + q:MC_CDEC + q + 1], bank[:].rearrange("p (b d) -> p b d", b=4), ALU.mult, ALU.add).then_inc(new_d.sem, 1)

            def start():
                nc.vector.memset(S[:], 0.0).then_inc(s_zero.sem, 1)
                nc.vector.memset(R[:], 0.0).then_inc(s_zero.sem, 1)
                nc.vector.memset(S0[:], 0.0).then_inc(s_zero.sem, 1)
                dve.wait_ge(s_zero.sem, 3)
                state_d.prime(dve)
                ya_d.prime(dve)
                const.wait(dve)
                f_mix1(0, 0, 0)
                f_mix2(0, 0)
                f_mix3(0, 0)
                f_lora(0, 0)
                f_kk1(0, 0)
                f_z(0)
                f_lwa(0)
                f_kk2(0, 0)
                f_rot(0, 0, 0)
                f_scale(0, 0)

            def body(t, u, i):
                grams(t, u, mc, False)
                if later(t, 1):
                    norms1(t - 1)
                f_mix1(t + 1, 1 - u, i + u)
                level(t, 1)
                f_mix2(t + 1, 1 - u)
                level(t, 2)
                f_mix3(t + 1, 1 - u)
                level(t, 3)
                f_lora(t + 1, 1 - u)
                f_kk1(t + 1, 1 - u)
                if later(t, 1):
                    norms2(t - 1)
                level(t, 4)
                f_z(t + 1)
                if later(t, 1):
                    norms3(t - 1, 1 - u)
                level(t, 5)
                f_lwa(t + 1)
                f_kk2(t + 1, 1 - u)
                level(t, 6)
                f_rot(t + 1, 1 - u, i + u)
                f_scale(t + 1, 1 - u)
                tail(t, u, mc, False)

            def end():
                grams(NT, 0, mcs, True)
                norms1(NT - 1)
                level(NT, 1, LEVELS_S - 1)
                norms2(NT - 1)
                norms3(NT - 1, 1)
                level(NT, 2, LEVELS_S - 1)
                tail(NT, 0, mcs, True)
                norms1(NT)
                norms2(NT)
                norms3(NT, 0)
                sampled_states(NT, 0, mcs)

            tiles(dve, start, body, end)

        @block.gpsimd
        def _(pool):
            tt = nc.gpsimd.tensor_tensor

            def f_rn(t):
                pool.wait_ge(kk_d.sem, kk_d.at(t, 3))
                tt(rn[:], ss[:], halves[:, 0:HA], ALU.pow).then_inc(rn_g.sem, 1)

            def mask_e(t, g, j, c):
                m = c[:, MC_LVL + j * P:MC_LVL + (j + 1) * P].unsqueeze(1).broadcast_to([P, 4, P])
                tt(ET[g][:], G[:, 4 * g:4 * g + 4, 0], m, ALU.mult).then_inc(et_g.sem, 1)

            def first(t, c):
                m0 = c[:, MC_LVL:MC_LVL + P].unsqueeze(1).broadcast_to([P, 4, P])
                for g in range(2):
                    pool.wait_ge(gram_d.sem, gram_d.at(t, 4 * g + 4))
                    mask_e(t, g, 1, c)
                    tt(MT[g][:], G[:, 4 * g:4 * g + 4, 0], m0, ALU.mult).then_inc(mt0_g.sem, 1)
                    pool.wait_ge(mt0_g.sem, mt0_g.at(t, 2 * g + 1))
                    tt(MT[g][:], MT[g][:], ident[:].unsqueeze(1).broadcast_to([P, 4, P]), ALU.add).then_inc(mt0_g.sem, 1)

            def level(t, j, c):
                for g in range(2):
                    pool.wait_ge(x_p.sem, x_p.at(t, 2 * (j - 2) + g + 1))
                    mask_e(t, g, j, c)

            def tail(t, u):
                pool.wait_ge(sil_a.sem, sil_a.at(t))
                tt(sg[:], sg[:], one[:].broadcast_to([P, WA]), ALU.add).then_inc(sil1_g.sem, 1)
                pool.wait_ge(sil1_g.sem, sil1_g.at(t))
                tt(sg[:], sg[:], curB[u][:, 1024:1536], ALU.mult).then_inc(sil_g.sem, 1)

            def norms(t):
                pool.wait_ge(yb_d.sem, yb_d.at(t, 5))
                tt(rs[:, HA:], var[:, HA:], halves[:, 0:HB], ALU.pow).then_inc(rs_g.sem, 1)
                pool.wait_ge(ya_d.sem, ya_d.at(t, 6))
                tt(rs[:, 0:HA], var[:, 0:HA], halves[:, 0:HA], ALU.pow).then_inc(rs_g.sem, 1)

            def start():
                nc.gpsimd.memset(halves[:], -0.5).then_inc(half_set.sem, 1)
                nc.gpsimd.memset(one[:], 1.0).then_inc(half_set.sem, 1)
                pool.wait_ge(half_set.sem, 2)
                const.wait(pool)
                f_rn(0)

            def body(t, u, i):
                first(t, mc)
                level(t, 2, mc)
                if later(t, 1):
                    norms(t - 1)
                level(t, 3, mc)
                level(t, 4, mc)
                f_rn(t + 1)
                level(t, 5, mc)
                level(t, 6, mc)
                tail(t, u)

            def end():
                first(NT, mcs)
                level(NT, 2, mcs)
                norms(NT - 1)
                tail(NT, 0)
                norms(NT)

            tiles(pool, start, body, end)

        ex.close()
        nc.clear_and_free_semaphores([s.sem for s in signals])
        nc.all_engine_barrier()



def normalize(dve, s, t, base, x, stats, mv, rs, rs_done, out, g, b, eps=LN_EPS):
    for half in range(2):
        dve.bn_stats(stats[:, 6 * half:6 * half + 6], x[:, 512 * half:512 * half + 512]).then_inc(s.sem, 1)
    dve.wait_ge(s.sem, s.at(t, base + 2))
    dve.memset(mv[:, 3:4], 0.0)
    dve.bn_aggr(mv[:, 0:2], stats[:]).then_inc(s.sem, 1)
    dve.wait_ge(s.sem, s.at(t, base + 3))
    dve.tensor_scalar(mv[:, 2:3], mv[:, 1:2], eps, None, ALU.add).then_inc(s.sem, 1)
    dve.scalar_tensor_tensor(out, x, mv[:, 0:1], g, ALU.subtract, ALU.mult).then_inc(s.sem, 1)
    dve.wait_ge(s.sem, s.at(t, base + 5))
    dve.wait_ge(rs_done.sem, rs_done.at(t, 1))
    dve.scalar_tensor_tensor(out, out, rs, b, ALU.mult, ALU.add).then_inc(s.sem, 1)


def merge(nc, soft, x_rows, shift_p, shift_s, yT_d, w_out, w_router, vec2, ident_d, ident, halves, h_rows, h_dram, logits):
    pieces = 4
    kp = KD // pieces
    with ExitStack() as ctx:
        def sb(name, shape):
            return ctx.enter_context(nc.sbuf_tensor("mg_" + name, shape, F32))

        def half_precision(name, shape):
            return ctx.enter_context(nc.sbuf_tensor("mg_" + name, shape, F16))

        def two(name, shape):
            return [sb(f"{name}{u}", shape) for u in range(2)]

        def sig(name, per, by=1, primed=False):
            return Signal(nc, ctx, "mg_" + name, per, by, primed)

        wo = sb("wo", [P, KD, D])
        woh, wol = half_precision("woh", [P, KD, D]), half_precision("wol", [P, KD, D])
        yh, yl = ([half_precision(f"{n}{u}", [P, KD, P]) for u in range(2)] for n in ("yh", "yl"))
        wr = sb("wr", [P, KD, NG + NE])
        gb = sb("gb", [P, 2 * D + NG + NE])
        yT, x, h, hs = two("yT", [P, KD, P]), two("x", [P, D]), two("h", [P, D]), two("hs", [P, KD, P])
        stats, mv, rs = sb("stats", [P, 12]), sb("mv", [P, 4]), sb("rs", [P, 1])
        B = [ctx.enter_context(nc.psum_tensor(f"mg_ps{b}", [P, 512], F32)) for b in range(8)]

        half_set = sig("half_set", 1)
        stored = sig("stored", 1, 16)
        const_in = sig("const_in", 3, 16)
        wo_in = [sig(f"wo_in{half}", 1, 16) for half in range(2)]
        yT_in = [Signal(nc, soft, f"mg_yT_in{u}", 1, 16) for u in range(2)]
        x_in = [Signal(nc, soft, f"mg_x_in{u}", 1, 16) for u in range(2)]
        wo_hi, wo_lo = sig("wo_hi", 1), sig("wo_lo", 1)
        y_hi, y_lo = sig("y_hi", 1), sig("y_lo", 1)
        mix_p = sig("mix_p", 2)
        h_d = sig("h_d", 8)
        rs_g = sig("rs_g", 1)
        turn_p = sig("turn_p", 2)
        rows_a = sig("rows_a", 1)
        turn_a = sig("turn_a", 2, primed=True)
        router_p = sig("router_p", 1, primed=True)
        logit_d = sig("logit_d", 1, primed=True)

        with nc.Block() as block:

            def loop(eng, tile):
                with eng.Fori(0, NT // 2 - 1) as i:
                    for u in range(2):
                        tile(2 * i + u, u, i, True)
                tile(NT - 2, 0, NT // 2 - 1, True)
                tile(NT - 1, 1, NT // 2 - 1, False)
                tile(NT, 0, NT // 2, False)

            def pieces_of(half):
                for c in range(pieces):
                    r, cols = slice(kp * c, kp * c + kp), slice(512 * half, 512 * half + 512)
                    yield woh[:, r, cols], wol[:, r, cols], wo[:, r, cols], pieces * half + c

            @block.sync
            def _(sp):
                for half in range(2):
                    if half == 1:
                        sp.wait_ge(yT_in[0].sem, 16)
                    sp.dma_start(wo[:, :, 512 * half:512 * half + 512], w_out[:, :, 512 * half:512 * half + 512]).then_inc(wo_in[half].sem, 16)
                for dst, src in ((gb, vec2.broadcast_to([P, 2 * D + NG + NE])), (ident, ident_d), (wr, w_router)):
                    sp.dma_start(dst[:], src).then_inc(const_in.sem, 16)

                sp.dma_start(shift_p, x_rows[SEQ:SEQ + 1]).then_inc(stored.sem, 16)
                last = x_rows[SAMPLE0:SAMPLE0 + DB * (DS + 1)].rearrange("(b t) c -> b t c", b=DB)[:, DS]
                sp.dma_start(shift_s, last).then_inc(stored.sem, 16)

                def store(t, u):
                    sp.wait_ge(rows_a.sem, rows_a.at(t))
                    sp.dma_start(h_dram[t], h_rows[:, t]).then_inc(stored.sem, 16)
                with sp.Fori(0, NT) as t:
                    store(t, 0)
                store(NT, 0)
                sp.wait_ge(stored.sem, 16 * (TILES + 2))

            @block.gpsimd
            def _(pool):
                nc.gpsimd.memset(halves[:], -0.5).then_inc(half_set.sem, 1)
                pool.wait_ge(half_set.sem, 1)

                def load(t, u):
                    pool.dma_start(yT[u][:], yT_d[t]).then_inc(yT_in[u].sem, 16)
                    if isinstance(t, int) and t == NT:
                        pool.dma_start(x[u][0:TS], x_rows[SAMPLE0:SAMPLE0 + DB * (DS + 1)].rearrange("(b t) c -> b t c", b=DB)[:, 1:]).then_inc(x_in[u].sem, 16)
                    else:
                        pool.dma_start(x[u][:], x_rows[1:1 + SEQ].rearrange("(n p) c -> n p c", p=P)[t]).then_inc(x_in[u].sem, 16)

                def power(t):
                    pool.wait_ge(h_d.sem, h_d.at(t, 6))
                    nc.gpsimd.tensor_tensor(rs[:], mv[:, 2:3], halves[:], ALU.pow).then_inc(rs_g.sem, 1)

                load(0, 0)
                load(1, 1)
                with pool.Fori(0, NT // 2 - 1) as i:
                    for u in range(2):
                        power(2 * i + u)
                        load(2 * i + u + 2, u)
                power(NT - 2)
                load(NT, 0)
                power(NT - 1)
                power(NT)

            @block.tensor
            def _(pe):
                def mix(t, u, i):
                    pe.wait_ge(y_lo.sem, y_lo.at(t))
                    for half in range(2):
                        for k in range(KD):
                            if isinstance(t, int) and t == 0 and k % kp == 0:
                                pe.wait_ge(wo_lo.sem, pieces * half + k // kp + 1)
                            for n, (x, w) in enumerate(((yh, woh), (yh, wol), (yl, woh))):
                                m = nc.tensor.matmul(B[2 * u + half][:], x[u][:, k], w[:, k, 512 * half:512 * half + 512], start=(k == 0 and n == 0), stop=(k == KD - 1 and n == 2))
                        m.then_inc(mix_p.sem, 1)

                def turn(t, u):
                    pe.wait_ge(h_d.sem, h_d.at(t))
                    for half in range(2):
                        pe.wait_ge(turn_a.sem, turn_a.at(t, 0))
                        for q in range(4):
                            k = 4 * half + q
                            m = nc.tensor.transpose(B[4 + half][:, q * P:(q + 1) * P], h[u][:, k * P:(k + 1) * P], ident[:])
                        m.then_inc(turn_p.sem, 1)

                def router(t, u):
                    pe.wait_ge(turn_a.sem, turn_a.at(t))
                    pe.wait_ge(logit_d.sem, logit_d.at(t, 0))
                    for k in range(KD):
                        m = nc.tensor.matmul(B[6][:, 0:NG + NE], hs[u][:, k], wr[:, k], start=(k == 0), stop=(k == KD - 1))
                    m.then_inc(router_p.sem, 1)

                router_p.prime(pe)
                mix(0, 0, 0)
                pe.wait_ge(const_in.sem, const_in.at(0))
                with pe.Fori(0, NT // 2) as i:
                    mix(2 * i + 1, 1, i)
                    turn(2 * i, 0)
                    router(2 * i, 0)
                    mix(2 * i + 2, 0, i + 1)
                    turn(2 * i + 1, 1)
                    router(2 * i + 1, 1)
                turn(NT, 0)
                router(NT, 0)

            @block.scalar
            def _(act):
                def split(t, u, i):
                    act.wait_ge(yT_in[u].sem, (i + 1) * 16)
                    if not (isinstance(t, int) and t < 2):
                        act.wait_ge(mix_p.sem, mix_p.at(t - 2))
                    split_hi(nc.scalar, yh[u][:], yT[u][:], 1.0).then_inc(y_hi.sem, 1)

                def tile(t, u, i, ahead):
                    act.wait_ge(h_d.sem, h_d.at(t))
                    nc.scalar.copy(h_rows[:, t], h[u][:]).then_inc(rows_a.sem, 1)
                    if ahead:
                        split(t + 2, u, i + 1)
                    act.wait_ge(router_p.sem, router_p.at(t, 0))
                    for half in range(2):
                        act.wait_ge(turn_p.sem, turn_p.at(t, half + 1))
                        nc.scalar.copy(hs[u][:, 4 * half:4 * half + 4], B[4 + half][:].rearrange("p (k t) -> p k t", t=P)).then_inc(turn_a.sem, 1)

                turn_a.prime(act)
                for half in range(2):
                    act.wait_ge(wo_in[half].sem, 16)
                    for hi, _, w, c in pieces_of(half):
                        split_hi(nc.scalar, hi, w, W_SCALE).then_inc(wo_hi.sem, 1)
                        if c % pieces == 1:
                            split(half, half, 0)
                loop(act, tile)

            @block.vector
            def _(dve):
                def split(t, u):
                    dve.wait_ge(y_hi.sem, y_hi.at(t))
                    split_lo(nc.vector, yl[u][:], yT[u][:], 1.0, yh[u][:]).then_inc(y_lo.sem, 1)

                def tile(t, u, i, ahead):
                    dve.wait_ge(x_in[u].sem, (i + 1) * 16)
                    dve.wait_ge(turn_a.sem, turn_a.at(t, 0))
                    for half in range(2):
                        c = slice(512 * half, 512 * half + 512)
                        dve.wait_ge(mix_p.sem, mix_p.at(t, half + 1))
                        nc.vector.scalar_tensor_tensor(h[u][:, c], x[u][:, c], ALPHA * W_SCALE, B[2 * u + half][:], ALU.mult, ALU.add).then_inc(h_d.sem, 1)
                    dve.wait_ge(h_d.sem, h_d.at(t, 2))
                    normalize(nc.vector, h_d, t, 2, h[u][:], stats, mv, rs[:], rs_g, h[u][:], gb[:, 0:D], gb[:, D:2 * D], LN_EPS * W_SCALE ** 2)
                    if ahead:
                        split(t + 2, u)
                    dve.wait_ge(router_p.sem, router_p.at(t))
                    nc.vector.tensor_tensor(logits[:, t], B[6][:, 0:NG + NE], gb[:, 2 * D:], ALU.add).then_inc(logit_d.sem, 1)

                logit_d.prime(dve)
                for half in range(2):
                    for hi, lo, w, c in pieces_of(half):
                        dve.wait_ge(wo_hi.sem, c + 1)
                        split_lo(nc.vector, lo, w, W_SCALE, hi).then_inc(wo_lo.sem, 1)
                        if c % pieces == 1:
                            split(half, half)
                dve.wait_ge(const_in.sem, const_in.at(0))
                loop(dve, tile)


def route(nc, soft, weights, logits, h_rows, rconst, slot_u, weight, tile_expert, sorted_h):
    n = TILES
    with ExitStack() as ctx:
        def sb(name, shape, dt=F32):
            return ctx.enter_context(nc.sbuf_tensor("rt_" + name, shape, dt))

        rc = sb("rc", [P, RC_N])
        ones = sb("ones", [P, P])
        cmax, z, gp, pm, v1, v2, e, w1 = (sb(x, [P, n]) for x in ("cmax", "z", "gp", "pm", "v1", "v2", "e", "w1"))
        c, ex, pr, oh, f4, oh1, oh2, d = (sb(x, [P, n, 4]) for x in ("c", "ex", "pr", "oh", "f4", "oh1", "oh2", "d"))
        prod = sb("prod", [P, n, 4, 4])
        E = sb("E", [P, 2, n, NG, EPG])
        O = sb("O", [P, n, NE])
        pre = sb("pre", [P, n + 1, NE])
        slot = sb("slot", [P, n, NE])
        hit = sb("hit", [P, n, NE])
        slot_f = sb("slot_f", [P, 2, n])
        cmp = sb("cmp", [P, NE, n])
        ntl, tb, tend = sb("ntl", [P, NE]), sb("tb", [P, NE]), sb("tend", [P, NE])
        tri16 = sb("tri16", [P, NE, NE])
        cmp2 = sb("cmp2", [P, SLOTS // P, NE])
        te = sb("te", [P, SLOTS // P])
        ps = [ctx.enter_context(nc.psum_tensor(f"rt_ps{b}", [P, 512], F32)) for b in range(2)]
        const_in = Signal(nc, ctx, "rt_const_in", 1, 16)
        step = Signal(nc, ctx, "rt_step", 1)
        exp_a = Signal(nc, ctx, "rt_exp_a", 1)
        count_p = Signal(nc, ctx, "rt_count_p", 1)
        slots_d = Signal(nc, ctx, "rt_slots_d", 1)
        scattered = Signal(nc, soft, "rt_scattered", 2 * n, 16)
        prio = rc[:, RC_PRIO:RC_PRIO + 4]

        def over(x):
            return x.unsqueeze(2).broadcast_to([P, n, 4])

        with nc.Block() as block:

            @block.sync
            def _(sp):
                sp.dma_start(rc[:], rconst).then_inc(const_in.sem, 16)
                for j in range(weights.early):
                    weights.load(sp, j, j)

            @block.scalar
            def _(act):
                act.wait_ge(step.sem, C_READY)
                nc.scalar.activation(ex[:], c[:], ACT.Exp).then_inc(exp_a.sem, 1)
                act.wait_ge(step.sem, V2_READY)
                nc.scalar.activation(e[:], v2[:], ACT.Exp).then_inc(exp_a.sem, 1)

            @block.tensor
            def _(pe):
                pe.wait_ge(step.sem, O_READY)
                rows = O[:].rearrange("p n e -> p (n e)")
                nc.tensor.matmul(ps[0][:, 0:n * NE], rc[:, RC_TRI:RC_TRI + P], rows, start=True, stop=True).then_inc(count_p.sem, 1)
                nc.tensor.matmul(ps[1][:, 0:n * NE], ones[:], rows, start=True, stop=True).then_inc(count_p.sem, 1)

            @block.gpsimd
            def _(pool):
                pool.wait_ge(slots_d.sem, 1)
                for t in range(n):
                    rows = P if t < NT else TS
                    for k in range(2):
                        where = bass.IndirectOffsetOnAxis(ap=slot_u[0:rows, k, t:t + 1], axis=0)
                        pool.indirect_dma_start(out=sorted_h, out_offset=where, in_=h_rows[0:rows, t], in_offset=None).then_inc(scattered.sem, 16)
                pool.wait_ge(scattered.sem, scattered.at(1, 0))

            @block.vector
            def _(dve):
                tt, ts, red = nc.vector.tensor_tensor, nc.vector.tensor_scalar, nc.vector.tensor_reduce
                done = [0]

                def then(ins):
                    done[0] += 1
                    ins.then_inc(step.sem, 1)
                    dve.wait_ge(step.sem, done[0])

                def first_max(out, x, floor):
                    then(tt(pr[:], x, floor, ALU.is_ge))
                    then(tt(pr[:], pr[:], prio.unsqueeze(1).broadcast_to([P, n, 4]), ALU.mult))
                    then(red(pm[:], pr[:], AX, ALU.max))
                    then(tt(out, pr[:], over(pm[:]), ALU.is_equal))

                dve.wait_ge(const_in.sem, 16)
                coarse = logits[:, :, 0:NG]
                fine = logits[:, :, NG:].rearrange("p n (g j) -> p n g j", g=NG)
                then(red(cmax[:], coarse, AX, ALU.max))
                then(tt(c[:], coarse, over(cmax[:]), ALU.subtract))
                assert done[0] == C_READY
                first_max(oh[:], coarse, over(cmax[:]))
                then(tt(prod[:], fine, oh[:].unsqueeze(3).broadcast_to([P, n, 4, 4]), ALU.mult))
                then(red(f4[:], prod[:].rearrange("p n g j -> p n j g"), AX, ALU.add))
                then(red(v1[:], f4[:], AX, ALU.max))
                first_max(oh1[:], f4[:], over(v1[:]))
                then(tt(d[:], f4[:], over(v1[:]), ALU.subtract))
                then(nc.vector.scalar_tensor_tensor(d[:], oh1[:], -3e38, d[:], ALU.mult, ALU.add))
                then(red(v2[:], d[:], AX, ALU.max))
                assert done[0] == V2_READY
                first_max(oh2[:], d[:], over(v2[:]))
                for k, o in enumerate((oh1, oh2)):
                    then(tt(E[:, k], oh[:].unsqueeze(3).broadcast_to([P, n, 4, 4]), o[:].unsqueeze(2).broadcast_to([P, n, 4, 4]), ALU.mult))
                flat = [E[:, k].rearrange("p n g j -> p n (g j)") for k in range(2)]
                then(tt(O[:], flat[0], flat[1], ALU.add))
                then(tt(O[:], O[:], rc[:, RC_VALID:RC_VALID + n].unsqueeze(2).broadcast_to([P, n, NE]), ALU.mult))
                then(nc.vector.memset(ones[:], 1.0))
                assert done[0] == O_READY
                then(nc.vector.memset(pre[:, 0], 0.0))
                dve.wait_ge(count_p.sem, 2)
                for t in range(n):
                    then(tt(pre[:, t + 1], ps[1][:, t * NE:(t + 1) * NE], pre[:, t], ALU.add))
                thr = rc[:, RC_THR:RC_THR + n].unsqueeze(1).broadcast_to([P, NE, n])
                then(tt(cmp[:], pre[:, n].unsqueeze(2).broadcast_to([P, NE, n]), thr, ALU.is_gt))
                then(red(ntl[:], cmp[:], AX, ALU.add))
                before = rc[:, RC_LT:RC_LT + NE * NE].rearrange("p (a b) -> p a b", a=NE)
                then(tt(tri16[:], before, ntl[:].unsqueeze(1).broadcast_to([P, NE, NE]), ALU.mult))
                then(red(tb[:], tri16[:], AX, ALU.add))
                then(nc.vector.scalar_tensor_tensor(tend[:], tb[:], float(NE), ntl[:], ALU.add, ALU.add))
                then(ts(tb[:], tb[:], float(P), float((NE - 1) * P), ALU.mult, ALU.add))
                first_slot = rc[:, RC_SLOT:RC_SLOT + NE]
                then(tt(tb[:], tb[:], first_slot, ALU.subtract))
                then(tt(slot[:], ps[0][:, 0:n * NE].rearrange("p (n e) -> p n e", n=n), pre[:, 0:n], ALU.add))
                then(ts(hit[:], slot[:], float(P), None, ALU.is_ge))
                then(tt(hit[:], hit[:], tb[:].unsqueeze(1).broadcast_to([P, n, NE]), ALU.mult))
                then(tt(slot[:], slot[:], hit[:], ALU.add))
                then(tt(slot[:], slot[:], first_slot.unsqueeze(1).broadcast_to([P, n, NE]), ALU.add))
                for k in range(2):
                    then(tt(hit[:], slot[:], flat[k], ALU.mult))
                    then(red(slot_f[:, k], hit[:], AX, ALU.add))
                then(nc.vector.tensor_copy(slot_u[:], slot_f[:]))
                nc.vector.nop().then_inc(slots_d.sem, 1)
                tiles_at = rc[:, RC_TILE:RC_TILE + SLOTS // P].unsqueeze(2).broadcast_to([P, SLOTS // P, NE])
                then(tt(cmp2[:], tiles_at, tend[:].unsqueeze(1).broadcast_to([P, SLOTS // P, NE]), ALU.is_ge))
                then(red(te[:], cmp2[:], AX, ALU.add))
                then(nc.vector.scalar_tensor_tensor(te[:], te[:], float(NE - 1), rc[:, RC_OWN:RC_OWN + SLOTS // P], ALU.min, ALU.add))
                then(nc.vector.tensor_copy(tile_expert[:], te[:]))
                dve.wait_ge(exp_a.sem, 2)
                then(red(z[:], ex[:], AX, ALU.add))
                then(nc.vector.reciprocal(gp[:], z[:]))
                then(ts(w1[:], e[:], 1.0, None, ALU.add))
                then(nc.vector.reciprocal(w1[:], w1[:]))
                then(nc.vector.scalar_tensor_tensor(weight[:, 0], w1[:], 0.5, gp[:], ALU.mult, ALU.mult))
                then(tt(weight[:, 1], e[:], weight[:, 0], ALU.mult))


class ExpertWeights:

    ahead = 4
    early = 2

    def __init__(self, nc, ctx, w13_d, w2_d):
        def ring(name, shape):
            return [ctx.enter_context(nc.sbuf_tensor(f"ex_{name}{u}", shape, F32)) for u in range(self.ahead)]

        self.w13_d, self.w2_d = w13_d, w2_d
        self.w13, self.w2 = ring("w13", [P, KD, 2 * FE]), ring("w2", [P, FE // P, D])
        self.w13_in = [Signal(nc, ctx, f"ex_w13_in{u}", 1, 16) for u in range(self.ahead)]
        self.w2_in = [Signal(nc, ctx, f"ex_w2_in{u}", 1, 16) for u in range(self.ahead)]

    def load13(self, eng, u, expert):
        eng.dma_start(self.w13[u][:], self.w13_d[expert]).then_inc(self.w13_in[u].sem, 16)

    def load2(self, eng, u, expert):
        eng.dma_start(self.w2[u][:], self.w2_d[expert]).then_inc(self.w2_in[u].sem, 16)

    def load(self, eng, u, expert):
        self.load13(eng, u, expert)
        self.load2(eng, u, expert)


def experts(nc, weights, ident, tile_expert, sorted_h, sorted_y, const, w_ple, w_pgate, vec3):
    NJ = SLOTS // P
    NF = FE // P
    AHEAD, w13, w2, w13_in, w2_in = weights.ahead, weights.w13, weights.w2, weights.w13_in, weights.w2_in
    assert NJ % AHEAD == 0 and NJ // AHEAD == KD
    sh, sy = (x.rearrange("(j p) d -> j p d", p=P) for x in (sorted_h, sorted_y))
    with ExitStack() as ctx:
        def ring(n, name, shape):
            return [ctx.enter_context(nc.sbuf_tensor(f"ex_{name}{u}", shape, F32)) for u in range(n)]

        def sig(name, per, by=1, primed=False):
            return Signal(nc, ctx, "ex_" + name, per, by, primed)

        x = ring(AHEAD, "x", [P, D])
        xT, th, hid, hidT, y = (ring(2, "xT", [P, KD, P]), ring(2, "th", [P, FE]), ring(2, "hid", [P, FE]),
                                ring(2, "hidT", [P, NF, P]), ring(2, "y", [P, D]))
        B = [ctx.enter_context(nc.psum_tensor(f"ex_ps{b}", [P, 512], F32)) for b in range(7)]
        x_in = [sig(f"x_in{u}", 1, 16) for u in range(AHEAD)]
        y_out = [sig(f"y_out{u}", 1, 16, primed=True) for u in range(2)]
        turn_p = sig("turn_p", 2)
        turn_a = sig("turn_a", 2)
        up_p = sig("up_p", 1)
        th_a = sig("th_a", 1)
        hid_d = sig("hid_d", 2)
        hidT_p = sig("hidT_p", 1)
        hidT_a = sig("hidT_a", 1)
        down_p = sig("down_p", 2)
        y_a = sig("y_a", 1)
        y_d = sig("y_d", 1)

        with nc.Block() as block:

            def tiles(eng, step, turn=None):
                with eng.Fori(0, NJ // AHEAD - 1) as i:
                    for b in range(1, AHEAD + 1):
                        step(AHEAD * i + b, b, i)
                    if turn is not None:
                        turn(i)
                for b in range(1, AHEAD):
                    step(NJ - AHEAD + b, b, NJ // AHEAD - 1)

            @block.sync
            def _(sp):
                def expert_of(j):
                    row = tile_expert[0:1, j:j + 1] if isinstance(j, int) else tile_expert[0:1, bass.ds(j, 1)]
                    return sp.value_load(row, min_val=0, max_val=NE - 1)

                def store(j, u):
                    sp.wait_ge(y_a.sem, y_a.at(j))
                    sp.wait_ge(y_d.sem, y_d.at(j))
                    sp.dma_start(sy[j], y[u][:]).then_inc(y_out[u].sem, 16)

                for u in range(2):
                    y_out[u].prime(sp)
                for u in range(AHEAD):
                    sp.dma_start(x[u][:], sh[u]).then_inc(x_in[u].sem, 16)
                    if u >= weights.early:
                        weights.load(sp, u, u)
                const.load(sp, w_ple, vec3)
                with sp.Fori(0, NJ // AHEAD - 1) as i:
                    const.load_part(sp, w_pgate, i)
                    for u in range(AHEAD):
                        j = AHEAD * i + u
                        expert = expert_of(j + AHEAD)
                        sp.wait_ge(turn_p.sem, turn_p.at(j))
                        sp.dma_start(x[u][:], sh[j + AHEAD]).then_inc(x_in[u].sem, 16)
                        sp.wait_ge(up_p.sem, up_p.at(j))
                        weights.load13(sp, u, expert)
                        sp.wait_ge(down_p.sem, down_p.at(j))
                        weights.load2(sp, u, expert)
                        store(j, u % 2)
                const.load_part(sp, w_pgate, KD - 1)
                for u in range(AHEAD):
                    store(NJ - AHEAD + u, u % 2)
                for u in range(2):
                    sp.wait_ge(y_out[u].sem, y_out[u].at(NJ // 2 - 1))

            @block.tensor
            def _(pe):
                mm = nc.tensor.matmul

                def turn(j, b, i):
                    w, u = b % AHEAD, b % 2
                    pe.wait_ge(x_in[w].sem, (i + b // AHEAD + 1) * 16)
                    for half in range(2):
                        if not (isinstance(j, int) and j == 0):
                            pe.wait_ge(turn_a.sem, turn_a.at(j - 1, half + 1))
                        for q in range(4):
                            k = 4 * half + q
                            m = nc.tensor.transpose(B[2 + half][:, q * P:(q + 1) * P], x[w][:, k * P:(k + 1) * P], ident[:])
                        m.then_inc(turn_p.sem, 1)

                def up(j, b, i):
                    w, u = b % AHEAD, b % 2
                    pe.wait_ge(w13_in[w].sem, (i + b // AHEAD + 1) * 16)
                    pe.wait_ge(turn_a.sem, turn_a.at(j))
                    for k in range(KD):
                        m = mm(B[u][:], xT[u][:, k], w13[w][:, k], start=(k == 0), stop=(k == KD - 1))
                    m.then_inc(up_p.sem, 1)

                def down(j, b, i):
                    w, u = b % AHEAD, b % 2
                    pe.wait_ge(w2_in[w].sem, (i + b // AHEAD + 1) * 16)
                    pe.wait_ge(hidT_a.sem, hidT_a.at(j))
                    for half in range(2):
                        s = (y_a, y_d)[half]
                        if not (isinstance(j, int) and j == 0):
                            pe.wait_ge(s.sem, s.at(j, 0))
                        for f in range(NF):
                            m = mm(B[5 + half][:], hidT[u][:, f], w2[w][:, f, 512 * half:512 * half + 512], start=(f == 0), stop=(f == NF - 1))
                        m.then_inc(down_p.sem, 1)

                def turn_hid(j, b):
                    u = b % 2
                    pe.wait_ge(hid_d.sem, hid_d.at(j))
                    for f in range(NF):
                        m = nc.tensor.transpose(B[4][:, f * P:(f + 1) * P], hid[u][:, f * P:(f + 1) * P], ident[:])
                    m.then_inc(hidT_p.sem, 1)

                def step(j, b, i):
                    up(j, b, i)
                    if not (isinstance(j, int) and j == NJ - 1):
                        turn(j + 1, b + 1, i)
                    down(j - 1, b - 1, i)
                    turn_hid(j, b)

                turn(0, 0, 0)
                up(0, 0, 0)
                turn(1, 1, 0)
                turn_hid(0, 0)
                tiles(pe, step)
                down(NJ - 1, AHEAD - 1, NJ // AHEAD - 1)

            def y_stored(eng, j, b, i):
                eng.wait_ge(y_out[b % 2].sem, y_out[b % 2].at(i * (AHEAD // 2) + b // 2, 0))

            @block.scalar
            def _(act):
                def turned(j, b):
                    for half in range(2):
                        act.wait_ge(turn_p.sem, turn_p.at(j, half + 1))
                        nc.scalar.copy(xT[b % 2][:, 4 * half:4 * half + 4], B[2 + half][:].rearrange("p (k t) -> p k t", t=P)).then_inc(turn_a.sem, 1)

                def hidden(j, b):
                    act.wait_ge(up_p.sem, up_p.at(j))
                    nc.scalar.activation(th[b % 2][:], B[b % 2][:, 0:FE], ACT.Tanh, scale=0.5).then_inc(th_a.sem, 1)

                def hid_turned(j, b):
                    act.wait_ge(hidT_p.sem, hidT_p.at(j))
                    nc.scalar.copy(hidT[b % 2][:], B[4][:, 0:FE].rearrange("p (f t) -> p f t", t=P)).then_inc(hidT_a.sem, 1)

                def out(j, b, i):
                    y_stored(act, j, b, i)
                    act.wait_ge(down_p.sem, down_p.at(j, 1))
                    nc.scalar.copy(y[b % 2][:, 0:512], B[5][:]).then_inc(y_a.sem, 1)

                def step(j, b, i):
                    hidden(j, b)
                    if not (isinstance(j, int) and j == NJ - 1):
                        turned(j + 1, b + 1)
                    out(j - 1, b - 1, i)
                    hid_turned(j, b)

                turned(0, 0)
                hidden(0, 0)
                turned(1, 1)
                hid_turned(0, 0)
                tiles(act, step, lambda i: const.part_hi(act, nc.scalar, i))
                out(NJ - 1, AHEAD - 1, NJ // AHEAD - 1)
                const.rest_hi(act, nc.scalar)

            @block.vector
            def _(dve):
                def hidden(j, b):
                    u = b % 2
                    dve.wait_ge(th_a.sem, th_a.at(j))
                    nc.vector.scalar_tensor_tensor(th[u][:], th[u][:], 1.0, B[u][:, 0:FE], ALU.add, ALU.mult).then_inc(hid_d.sem, 1)
                    dve.wait_ge(hid_d.sem, hid_d.at(j, 1))
                    nc.vector.tensor_tensor(hid[u][:], th[u][:], B[u][:, FE:], ALU.mult).then_inc(hid_d.sem, 1)

                def out(j, b, i):
                    y_stored(dve, j, b, i)
                    dve.wait_ge(down_p.sem, down_p.at(j, 2))
                    nc.vector.tensor_copy(y[b % 2][:, 512:], B[6][:]).then_inc(y_d.sem, 1)

                def step(j, b, i):
                    hidden(j, b)
                    out(j - 1, b - 1, i)

                hidden(0, 0)
                tiles(dve, step, lambda i: const.part_lo(dve, nc.vector, i))
                out(NJ - 1, AHEAD - 1, NJ // AHEAD - 1)
                const.rest_lo(dve, nc.vector)


class FinishConstants:

    def __init__(self, nc, ctx, h_rows):
        KP = D_PLE // P
        bits = h_rows[:].bitcast(F16)
        self.wgh, self.wgl = bits[:, 0:KD, 0:D], bits[:, 0:KD, D:2 * D]
        self.wph, self.wpl = (ctx.enter_context(nc.sbuf_tensor(f"fi_wp{n}", [P, KP, D], F16)) for n in "hl")
        self.gb = ctx.enter_context(nc.sbuf_tensor("fi_gb", [P, 3 * D], F32))
        self.stage = ctx.enter_context(nc.sbuf_tensor("fi_stage", [P, D], F32))
        self.wp = ctx.enter_context(nc.sbuf_tensor("fi_wp", [P, KP, D], F32))
        self.loaded = Signal(nc, ctx, "fi_loaded", 1, 16)
        self.hi = Signal(nc, ctx, "fi_w_hi", 1)
        self.lo = Signal(nc, ctx, "fi_w_lo", 1, primed=True)

    def load(self, sp, w_ple, vec3):
        self.lo.prime(sp)
        sp.dma_start(self.gb[:], vec3.broadcast_to([P, 3 * D])).then_inc(self.loaded.sem, 16)
        sp.dma_start(self.wp[:], w_ple).then_inc(self.loaded.sem, 16)

    def load_part(self, sp, w_pgate, k):
        sp.wait_ge(self.lo.sem, self.lo.at(k, 0))
        block = w_pgate[:, k] if isinstance(k, int) else w_pgate[:, bass.ds(k, 1)].rearrange("p one d -> p (one d)")
        sp.dma_start(self.stage[:], block).then_inc(self.loaded.sem, 16)

    @staticmethod
    def block(w, k):
        return w[:, k] if isinstance(k, int) else w[:, bass.ds(k, 1)].rearrange("p one d -> p (one d)")

    def part_hi(self, act, scalar, k):
        act.wait_ge(self.loaded.sem, self.loaded.at(k + 2))
        split_hi(scalar, self.block(self.wgh, k), self.stage[:], W_SCALE).then_inc(self.hi.sem, 1)

    def part_lo(self, dve, vector, k):
        dve.wait_ge(self.hi.sem, self.hi.at(k))
        split_lo(vector, self.block(self.wgl, k), self.stage[:], W_SCALE, self.block(self.wgh, k)).then_inc(self.lo.sem, 1)

    def rest_hi(self, act, scalar):
        self.part_hi(act, scalar, KD - 1)
        split_hi(scalar, self.wph[:], self.wp[:], W_SCALE).then_inc(self.hi.sem, 1)

    def rest_lo(self, dve, vector):
        self.part_lo(dve, vector, KD - 1)
        dve.wait_ge(self.hi.sem, self.hi.at(KD))
        split_lo(vector, self.wpl[:], self.wp[:], W_SCALE, self.wph[:]).then_inc(self.lo.sem, 1)

    def wait(self, pe):
        pe.wait_ge(self.lo.sem, self.lo.at(KD))


def finish(nc, soft, const, ident, halves, h_dram, slot_u, weight, sorted_y, pT_d, out_d):
    with ExitStack() as ctx:
        def sb(name, shape, dt=F32):
            return ctx.enter_context(nc.sbuf_tensor("fi_" + name, shape, dt))

        def two(name, shape, dt=F32):
            return [sb(f"{name}{u}", shape, dt) for u in range(2)]

        def sig(name, per, by=1, primed=False):
            return Signal(nc, ctx, "fi_" + name, per, by, primed)

        KP = D_PLE // P
        wph, wpl, wgh, wgl, gb = const.wph, const.wpl, const.wgh, const.wgl, const.gb
        pT, h1, h, q = two("pT", [P, KP, P]), two("h1", [P, D]), two("h", [P, D]), two("q", [P, D])
        ph, pl = two("ph", [P, KP, P], F16), two("pl", [P, KP, P], F16)
        hh, hl = two("hh", [P, KD, P], F16), two("hl", [P, KD, P], F16)
        junk = sb("junk", [P, D])
        y0, y1 = two("y0", [P, D]), two("y1", [P, D])
        stats, mv, rs, rr = sb("stats", [P, 12]), sb("mv", [P, 4]), sb("rs", [P, 1]), sb("rr", [P, 1])
        ssq = two("ssq", [P, 1])
        var2 = sb("var2", [P, 1])
        turn_b, gate_b = ([ctx.enter_context(nc.psum_tensor(f"fi_{n}{b}", [P, 512], F32)) for b in range(2)] for n in ("turn", "gate"))
        ple_b = [ctx.enter_context(nc.psum_tensor(f"fi_ple{b}", [P, 512], F32)) for b in range(4)]
        pT_in = [sig(f"pT_in{u}", 1, 16) for u in range(2)]
        h1_in = [sig(f"h1_in{u}", 1, 16) for u in range(2)]
        y_in = [Signal(nc, soft, f"fi_y_in{u}", 2, 16) for u in range(2)]
        p_a, p_d = sig("p_a", 1), sig("p_d", 1)
        y0_a = sig("y0_a", 1)
        h_d = sig("h_d", 8)
        rs_g = sig("rs_g", 1)
        turn_p = sig("turn_p", 2)
        turn_a, turn_d = sig("turn_a", 2), sig("turn_d", 2)
        gate_p = sig("gate_p", 2)
        ple_p = sig("ple_p", 2)
        tanh_a = sig("tanh_a", 2)
        sq_a = sig("sq_a", 1)
        q_d = sig("q_d", 5, primed=True)
        rr_g = sig("rr_g", 1)
        out_s = [sig(f"out_s{u}", 1, 16, primed=True) for u in range(2)]

        with nc.Block() as block:

            def steps(eng, step):
                step(0, 0, 0, True)
                with eng.Fori(0, NT // 2 - 1) as i:
                    step(2 * i + 1, 1, i, True)
                    step(2 * i + 2, 0, i + 1, True)
                step(NT - 1, 1, NT // 2 - 1, True)
                step(NT, 0, NT // 2, False)

            def first(t):
                return isinstance(t, int) and t == 0

            @block.sync
            def _(sp):
                def load_p(t, u):
                    sp.dma_start(pT[u][:], pT_d[t]).then_inc(pT_in[u].sem, 16)

                def load_h(t, u):
                    sp.dma_start(h1[u][:], h_dram[t]).then_inc(h1_in[u].sem, 16)

                def store(t, u):
                    sp.wait_ge(q_d.sem, q_d.at(t))
                    sp.dma_start(out_d[t], q[u][:]).then_inc(out_s[u].sem, 16)

                for u in range(2):
                    out_s[u].prime(sp)
                    load_p(u, u)
                    load_h(u, u)
                with sp.Fori(0, NT // 2 - 1) as i:
                    for u in range(2):
                        t = 2 * i + u
                        sp.wait_ge(p_d.sem, p_d.at(t))
                        load_p(t + 2, u)
                        sp.wait_ge(h_d.sem, h_d.at(t, 2))
                        load_h(t + 2, u)
                        store(t, u)
                sp.wait_ge(p_d.sem, p_d.at(NT - 2))
                load_p(NT, 0)
                sp.wait_ge(h_d.sem, h_d.at(NT - 2, 2))
                load_h(NT, 0)
                store(NT - 2, 0)
                store(NT - 1, 1)
                store(NT, 0)
                sp.wait_ge(out_s[0].sem, out_s[0].at(NT // 2))
                sp.wait_ge(out_s[1].sem, out_s[1].at(NT // 2 - 1))

            @block.gpsimd
            def _(pool):
                def gather(t, u):
                    rows = TS if t == NT else P
                    for k, y in enumerate((y0, y1)):
                        where = bass.IndirectOffsetOnAxis(ap=slot_u[0:rows, k, t:t + 1], axis=0)
                        pool.indirect_dma_start(out=y[u][0:rows], out_offset=None, in_=sorted_y, in_offset=where).then_inc(y_in[u].sem, 16)

                def power(t):
                    pool.wait_ge(h_d.sem, h_d.at(t, 6))
                    nc.gpsimd.tensor_tensor(rs[:], mv[:, 2:3], halves[:], ALU.pow).then_inc(rs_g.sem, 1)

                def power2(t):
                    pool.wait_ge(q_d.sem, q_d.at(t, 3))
                    nc.gpsimd.tensor_tensor(rr[:], var2[:], halves[:], ALU.pow).then_inc(rr_g.sem, 1)

                gather(0, 0)
                gather(1, 1)
                power(0)
                gather(2, 0)
                for t in range(1, TILES):
                    power(t)
                    if t + 2 < TILES:
                        gather(t + 2, t % 2)
                    power2(t - 1)
                power2(NT)

            @block.tensor
            def _(pe):
                def three(bank, hi, lo, wh, wl, blocks, half):
                    cols = slice(512 * half, 512 * half + 512)
                    for k in range(blocks):
                        for n, (x, w) in enumerate(((hi, wh), (hi, wl), (lo, wh))):
                            m = nc.tensor.matmul(bank[:], x[:, k], w[:, k, cols], start=(k == 0 and n == 0), stop=(k == blocks - 1 and n == 2))
                    return m

                def embed(t, u):
                    pe.wait_ge(p_d.sem, p_d.at(t))
                    if not (isinstance(t, int) and t < 2):
                        pe.wait_ge(q_d.sem, q_d.at(t - 2, 2))
                    for half in range(2):
                        three(ple_b[2 * u + half], ph[u], pl[u], wph, wpl, KP, half).then_inc(ple_p.sem, 1)

                def step(t, u, k, more):
                    pe.wait_ge(h_d.sem, h_d.at(t))
                    for half in range(2):
                        if not first(t):
                            pe.wait_ge(turn_d.sem, turn_d.at(t - 1, half + 1))
                        for c in range(4):
                            n = 4 * half + c
                            m = nc.tensor.transpose(turn_b[half][:, c * P:(c + 1) * P], h[u][:, n * P:(n + 1) * P], ident[:])
                        m.then_inc(turn_p.sem, 1)
                    pe.wait_ge(turn_d.sem, turn_d.at(t))
                    for half in range(2):
                        if not first(t):
                            pe.wait_ge(tanh_a.sem, tanh_a.at(t - 1, half + 1))
                        three(gate_b[half], hh[u], hl[u], wgh, wgl, KD, half).then_inc(gate_p.sem, 1)
                    if more:
                        embed(t + 1, 1 - u)

                const.wait(pe)
                embed(0, 0)
                steps(pe, step)

            @block.scalar
            def _(act):
                def weighted(t, u, k):
                    act.wait_ge(y_in[u].sem, (k + 1) * 32)
                    w = weight[:, 0, t:t + 1] if isinstance(t, int) else weight[:, 0, bass.ds(t, 1)]
                    nc.scalar.activation(y0[u][:], y0[u][:], ACT.Copy, scale=w).then_inc(y0_a.sem, 1)

                def split_p(t, u, k):
                    act.wait_ge(pT_in[u].sem, (k + 1) * 16)
                    if not (isinstance(t, int) and t < 2):
                        act.wait_ge(ple_p.sem, ple_p.at(t - 2))
                    split_hi(nc.scalar, ph[u][:], pT[u][:], 1.0).then_inc(p_a.sem, 1)

                def square(t, u):
                    act.wait_ge(q_d.sem, q_d.at(t, 2))
                    nc.scalar.activation(junk[:], q[u][:], ACT.Square, accum_out=ssq[u][:]).then_inc(sq_a.sem, 1)

                def step(t, u, k, more):
                    for half in range(2):
                        act.wait_ge(turn_p.sem, turn_p.at(t, half + 1))
                        split_hi(nc.scalar, hh[u][:, 4 * half:4 * half + 4], turn_b[half][:].rearrange("p (k t) -> p k t", t=P), 1.0).then_inc(turn_a.sem, 1)
                    if not first(t):
                        square(t - 1, 1 - u)
                    if more:
                        weighted(t + 1, 1 - u, k + u)
                        split_p(t + 1, 1 - u, k + u)
                    act.wait_ge(out_s[u].sem, out_s[u].at(k, 0))
                    for half in range(2):
                        act.wait_ge(gate_p.sem, gate_p.at(t, half + 1))
                        nc.scalar.activation(q[u][:, 512 * half:512 * half + 512], gate_b[half][:], ACT.Tanh, scale=0.5 / W_SCALE).then_inc(tanh_a.sem, 1)

                split_p(0, 0, 0)
                weighted(0, 0, 0)
                steps(act, step)
                square(NT, 0)

            @block.vector
            def _(dve):
                stt = nc.vector.scalar_tensor_tensor

                def norm(t, u, k):
                    if not first(t):
                        dve.wait_ge(q_d.sem, q_d.at(t - 2))
                    dve.wait_ge(y0_a.sem, y0_a.at(t))
                    w = weight[:, 1, t:t + 1] if isinstance(t, int) else weight[:, 1, bass.ds(t, 1)]
                    stt(y0[u][:], y1[u][:], w, y0[u][:], ALU.mult, ALU.add).then_inc(h_d.sem, 1)
                    dve.wait_ge(h_d.sem, h_d.at(t, 1))
                    dve.wait_ge(h1_in[u].sem, (k + 1) * 16)
                    stt(h[u][:], h1[u][:], ALPHA, y0[u][:], ALU.mult, ALU.add).then_inc(h_d.sem, 1)
                    dve.wait_ge(h_d.sem, h_d.at(t, 2))
                    normalize(nc.vector, h_d, t, 2, h[u][:], stats, mv, rs[:], rs_g, h[u][:], gb[:, 0:D], gb[:, D:2 * D])

                def split_p(t, u):
                    dve.wait_ge(p_a.sem, p_a.at(t))
                    split_lo(nc.vector, pl[u][:], pT[u][:], 1.0, ph[u][:]).then_inc(p_d.sem, 1)

                def embed(t, u):
                    for half in range(2):
                        c = slice(512 * half, 512 * half + 512)
                        dve.wait_ge(tanh_a.sem, tanh_a.at(t, half + 1))
                        stt(q[u][:, c], q[u][:, c], 1.0, ple_b[2 * u + half][:], ALU.add, ALU.mult).then_inc(q_d.sem, 1)
                    dve.wait_ge(sq_a.sem, sq_a.at(t))
                    nc.vector.tensor_scalar(var2[:], ssq[u][:], 1.0 / D, (2 * W_SCALE) ** 2 * LN_EPS, ALU.mult, ALU.add).then_inc(q_d.sem, 1)
                    nc.vector.tensor_tensor(q[u][:], q[u][:], gb[:, 2 * D:], ALU.mult).then_inc(q_d.sem, 1)
                    dve.wait_ge(q_d.sem, q_d.at(t, 4))
                    dve.wait_ge(rr_g.sem, rr_g.at(t))
                    stt(q[u][:], q[u][:], rr[:], h[u][:], ALU.mult, ALU.add).then_inc(q_d.sem, 1)

                def step(t, u, k, more):
                    norm(t, u, k)
                    for half in range(2):
                        dve.wait_ge(turn_a.sem, turn_a.at(t, half + 1))
                        r = slice(4 * half, 4 * half + 4)
                        split_lo(nc.vector, hl[u][:, r], turn_b[half][:].rearrange("p (k t) -> p k t", t=P), 1.0, hh[u][:, r]).then_inc(turn_d.sem, 1)
                    if not first(t):
                        embed(t - 1, 1 - u)
                    if more:
                        split_p(t + 1, 1 - u)

                q_d.prime(dve)
                split_p(0, 0)
                steps(dve, step)
                embed(NT, 0)


INPUTS = ["x_all", "x_rows", "w_in", "vecs", "w_lora", "w_gate", "fconst", "mconst", "ident", "s0T", "r0", "w_out", "w_router",
          "vec2", "rconst", "w13", "w2", "pT", "w_ple", "w_pgate", "vec3"]
OUTPUTS = {"out": (TILES, P, D), "shift_p": (1, D), "shift_s": (DB, D), "wkv_p": (P, 4, NA), "ret_p": (P, 2, NV), "wkv_s": (P, DB, 4, NA), "ret_s": (P, DB, 2, NV)}


def program(nc, a, o):
    proj = nc.dram_tensor("proj", (ROWS, IN_W), F32, kind="Internal").ap()
    yT_d = nc.dram_tensor("yT_d", (TILES, P, KD, P), F32, kind="Internal").ap()
    sorted_h = nc.dram_tensor("sorted_h", (SLOTS, D), F32, kind="Internal").ap()
    sorted_y = nc.dram_tensor("sorted_y", (SLOTS, D), F32, kind="Internal").ap()
    with ExitStack() as soft:
        with ExitStack() as ctx:
            const = MixerConstants(nc, ctx)
            project(nc, soft, a["x_all"], a["w_in"], proj, sorted_h,
                    lambda sp: const.load(sp, a["vecs"], a["w_lora"], a["w_gate"], a["mconst"], a["ident"]))
            mixer(nc, const, proj, a["fconst"], a["s0T"], a["r0"], yT_d, o["wkv_p"], o["ret_p"], o["wkv_s"], o["ret_s"])
        h_dram = nc.dram_tensor("h_dram", (TILES, P, D), F32, kind="Internal").ap()
        with ExitStack() as ctx:
            weight = ctx.enter_context(nc.sbuf_tensor("weight", [P, 2, TILES], F32))
            slot_u = ctx.enter_context(nc.sbuf_tensor("slot_u", [P, 2, TILES], U32))
            tile_expert = ctx.enter_context(nc.sbuf_tensor("tile_expert", [P, SLOTS // P], I32))
            ident = ctx.enter_context(nc.sbuf_tensor("ident", [P, P], F32))
            halves = ctx.enter_context(nc.sbuf_tensor("halves", [P, 1], F32))
            h_rows = ctx.enter_context(nc.sbuf_tensor("h_rows", [P, TILES, D], F32))
            logits = ctx.enter_context(nc.sbuf_tensor("logits", [P, TILES, NG + NE], F32))
            merge(nc, soft, a["x_rows"], o["shift_p"], o["shift_s"], yT_d, a["w_out"], a["w_router"], a["vec2"], a["ident"], ident, halves, h_rows, h_dram, logits)
            const = FinishConstants(nc, ctx, h_rows)
            with ExitStack() as ring:
                weights = ExpertWeights(nc, ring, a["w13"], a["w2"])
                route(nc, soft, weights, logits, h_rows, a["rconst"], slot_u, weight, tile_expert, sorted_h)
                experts(nc, weights, ident, tile_expert, sorted_h, sorted_y, const, a["w_ple"], a["w_pgate"], a["vec3"])
            finish(nc, soft, const, ident, halves, h_dram, slot_u, weight, sorted_y, a["pT"], o["out"])


def layout(inputs):
    z = {n: np.asarray(a) for n, a in inputs.items()}
    out = {}
    rows = np.zeros((ROWS, D), np.float32)
    rows[1:1 + SEQ] = z["x_prompt"][0]
    tail = rows[SAMPLE0:SAMPLE0 + DB * (DS + 1)].reshape(DB, DS + 1, D)
    tail[:, 0] = z["state_shift"][0]
    tail[:, 1:] = z["x_sample"]
    out["x_rows"] = rows
    out["x_all"] = np.ascontiguousarray(rows.reshape(TILES, P, KD, P).transpose(3, 0, 2, 1))
    out["w_in"] = np.ascontiguousarray(z["w_in"][0].reshape(KD, P, NSLICE, SLICE).transpose(2, 1, 0, 3))
    out["vecs"] = np.concatenate([z[n][0].reshape(-1) for n in VEC])[None]
    out["w_lora"] = np.concatenate([z["w_decay_up"][0], z["w_aaa_up"][0]])
    out["w_gate"] = z["w_gate_up"][0]
    out["s0T"] = z["state_wkv"][0].reshape(DB, 4, 2, NA, NA).transpose(2, 4, 0, 1, 3).reshape(P, DB, 4, NA)
    out["r0"] = z["state_ret"][0].reshape(DB, 2, 2, NK, NV).transpose(2, 3, 0, 1, 4).reshape(P, DB, 2, NV)
    out["w_out"] = z["w_out"][0].reshape(KD, P, D).transpose(1, 0, 2)
    out["w_router"] = np.concatenate([z["router_coarse_w"][0], z["router_fine_w"][0]], 1).reshape(KD, P, NG + NE).transpose(1, 0, 2)
    out["vec2"] = np.concatenate([z[n][0] for n in ("ln1_g", "ln1_b", "router_coarse_b", "router_fine_b")])[None]
    out["w13"] = np.stack([z["expert_" + n][0].reshape(NE, KD, P, FE) for n in ("w1", "w3")], 3).transpose(0, 2, 1, 3, 4).reshape(NE, P, KD, 2 * FE)
    out["w2"] = z["expert_w2"][0].reshape(NE, FE // P, P, D).transpose(0, 2, 1, 3)
    p = np.zeros((ROWS, D_PLE), np.float32)
    p[:SEQ] = z["p_prompt"][0, 0]
    p[SEQ:SEQ + TS] = z["p_sample"][0].reshape(TS, D_PLE)
    out["pT"] = p.reshape(TILES, P, D_PLE // P, P).transpose(0, 3, 2, 1)
    out["w_ple"] = z["w_ple"][0].reshape(D_PLE // P, P, D).transpose(1, 0, 2)
    out["w_pgate"] = z["w_ple_gate"][0].reshape(KD, P, D).transpose(1, 0, 2)
    out["vec3"] = np.concatenate([z[n][0] for n in ("ln2_g", "ln2_b", "ple_norm_g")])[None]
    out["fconst"], out["mconst"], out["rconst"] = shape_constants()
    out["ident"] = np.eye(P, dtype=np.float32)
    return out


def kernel(**inputs):
    import concourse.bacc as bacc
    from concourse.bass_utils import run_bass_kernel_spmd as run

    laid = layout(inputs)
    nc = bacc.Bacc("TRN2", target_bir_lowering=False, num_devices=1)
    arrays, a, o = {}, {}, {}
    for name in INPUTS:
        arrays["in_" + name] = np.ascontiguousarray(laid[name])
        a[name] = nc.dram_tensor("in_" + name, arrays["in_" + name].shape, F32, kind="ExternalInput").ap()
    for name, shape in OUTPUTS.items():
        o[name] = nc.dram_tensor("out_" + name, shape, F32, kind="ExternalOutput").ap()
    program(nc, a, o)
    got = run(nc, [arrays], core_ids=[0]).results[0]
    y = np.asarray(got["out_out"]).reshape(ROWS, D)
    wkv_p = np.asarray(got["out_wkv_p"]).reshape(2, NA, 4, NA).transpose(2, 0, 3, 1).reshape(1, 1, HA, NA, NA)
    ret_p = np.asarray(got["out_ret_p"]).reshape(2, NK, 2, NV).transpose(2, 0, 1, 3).reshape(1, 1, HB, NK, NV)
    wkv_s = np.asarray(got["out_wkv_s"]).reshape(2, NA, DB, 4, NA).transpose(2, 3, 0, 4, 1).reshape(1, DB, HA, NA, NA)
    ret_s = np.asarray(got["out_ret_s"]).reshape(2, NK, DB, 2, NV).transpose(2, 3, 0, 1, 4).reshape(1, DB, HB, NK, NV)
    shift_p = np.asarray(got["out_shift_p"]).reshape(1, 1, D)
    shift_s = np.asarray(got["out_shift_s"]).reshape(1, DB, D)
    return (y[:SEQ].reshape(1, SEQ, D), y[SEQ:SEQ + TS].reshape(DB, DS, D), wkv_p, shift_p, ret_p, wkv_s, shift_s, ret_s)
```
